# Optimizing a Trainium2 kernel written in Bass

```python
import jax, jax.numpy as jnp
from jax import lax
import numpy as np

D_MODEL = 1024
BATCH = 1
SEQ = 512
DEPTH = 1

MEM_LEN = 256
HG_HEADS = 4
HG_DK = 128
HG_DV = 128
HG_WIDTH = HG_HEADS * HG_DV
HG_CHUNK = 64
SG_GROUPS = 4
SG_DIM = 128
SG_WIDTH = SG_GROUPS * SG_DIM
SG_CHUNK = 128
MIX_WIDTH = HG_WIDTH + SG_WIDTH
IN_WIDTH = 4 * HG_WIDTH + 2 * SG_WIDTH
X_HEADS = 4
X_HEAD_DIM = D_MODEL // X_HEADS
D_FF = 2816
ALPHA = (2.0 * DEPTH) ** 0.25
BETA = (8.0 * DEPTH) ** -0.25
LN_EPS = 1e-5


def _layer_norm(x, g, b):
    xf = x.astype(jnp.float32)
    mu = jnp.mean(xf, axis=-1, keepdims=True)
    var = jnp.mean(jnp.square(xf - mu), axis=-1, keepdims=True)
    return ((xf - mu) * lax.rsqrt(var + LN_EPS) * g + b).astype(x.dtype)

def _rms_norm(x, g):
    xf = x.astype(jnp.float32)
    return xf * lax.rsqrt(jnp.mean(jnp.square(xf), axis=-1, keepdims=True) + LN_EPS) * g

def _swiglu(x, w_gate, w_up, w_down):
    return (jax.nn.silu(x @ w_gate) * (x @ w_up)) @ w_down

def _hgrn2(q, fz, iv, lb):
    B, T, H, DK = q.shape
    DV = iv.shape[-1]
    n_chunks = T // HG_CHUNK
    q = q.astype(jnp.float32)
    fz = fz.astype(jnp.float32)
    iv = iv.astype(jnp.float32)
    log_f = jnp.log(lb + (1.0 - lb) * jax.nn.sigmoid(fz))
    k = (1.0 - lb) * jax.nn.sigmoid(-fz)

    def chunks(a):
        return a.reshape(B, n_chunks, HG_CHUNK, H, a.shape[-1]).transpose(1, 0, 3, 2, 4)

    causal = jnp.tril(jnp.ones((HG_CHUNK, HG_CHUNK), dtype=bool))[:, :, None]

    def step(S, inp):
        qc, kc, vc, lfc = inp
        b = jnp.cumsum(lfc, axis=2)
        diff = b[:, :, :, None, :] - b[:, :, None, :, :]
        decay = jnp.where(causal, jnp.exp(jnp.where(causal, diff, 0.0)), 0.0)
        scores = jnp.einsum('bhtd,bhsd,bhtsd->bhts', qc, kc, decay)
        o = (jnp.einsum('bhts,bhsv->bhtv', scores, vc)
             + jnp.einsum('bhtd,bhdv->bhtv', qc * jnp.exp(b), S))
        b_end = b[:, :, -1:, :]
        S = (jnp.exp(b_end[:, :, 0, :])[..., None] * S
             + jnp.einsum('bhsd,bhsv->bhdv', kc * jnp.exp(b_end - b), vc))
        return S, o

    S0 = jnp.zeros((B, H, DK, DV), jnp.float32)
    _, o = lax.scan(step, S0, (chunks(q), chunks(k), chunks(iv), chunks(log_f)))
    return o.transpose(1, 0, 3, 2, 4).reshape(B, T, H, DV)

def _spatial_gating(uv, w_s, b_s, ln_g, ln_b):
    B, T, _ = uv.shape
    u, v = jnp.split(uv, 2, axis=-1)
    v = _layer_norm(v.reshape(B, T, SG_GROUPS, SG_DIM), ln_g, ln_b)
    v = v.reshape(B, T // SG_CHUNK, SG_CHUNK, SG_GROUPS, SG_DIM)
    causal = jnp.tril(jnp.ones((SG_CHUNK, SG_CHUNK), dtype=bool))
    w = jnp.where(causal, w_s, 0.0)
    s = jnp.einsum('gts,bnsgc->bntgc', w, v) + b_s.T[None, None, :, :, None]
    return u * s.reshape(B, T, SG_WIDTH)

def _token_mixers(h, w_in, lb, hg_norm_g, sg_ln_g, sg_ln_b, sg_w_s, sg_b_s, w_out):
    B, T, _ = h.shape
    proj = h @ w_in
    q, fz, iv, g, uv = jnp.split(
        proj, [HG_WIDTH, 2 * HG_WIDTH, 3 * HG_WIDTH, 4 * HG_WIDTH], axis=-1)
    heads = lambda a: a.reshape(B, T, HG_HEADS, -1)
    o = _hgrn2(heads(q), heads(fz), heads(iv), lb)
    o = _rms_norm(o, hg_norm_g) * jax.nn.silu(heads(g).astype(jnp.float32))
    o_a = o.reshape(B, T, HG_WIDTH).astype(h.dtype)
    o_b = _spatial_gating(jax.nn.gelu(uv), sg_w_s, sg_b_s, sg_ln_g, sg_ln_b)
    return jnp.concatenate([o_a, o_b], axis=-1) @ w_out

def _memory_cross_attention(h, mem, mem_g, mem_b, wq, wk, wv, wo):
    B, T, _ = h.shape
    M = mem.shape[1]
    m = _layer_norm(mem, mem_g, mem_b)
    q = (h @ wq).reshape(B, T, X_HEADS, X_HEAD_DIM)
    k = (m @ wk).reshape(B, M, X_HEADS, X_HEAD_DIM)
    v = (m @ wv).reshape(B, M, X_HEADS, X_HEAD_DIM)
    s = jnp.einsum('bthd,bmhd->bhtm', q.astype(jnp.float32), k.astype(jnp.float32)) * (X_HEAD_DIM ** -0.5)
    p = jax.nn.softmax(s, axis=-1).astype(h.dtype)
    o = jnp.einsum('bhtm,bmhd->bthd', p, v).reshape(B, T, D_MODEL)
    return o @ wo

def first_inputs(seed: int = 0) -> dict:
    key = jax.random.key(seed)
    ks = iter(jax.random.split(key, 48))
    L = DEPTH

    def nrm(shape, scale):
        return jax.random.normal(next(ks), shape, jnp.float32) * scale

    def gain(shape):
        return 1.0 + nrm(shape, 0.05)

    def bias(shape):
        return nrm(shape, 0.01)

    d_in = D_MODEL ** -0.5
    f_in = D_FF ** -0.5
    return {
        "x": nrm((BATCH, SEQ, D_MODEL), 1.0),
        "mem": nrm((BATCH, MEM_LEN, D_MODEL), 1.0),
        "ffn1_w_gate": nrm((L, D_MODEL, D_FF), d_in),
        "ffn1_w_up": nrm((L, D_MODEL, D_FF), d_in),
        "ffn1_w_down": nrm((L, D_FF, D_MODEL), f_in * BETA),
        "ln1_g": gain((L, D_MODEL)),
        "ln1_b": bias((L, D_MODEL)),
        "w_in": nrm((L, D_MODEL, IN_WIDTH), d_in),
        "hg_lb_logits": nrm((DEPTH + 1, HG_HEADS, HG_DK), 0.5),
        "hg_norm_g": gain((L, HG_DV)),
        "sg_ln_g": gain((L, SG_GROUPS, SG_DIM)),
        "sg_ln_b": bias((L, SG_GROUPS, SG_DIM)),
        "sg_w_s": nrm((L, SG_GROUPS, SG_CHUNK, SG_CHUNK), SG_CHUNK ** -0.5),
        "sg_b_s": gain((L, SG_GROUPS, SG_CHUNK)),
        "w_out": nrm((L, MIX_WIDTH, D_MODEL), (MIX_WIDTH ** -0.5) * BETA),
        "ln2_g": gain((L, D_MODEL)),
        "ln2_b": bias((L, D_MODEL)),
        "mem_ln_g": gain((L, D_MODEL)),
        "mem_ln_b": bias((L, D_MODEL)),
        "xa_w_q": nrm((L, D_MODEL, D_MODEL), d_in),
        "xa_w_k": nrm((L, D_MODEL, D_MODEL), d_in),
        "xa_w_v": nrm((L, D_MODEL, D_MODEL), d_in * BETA),
        "xa_w_o": nrm((L, D_MODEL, D_MODEL), d_in * BETA),
        "ln3_g": gain((L, D_MODEL)),
        "ln3_b": bias((L, D_MODEL)),
        "ffn2_w_gate": nrm((L, D_MODEL, D_FF), d_in),
        "ffn2_w_up": nrm((L, D_MODEL, D_FF), d_in),
        "ffn2_w_down": nrm((L, D_FF, D_MODEL), f_in * BETA),
        "ln4_g": gain((L, D_MODEL)),
        "ln4_b": bias((L, D_MODEL)),
    }

def first_block(x, mem, ffn1_w_gate, ffn1_w_up, ffn1_w_down, ln1_g, ln1_b,
              w_in, hg_lb_logits, hg_norm_g, sg_ln_g, sg_ln_b, sg_w_s, sg_b_s,
              w_out, ln2_g, ln2_b, mem_ln_g, mem_ln_b, xa_w_q, xa_w_k, xa_w_v,
              xa_w_o, ln3_g, ln3_b, ffn2_w_gate, ffn2_w_up, ffn2_w_down,
              ln4_g, ln4_b):
    lower_bounds = jnp.cumsum(jax.nn.softmax(hg_lb_logits.astype(jnp.float32), axis=0), axis=0)
    h = x
    for l in range(DEPTH):
        h = _layer_norm(ALPHA * h + 0.5 * _swiglu(h, ffn1_w_gate[l], ffn1_w_up[l], ffn1_w_down[l]),
                        ln1_g[l], ln1_b[l])
        mix = _token_mixers(h, w_in[l], lower_bounds[l], hg_norm_g[l], sg_ln_g[l], sg_ln_b[l],
                            sg_w_s[l], sg_b_s[l], w_out[l])
        h = _layer_norm(ALPHA * h + mix, ln2_g[l], ln2_b[l])
        xa = _memory_cross_attention(h, mem, mem_ln_g[l], mem_ln_b[l], xa_w_q[l], xa_w_k[l],
                                     xa_w_v[l], xa_w_o[l])
        h = _layer_norm(ALPHA * h + xa, ln3_g[l], ln3_b[l])
        h = _layer_norm(ALPHA * h + 0.5 * _swiglu(h, ffn2_w_gate[l], ffn2_w_up[l], ffn2_w_down[l]),
                        ln4_g[l], ln4_b[l])
    return h


HEAD_DIM = 64
N_Q_HEADS = 8
N_KV_HEADS = 2
Q_PER_KV = N_Q_HEADS // N_KV_HEADS
ATTN_WIDTH = N_Q_HEADS * HEAD_DIM
KV_WIDTH = N_KV_HEADS * HEAD_DIM
ROPE_PAIRS = HEAD_DIM // 4
ROPE_THETA = 10000.0
Q_BLOCK = 128
POOL_WINDOWS = (2, 4, 8, 16)
N_POOL_GROUPS = len(POOL_WINDOWS)
POOL_WIDTH = D_MODEL - ATTN_WIDTH
POOL_GROUP_DIM = POOL_WIDTH // N_POOL_GROUPS
MIX_WIDTH_2 = ATTN_WIDTH + POOL_WIDTH
IN_WIDTH_2 = ATTN_WIDTH + 2 * KV_WIDTH + POOL_WIDTH
D_FF_2 = ((8 * D_MODEL // 3 + 255) // 256) * 256
GRID_W = 64
EPS = 1e-6


def rmsnorm(x, g):
    xf = x.astype(jnp.float32)
    y = xf * lax.rsqrt(jnp.mean(xf * xf, axis=-1, keepdims=True) + EPS)
    return (y * g.astype(jnp.float32)).astype(x.dtype)

def rope_1d(x, ang):
    xf = x.astype(jnp.float32)
    x1, x2 = jnp.split(xf, 2, axis=-1)
    c = jnp.cos(ang)[None, :, None, :]
    s = jnp.sin(ang)[None, :, None, :]
    return jnp.concatenate([x1 * c - x2 * s, x2 * c + x1 * s], axis=-1).astype(x.dtype)

def axial_rope(x, ang_row, ang_col):
    xr, xc = jnp.split(x, 2, axis=-1)
    return jnp.concatenate([rope_1d(xr, ang_row), rope_1d(xc, ang_col)], axis=-1)

def attention_mixer(q, k, v, q_g, k_g, ang_row, ang_col):
    B, S, _ = q.shape
    q = q.reshape(B, S, N_Q_HEADS, HEAD_DIM)
    k = k.reshape(B, S, N_KV_HEADS, HEAD_DIM)
    v = v.reshape(B, S, N_KV_HEADS, HEAD_DIM)
    q = axial_rope(rmsnorm(q, q_g), ang_row, ang_col)
    k = axial_rope(rmsnorm(k, k_g), ang_row, ang_col)
    n_blk = S // Q_BLOCK
    qb = q.reshape(B, n_blk, Q_BLOCK, N_KV_HEADS, Q_PER_KV, HEAD_DIM).transpose(1, 0, 2, 3, 4, 5)
    scale = HEAD_DIM ** -0.5

    def block(qblk):
        s = jnp.einsum('bqkgd,bskd->bkgqs', qblk, k).astype(jnp.float32) * scale
        p = jax.nn.softmax(s, axis=-1)
        return jnp.einsum('bkgqs,bskd->bqkgd', p.astype(v.dtype), v)

    o = lax.map(block, qb)
    return o.transpose(1, 0, 2, 3, 4, 5).reshape(B, S, ATTN_WIDTH)

def pool_mixer(u, pool_w, pool_b, pool_scale):
    B, S, _ = u.shape
    ug = u.reshape(B, S, N_POOL_GROUPS, POOL_GROUP_DIM)
    uf = ug.astype(jnp.float32)
    csum = jnp.concatenate([jnp.zeros_like(uf[:, :1]), jnp.cumsum(uf, axis=1)], axis=1)
    t = jnp.arange(S)
    pooled = []
    for g, w in enumerate(POOL_WINDOWS):
        lo = jnp.clip(t - w // 2, 0, S)
        hi = jnp.clip(t - w // 2 + w, 0, S)
        cnt = (hi - lo).astype(jnp.float32)[None, :, None]
        cg = csum[:, :, g, :]
        mean = (cg[:, hi] - cg[:, lo]) / cnt
        pooled.append(mean - uf[:, :, g, :])
    pooled = jnp.stack(pooled, axis=1).astype(u.dtype)
    y = jnp.einsum('bgsc,gcd->bsgd', pooled, pool_w) + pool_b[None, None]
    return y.reshape(B, S, POOL_WIDTH) * pool_scale

def second_inputs(seed: int = 0) -> dict:
    key = jax.random.key(seed)
    ks = jax.random.split(key, 14)
    f32 = jnp.float32

    def nrm(k, shape, fan_in):
        return jax.random.normal(k, shape, f32) * fan_in ** -0.5

    def gain(k, shape):
        return 1.0 + 0.05 * jax.random.normal(k, shape, f32)

    res_scale = (2 * DEPTH) ** -0.5
    return {
        "x": jax.random.normal(ks[0], (BATCH, SEQ, D_MODEL), f32),
        "norm1_g": gain(ks[1], (DEPTH, D_MODEL)),
        "w_in": nrm(ks[2], (DEPTH, D_MODEL, IN_WIDTH_2), D_MODEL),
        "q_norm_g": gain(ks[3], (DEPTH, HEAD_DIM)),
        "k_norm_g": gain(ks[4], (DEPTH, HEAD_DIM)),
        "pool_w": nrm(ks[5], (DEPTH, N_POOL_GROUPS, POOL_GROUP_DIM, POOL_GROUP_DIM), POOL_GROUP_DIM),
        "pool_b": 0.02 * jax.random.normal(ks[6], (DEPTH, N_POOL_GROUPS, POOL_GROUP_DIM), f32),
        "pool_scale": gain(ks[7], (DEPTH, POOL_WIDTH)),
        "w_out": nrm(ks[8], (DEPTH, MIX_WIDTH_2, D_MODEL), MIX_WIDTH_2) * res_scale,
        "norm2_g": gain(ks[9], (DEPTH, D_MODEL)),
        "w_gate": nrm(ks[10], (DEPTH, D_MODEL, D_FF_2), D_MODEL),
        "w_up": nrm(ks[11], (DEPTH, D_MODEL, D_FF_2), D_MODEL),
        "w_down": nrm(ks[12], (DEPTH, D_FF_2, D_MODEL), D_FF_2) * res_scale,
    }

def second_block(x, norm1_g, w_in, q_norm_g, k_norm_g, pool_w, pool_b, pool_scale,
              w_out, norm2_g, w_gate, w_up, w_down):
    B, S, _ = x.shape
    rows = S // GRID_W
    row = jnp.repeat(jnp.arange(rows), GRID_W).astype(jnp.float32)
    col = (jnp.arange(S) % GRID_W).astype(jnp.float32)
    inv_freq = ROPE_THETA ** (-jnp.arange(ROPE_PAIRS, dtype=jnp.float32) / ROPE_PAIRS)
    ang_row = row[:, None] * inv_freq[None, :]
    ang_col = col[:, None] * inv_freq[None, :]

    splits = [ATTN_WIDTH, ATTN_WIDTH + KV_WIDTH, ATTN_WIDTH + 2 * KV_WIDTH]
    for l in range(DEPTH):
        h = rmsnorm(x, norm1_g[l])
        proj = h @ w_in[l]
        q, k, v, u = jnp.split(proj, splits, axis=-1)
        a = attention_mixer(q, k, v, q_norm_g[l], k_norm_g[l], ang_row, ang_col)
        p = pool_mixer(u, pool_w[l], pool_b[l], pool_scale[l])
        x = x + jnp.concatenate([a, p], axis=-1) @ w_out[l]
        h = rmsnorm(x, norm2_g[l])
        x = x + (jax.nn.silu(h @ w_gate[l]) * (h @ w_up[l])) @ w_down[l]
    return x


def setup_inputs(seed=0):
    out = dict(first_inputs(seed))
    for name, value in second_inputs(seed + 1).items():
        if name != "x":
            out[name + "_2"] = value
    return out


def reference(
    x, mem, ffn1_w_gate, ffn1_w_up, ffn1_w_down, ln1_g, ln1_b, w_in, hg_lb_logits, hg_norm_g,
    sg_ln_g, sg_ln_b, sg_w_s, sg_b_s, w_out, ln2_g, ln2_b, mem_ln_g, mem_ln_b, xa_w_q, xa_w_k,
    xa_w_v, xa_w_o, ln3_g, ln3_b, ffn2_w_gate, ffn2_w_up, ffn2_w_down, ln4_g, ln4_b, norm1_g_2,
    w_in_2, q_norm_g_2, k_norm_g_2, pool_w_2, pool_b_2, pool_scale_2, w_out_2, norm2_g_2,
    w_gate_2, w_up_2, w_down_2,
):
    x = first_block(
        x, mem, ffn1_w_gate, ffn1_w_up, ffn1_w_down, ln1_g, ln1_b, w_in, hg_lb_logits,
        hg_norm_g, sg_ln_g, sg_ln_b, sg_w_s, sg_b_s, w_out, ln2_g, ln2_b, mem_ln_g, mem_ln_b,
        xa_w_q, xa_w_k, xa_w_v, xa_w_o, ln3_g, ln3_b, ffn2_w_gate, ffn2_w_up, ffn2_w_down,
        ln4_g, ln4_b,
    )
    return second_block(
        x, norm1_g_2, w_in_2, q_norm_g_2, k_norm_g_2, pool_w_2, pool_b_2, pool_scale_2, w_out_2,
        norm2_g_2, w_gate_2, w_up_2, w_down_2,
    )


_drawn_inputs = setup_inputs


def setup_inputs(seed=0):
    import zlib

    import numpy as np

    out = dict(_drawn_inputs(seed))
    spreads = {}
    factors = {'ln1_b': 4.378,
     'hg_norm_g': 4.742,
     'sg_ln_g': 6.535,
     'sg_ln_b': 8.0,
     'sg_b_s': 4.916,
     'ln2_b': 5.184,
     'mem_ln_g': 8.0,
     'mem_ln_b': 8.0,
     'ln3_b': 5.337,
     'ln4_b': 5.355,
     'q_norm_g_2': 8.0,
     'k_norm_g_2': 8.0,
     'pool_b_2': 5.959,
     'pool_scale_2': 2.829,
     'norm2_g_2': 3.077}
    for name, (base, spread) in spreads.items():
        noise = np.random.default_rng([zlib.crc32(name.encode()), seed]).standard_normal(out[name].shape)
        drawn = base * np.exp(spread * noise) if base else spread * noise
        out[name] = __import__('jax').numpy.asarray(drawn.astype(out[name].dtype))
    for name, factor in factors.items():
        out[name] = (out[name] * factor).astype(out[name].dtype)
    return out
```

```python
from contextlib import ExitStack

import numpy as np

import concourse.bass as bass
from concourse import mybir

F32 = mybir.dt.float32
F32R = mybir.dt.float32r
I32 = mybir.dt.int32
ACT = mybir.ActivationFunctionType
ALU = mybir.AluOpType
AX = mybir.AxisListType

P = 128
T = 512
D = 1024
KD = D // P
TT = T // P
F = 2816
MEM = 256
MT = MEM // P
HG = 4
SG = 4
XH = 4
QH = 8
HD = 64
GRID_W = 64
ALPHA = 2.0 ** 0.25
LN_EPS = 1e-5
RMS_EPS = 1e-6
PARTS = (8, 8, 6)
assert sum(PARTS) * P == F
RAW = 4
SPLIT = 2
LEVELS = (6, 5, 4, 3, 2, 1, 0)

V_LN1G, V_LN1B, V_LN2G, V_LN2B, V_MEMG, V_MEMB, V_LN3G, V_LN3B, V_LN4G, V_LN4B, V_N1, V_N2 = range(0, 96, 8)
V_POOLB, V_POOLS, V_HGN, V_LB, V_QN, V_KN, V_ROWS = 96, 100, 104, 105, 113, 114, 115

C_ID, C_MEAN, C_M128, C_HEAD, C_ROT, C_DUP0, C_DUP1, C_N = range(8)


def shape_constants():
    i = np.arange(P)
    mats = np.zeros((C_N, P, P), np.float32)
    mats[C_ID] = np.eye(P)
    mats[C_MEAN] = 1.0 / D
    mats[C_M128] = 1.0 / P
    mats[C_HEAD] = (i[:, None] // HD == i[None, :] // HD) / HD
    q = HD // 4
    for d in range(P):
        if (d // q) % 2 == 0:
            mats[C_ROT, d + q, d] = -1.0
        else:
            mats[C_ROT, d - q, d] = 1.0
    for g in range(2):
        for d in range(P):
            mats[C_DUP0 + g, g * HD + d % HD, d] = 1.0
    masks = np.zeros((len(LEVELS) + 2, P, P), np.int32)
    s, t = i[:, None], i[None, :]
    for n, lv in enumerate(LEVELS):
        masks[n] = (s >> (lv + 1) == t >> (lv + 1)) & (s >> lv & 1 == 0) & (t >> lv & 1 == 1)
    masks[len(LEVELS)] = s == t
    masks[len(LEVELS) + 1] = s <= t
    freq = (np.float32(10000.0) ** (-np.arange(q, dtype=np.float32) / np.float32(q))).astype(np.float32)
    tok = np.arange(T)
    row, col = (tok // GRID_W).astype(np.float32), (tok % GRID_W).astype(np.float32)
    ang = np.zeros((P, T), np.float32)
    for d in range(P):
        ang[d] = (row if (d % HD) < HD // 2 else col) * freq[d % q]
    rope = np.stack([np.cos(ang), np.sin(ang)]).astype(np.float32)
    restart = np.ones((1, T), np.float32)
    restart[0, ::P] = 0.0
    rcnt = np.zeros((4, T), np.float32)
    for g in range(4):
        w = 2 << g
        rcnt[g] = 1.0 / (np.clip(tok - w // 2 + w, 0, T) - np.clip(tok - w // 2, 0, T))
    return {"c_mats": mats, "c_masks": masks, "c_rope": rope, "c_restart": restart, "c_rcnt": rcnt}


def build(nc, A, out):
    ctx = ExitStack()
    with ctx:
        def sem(name):
            return ctx.enter_context(nc.semaphore(name))

        top = [-(-nc.sbuf_base // 32) * 32]

        def sb(name, shape, dt=F32, at=None):
            size = int(np.prod(shape[1:])) * 4
            off = top[0] if at is None else at
            assert off + size <= nc.sbuf_usable_end, (name, off + size - nc.sbuf_usable_end)
            if at is None:
                top[0] += -(-size // 32) * 32
            return nc.alloc_sbuf_tensor_at(name, list(shape), dt, offset=off)

        bank = [ctx.enter_context(nc.psum_tensor(f"bank{i}", [P, T], F32)) for i in range(8)]

        res = sb("res", [P, KD, T])
        ahi = sb("ahi", [P, KD, T], F32R)
        alo = sb("alo", [P, KD, T], F32R)
        wraw = sb("wraw", [P, RAW, KD * P])
        whi = sb("whi", [P, SPLIT, KD * P], F32R)
        wlo = sb("wlo", [P, SPLIT, KD * P], F32R)
        mats = sb("mats", [P, C_N, P])
        masks = sb("masks", [P, len(LEVELS) + 2, P], I32)
        restart = sb("restart", [P, T])
        vecs = sb("vecs", [P, P])
        wT = sb("wT", [P, SG, P])
        small = sb("small", [P, 64])
        sgst = sb("sgst", [P, 4, 6])
        sgmv = sb("sgmv", [P, 4, 2])
        sgr = sb("sgr", [P, 4])
        mst = sb("mst", [P, 4, 6])
        mmv = sb("mmv", [P, 2, 2])
        mrs = sb("mrs", [P, 2])
        arena = top[0]
        ARENA = nc.sbuf_usable_end - arena

        def region(start):
            at = [arena + start]

            def take(name, shape, dt=F32):
                t = sb(name, shape, dt, at=at[0])
                at[0] += int(np.prod(shape[1:])) * 4
                return t
            return take

        KB = 1024
        take = region(0)
        gate = take("gate", [P, 2, T])
        hval = take("hval", [P, 2, T])
        rstd = take("rstd", [P, T])
        mean = take("mean", [P, T])
        sum1 = take("sum1", [P, T])
        sum2 = take("sum2", [P, T])
        square = gate
        var = hval
        WORK = 16 * KB
        take = region(WORK)
        hhi = take("hhi", [P, max(PARTS), T], F32R)
        hlo = take("hlo", [P, max(PARTS), T], F32R)
        take = region(WORK)
        xin = take("xin", [P, TT, D])
        vrow = take("vrow", [P, P])
        wsin = take("wsin", [P, SG, P])
        take = region(WORK)
        mk = take("mk", [P, HG, T])
        mq = take("mq", [P, HG, T])
        mg = take("mg", [P, HG, T])
        mu = take("mu", [P, SG, T])
        mv = take("mv", [P, SG, T])
        cum = take("cum", [P, HG, T])
        vT = take("vT", [P, HG, TT, P])
        ivt = take("ivt", [P, 2, T])
        acc = take("acc", [P, 2, T])
        dec = take("dec", [P, 2, T])
        qt = take("qt", [P, 2, T])
        kt = take("kt", [P, 2, T])
        sgb = take("sgb", [P, 3, T])
        vn = cum
        take = region(0)
        eb = take("eb", [P, T])
        qe = take("qe", [P, T])
        kend = take("kend", [P, 3 * P])
        kendT = take("kendT", [P, 3 * P])
        state = take("state", [P, 3, P])
        osq = take("osq", [P, T])
        ors = take("ors", [P, T])
        take = region(WORK)
        memin = take("memin", [P, MT, D])
        mhi = take("mhi", [P, KD, MEM], F32R)
        mlo = take("mlo", [P, KD, MEM], F32R)
        mval = take("mval", [P, 2, MEM])
        kx = take("kx", [P, KD, MEM])
        vx = take("vx", [P, MT, D])
        vxt = take("vxt", [P, 2, MEM])
        take = region(WORK + 48 * KB)
        qx = take("qx", [P, KD, T])
        take = region(WORK)
        px = take("px", [P, 2, TT, MEM])
        pxT = take("pxT", [P, 2, MT, T])
        take = region(WORK)
        sq = take("sq", [P, 4, T])
        skv = take("skv", [P, 2, T])
        su = take("su", [P, 4, T + 16])
        kk = take("kk", [P, 2, T])
        sv = take("sv", [P, TT, P])
        ps = take("ps", [P, 2, TT, T])
        psT = take("psT", [P, 2, TT, T])
        rope = take("rope", [P, 2, T])
        poolw = take("poolw", [P, 4, P])
        take = region(0)
        r1 = take("r1", [P, T])
        r2 = take("r2", [P, T])
        r3 = take("r3", [P, T])
        pa = take("pa", [P, T + 16])
        pb = take("pb", [P, T + 16])
        rcnt = take("rcnt", [P, T])
        take = region(WORK + 32 * KB)
        ob = take("ob", [P, 2, TT, P])
        assert ARENA >= WORK + 86 * KB, ARENA

        ident = mats[:, C_ID, :]

        def vcol(row):
            return vecs[:, row:row + 1]

        S_LB, S_OML, S_E0, S_E1, S_EPS5, S_EPS6, S_MX, S_NM, S_SM, S_RI = 0, 4, 8, 12, 16, 17, 20, 28, 36, 44

        class Phase:
            def __init__(self, name, kind, base, K, n, src):
                self.name, self.kind, self.base, self.K, self.n, self.src = name, kind, base, K, n, src

        phases, blocks = {}, []

        def add(name, kind, K, n, src):
            ph = Phase(name, kind, len(blocks), K, n, src)
            phases[name] = ph
            blocks.extend((ph, j) for j in range(n))

        def cols(w, k0, K, col):
            return w.rearrange("(k p) f -> p k f", p=P)[:, k0:k0 + K, bass.ds(col * P, P)]

        def add_ffn(name, wg, wu, wd):
            t0 = 0
            for part, n in enumerate(PARTS):
                def up(tile, odd, t0=t0):
                    return cols(wu if odd else wg, 0, KD, tile + t0)
                add(f"{name}_up{part}", "up", KD, 2 * n, up)
                add(f"{name}_down{part}", "down", n, KD, lambda j, t0=t0, n=n: cols(wd, t0, n, j))
                t0 += n

        IN_ORDER = list(range(4, 8)) + list(range(0, 4)) + list(range(8, 24))
        add_ffn("f1", A["ffn1_w_gate"][0], A["ffn1_w_up"][0], A["ffn1_w_down"][0])
        add("in", "lin", KD, 24, lambda j: cols(A["w_in"][0], 0, KD, IN_ORDER[j]))
        add("out", "lin", KD, KD, lambda j: cols(A["w_out"][0], 0, KD, j))
        add("mk", "lin", KD, KD, lambda j: cols(A["xa_w_k"][0], 0, KD, j))
        add("mv", "lin", KD, KD, lambda j: cols(A["xa_w_v"][0], 0, KD, j))
        add("xq", "lin", KD, KD, lambda j: cols(A["xa_w_q"][0], 0, KD, j))
        add("xo", "lin", KD, KD, lambda j: cols(A["xa_w_o"][0], 0, KD, j))
        add_ffn("f2", A["ffn2_w_gate"][0], A["ffn2_w_up"][0], A["ffn2_w_down"][0])
        add("in2", "lin", KD, 10, lambda j: cols(A["w_in_2"][0], 0, KD, j))
        add("out2", "lin", KD, KD, lambda j: cols(A["w_out_2"][0], 0, KD, j))
        add_ffn("f3", A["w_gate_2"][0], A["w_up_2"][0], A["w_down_2"][0])
        TILE0 = {"f1": 0, "f2": F // P, "f3": 2 * (F // P)}

        def part_tile0(name):
            return TILE0[name[:2]] + sum(PARTS[:int(name[-1])])

        raw_ready = [sem(f"raw_ready{i}") for i in range(RAW)]
        hi_ready = sem("hi_ready")
        lo_ready = sem("lo_ready")
        block_done = sem("block_done")
        bank_free = sem("bank_free")
        gate_done = sem("gate_done")
        value_done = sem("value_done")
        hidden_ready = sem("hidden_ready")
        act_ready = sem("act_ready")
        square_done = sem("square_done")
        sums_done = sem("sums_done")
        stat_mm = sem("stat_mm")
        var_ready = sem("var_ready")
        rstd_ready = sem("rstd_ready")
        normed = sem("normed")
        hi_act = sem("hi_act")
        lo_act = sem("lo_act")
        dve_chain = sem("dve_chain")
        act_chain = sem("act_chain")
        pool_chain = sem("pool_chain")

        def linker(eng, s):
            n = [0]

            def link(ins):
                n[0] += 1
                ins.then_inc(s, 1)
                eng.wait_ge(s, n[0])
            return link

        def slot_of(ph, jj, n):
            return (ph.base + jj) % n

        def each_block(eng, ph, step):
            loops = (ph.n - 4) // 4
            done = 0
            if loops >= 2:
                with eng.Fori(0, loops) as i:
                    for jj in range(4):
                        step(i, jj)
                done = 4 * loops
            for j in range(done, ph.n):
                step(0, j)

        def load_block(eng, ph, i, jj):
            b = ph.base + jj + 4 * i
            eng.wait_ge(lo_ready, b + 1)
            src = ph.src(2 * i + jj // 2, jj % 2) if ph.kind == "up" else ph.src(jj)
            slot = slot_of(ph, jj, RAW)
            dst = wraw[:, slot, 0:ph.K * P].rearrange("p (k f) -> p k f", f=P)
            eng.dma_start(dst, src).then_inc(raw_ready[slot], 16)

        def split_hi(eng, ph, i, jj):
            b = ph.base + jj + 4 * i
            n = ph.K * P
            slot, raw = slot_of(ph, jj, SPLIT), slot_of(ph, jj, RAW)
            eng.wait_ge(raw_ready[raw], 16 * ((ph.base + jj) // RAW + 1) + 16 * i)
            eng.wait_ge(block_done, b + 1)
            eng.copy(whi[:, slot, 0:n], wraw[:, raw, 0:n]).then_inc(hi_ready, 1)

        def split_lo(eng, ph, i, jj):
            b = ph.base + jj + 4 * i
            n = ph.K * P
            slot, raw = slot_of(ph, jj, SPLIT), slot_of(ph, jj, RAW)
            eng.wait_ge(hi_ready, b + 1)
            eng.tensor_tensor(wlo[:, slot, 0:n], wraw[:, raw, 0:n], whi[:, slot, 0:n],
                              ALU.subtract).then_inc(lo_ready, 1)

        def ahead(split, eng, ph, i, jj):
            if isinstance(i, int):
                b = ph.base + jj + 2
                if b < len(blocks):
                    split(eng, blocks[b][0], 0, blocks[b][1])
            else:
                split(eng, ph, i, jj + 2)

        def multiply(eng, ph, i, jj, xhi, xlo, width=T, ready=None):
            b = ph.base + jj + 4 * i
            slot = slot_of(ph, jj, SPLIT)
            o = bank[slot_of(ph, jj, RAW)][:, 0:width]
            eng.wait_ge(hi_ready, b + 1)
            eng.wait_ge(bank_free, b + 1)
            for k in range(ph.K):
                if ready is not None:
                    eng.wait_ge(*ready(k))
                w = whi[:, slot, k * P:(k + 1) * P]
                eng.matmul(o, w, xhi[:, k, :], start=(k == 0), stop=False)
                eng.matmul(o, w, xlo[:, k, :], start=False, stop=False)
            eng.wait_ge(lo_ready, RAW + b + 1)
            for k in range(ph.K):
                mm = eng.matmul(o, wlo[:, slot, k * P:(k + 1) * P], xhi[:, k, :],
                                start=False, stop=(k == ph.K - 1))
            mm.then_inc(block_done, 1)

        def bank_of(ph, jj):
            return bank[slot_of(ph, jj, RAW)]

        def wait_block(eng, ph, i, jj):
            eng.wait_ge(block_done, SPLIT + ph.base + jj + 4 * i + 1)

        NORMS = {"ln1": (0, True, V_LN1G, V_LN1B), "ln2": (1, True, V_LN2G, V_LN2B),
                 "ln3": (2, True, V_LN3G, V_LN3B), "ln4": (3, True, V_LN4G, V_LN4B),
                 "rms1": (4, False, V_N1, None), "rms2": (5, False, V_N2, None)}
        ACT0 = {"f1": 0, "in": 8, "out": 16, "xq": 24, "xo": 32, "f2": 40, "in2": 48, "out2": 56, "f3": 64}

        HI0 = {"ln1": 0, "ln2": 16, "ln3": 24, "rms1": 32, "rms2": 40}
        LO0 = {"rms1": ACT0["in2"], "rms2": ACT0["f3"]}

        s_x, s_mem, s_const, s_vec, s_ws, s_rows = (sem(n) for n in
                                                    ("x_loaded", "mem_loaded", "consts_loaded", "vectors_loaded",
                                                     "spatial_loaded", "rows_loaded"))
        s_xT = sem("x_transposed")
        s_xhi = sem("x_hi")
        s_vT0 = sem("vectors_transposed")
        s_vecs = sem("vectors_ready")
        s_lbe = sem("bound_exps")
        s_wsT = sem("spatial_transposed")
        s_wTz = sem("spatial_zeroed")
        s_wTr = sem("spatial_ready")
        s_out = sem("out_stored")
        s_oT = sem("out_transposed")
        s_ob = sem("out_copied")

        s_sig = sem("gates_sigmoid")
        s_fg = sem("forget_ready")
        s_lf = sem("log_forget")
        s_cum = sem("cum_ready")
        s_ivT = sem("values_transposed")
        s_ivc = sem("values_copied")
        s_arg = sem("decay_args")
        s_dexp = sem("decays")
        s_qk = sem("scaled_qk")
        s_smm = sem("score_products")
        s_put = sem("scores_put")
        s_az = sem("scores_zeroed")
        s_ebd = sem("exp_cum")
        s_kd = sem("key_decay_args")
        s_kde = sem("key_decays")
        s_ke = sem("end_keys")
        s_keT = sem("end_keys_transposed")
        s_kec = sem("end_keys_copied")
        s_um = sem("state_products")
        s_st = sem("states_ready")
        s_om = sem("outputs_product")
        s_osq = sem("outputs_squared")
        s_oss = sem("outputs_square_sum")
        s_ors = sem("outputs_rstd")
        s_on = sem("outputs_normed")
        s_act2 = sem("gates_activated")
        s_prod = sem("gated")
        s_gv = sem("gelu_done")
        s_gvT = sem("gelu_transposed")
        s_sgv = sem("spatial_var")
        s_sgr = sem("spatial_rstd")
        s_vn = sem("spatial_normed")
        s_sm = sem("spatial_products")
        s_so = sem("spatial_gated")
        s_mv = sem("mem_var")
        s_mr = sem("mem_rstd")
        s_mn = sem("mem_normed")
        s_mT = sem("mem_transposed")
        s_ma = sem("mem_affine")
        s_mh = sem("mem_hi")
        s_ml = sem("mem_lo")
        s_vxT = sem("mem_values_transposed")
        s_kv = sem("mem_kv_copied")
        s_sc = sem("scores")
        s_nm = sem("score_maxima")
        s_pe = sem("probabilities")
        s_pn = sem("probabilities_normed")
        s_pT = sem("probabilities_transposed")
        s_pcd = sem("probabilities_copied_dve")
        s_pca = sem("probabilities_copied_act")
        s_pv = sem("attended")
        s_ah = sem("attended_hi")
        s_rope = sem("rope_loaded")
        s_hsq = sem("head_squares")
        s_hss = sem("head_square_sums")
        s_hrs = sem("head_rstd")
        s_hn = sem("head_normed")
        s_hrot = sem("head_rotated")
        s_hr = sem("head_roped")
        s_dup = sem("keys_doubled")
        s_dupc = sem("keys_copied")
        s_svT = sem("self_values_transposed")
        s_pad = sem("pool_pads")
        s_pool = sem("pooled")
        s_rcn = sem("counts_loaded")
        s_pmm = sem("pool_products")
        s_py = sem("pool_out")
        s_pyh = sem("pool_out_hi")

        STEPS = [(h, n) for h in range(HG) for n in range(len(LEVELS) + 1)]
        SCALED = [s for s, (h, n) in enumerate(STEPS) if n < len(LEVELS)]
        NTH = {s: e for e, s in enumerate(SCALED)}
        plan = [("blk", j) for j in range(4)] + [("sig", h) for h in range(HG)]
        plan += [("blk", j) for j in range(4, 8)] + [("forget", h) for h in range(HG)]
        for h in range(HG):
            plan += [("blk", 8 + h), ("values", h)]
        tasks = []
        for s, (h, n) in enumerate(STEPS):
            tasks.append(("level", s))
            if n == len(LEVELS):
                tasks.append(("finish", h))
        per = -(-len(tasks) // 12)
        for j in range(12):
            plan += [("blk", 12 + j)] + tasks[per * j:per * (j + 1)]
        plan += [("silu", h) for h in range(HG)] + [("gate", h) for h in range(HG)]
        plan += [("gelu", g) for g in range(SG)] + [("spatial", g) for g in range(SG)]
        IN_DST = [(mk, h) for h in range(4)] + [(mq, h) for h in range(4)] + [(ivt, h % 2) for h in range(4)] + \
                 [(mg, h) for h in range(4)] + [(mu, h) for h in range(4)] + [(mv, h) for h in range(4)]

        def wait_in(eng, j):
            eng.wait_ge(bank_free, RAW + phases["in"].base + j + 1)

        def halves(t, lv):
            return t.rearrange("p (n two c) -> p n two c", two=2, c=1 << lv)

        block = ctx.enter_context(nc.Block())

        @block.sync
        def _(sp):
            def vec_rows(row, ap, n):
                sp.dma_start(vrow[row:row + n, :], ap).then_inc(s_vec, 16)

            sp.dma_start(mats[:, :, :], A["c_mats"].rearrange("n p f -> p n f")).then_inc(s_const, 16)
            sp.dma_start(xin[:, :, :], A["x"][0].rearrange("(n p) d -> p n d", p=P)).then_inc(s_x, 16)
            for row, name in ((V_LN1G, "ln1_g"), (V_LN1B, "ln1_b"), (V_LN2G, "ln2_g"), (V_LN2B, "ln2_b"),
                              (V_MEMG, "mem_ln_g"), (V_MEMB, "mem_ln_b"), (V_LN3G, "ln3_g"), (V_LN3B, "ln3_b"),
                              (V_LN4G, "ln4_g"), (V_LN4B, "ln4_b"), (V_N1, "norm1_g_2"), (V_N2, "norm2_g_2")):
                vec_rows(row, A[name].rearrange("o (k p) -> (o k) p", p=P), KD)
            vec_rows(V_POOLB, A["pool_b_2"][0], 4)
            vec_rows(V_POOLS, A["pool_scale_2"].rearrange("o (k p) -> (o k) p", p=P), 4)
            vec_rows(V_HGN, A["hg_norm_g"], 1)
            vec_rows(V_LB, A["hg_lb_logits"].rearrange("l h d -> (l h) d"), 8)
            for row, name in ((V_QN, "q_norm_g_2"), (V_KN, "k_norm_g_2")):
                for half in range(2):
                    sp.dma_start(vrow[row:row + 1, half * HD:(half + 1) * HD], A[name]).then_inc(s_vec, 16)
            sp.dma_start(masks[:, :, :], A["c_masks"].rearrange("n p f -> p n f")).then_inc(s_const, 16)
            sp.dma_start(restart[:, :], A["c_restart"].broadcast_to([P, T])).then_inc(s_const, 16)
            sp.dma_start(wsin[:, :, :], A["sg_w_s"][0].rearrange("g t s -> t g s")).then_inc(s_ws, 16)

            def stream(name):
                ph = phases[name]
                n4 = ph.n // 4
                if n4 >= 3:
                    if ph.kind == "up":
                        with sp.Fori(0, n4) as i:
                            for jj in range(4):
                                load_block(sp, ph, i, jj)
                        return
                for j in range(ph.n):
                    load_block(sp, ph, 0, j)

            def ffn(name):
                for part in range(len(PARTS)):
                    stream(f"{name}_up{part}")
                    stream(f"{name}_down{part}")

            ffn("f1")
            for j in range(4):
                load_block(sp, phases["in"], 0, j)
            wait_block(sp, phases["in"], 0, 0)
            for n, ap in enumerate((A["sg_ln_g"].rearrange("o g c -> o (g c)"), A["sg_ln_b"].rearrange("o g c -> o (g c)"),
                                    A["sg_b_s"].rearrange("o g c -> o (g c)"))):
                sp.dma_start(sgb[:, n, :], ap.broadcast_to([P, T])).then_inc(s_rows, 16)
            for j in range(4, 24):
                load_block(sp, phases["in"], 0, j)
            for j in range(4):
                load_block(sp, phases["out"], 0, j)
            sp.wait_ge(act_ready, ACT0["out"] + 8)
            sp.dma_start(memin[:, :, :], A["mem"][0].rearrange("(n p) d -> p n d", p=P)).then_inc(s_mem, 16)
            for j in range(4, KD):
                load_block(sp, phases["out"], 0, j)
            for name in ("mk", "mv", "xq", "xo"):
                stream(name)
            ffn("f2")
            stream("in2")
            wait_block(sp, phases["in2"], 0, 0)
            sp.dma_start(rope[:, :, :], A["c_rope"].rearrange("n p t -> p n t")).then_inc(s_rope, 16)
            sp.dma_start(poolw[:, :, :], A["pool_w_2"][0].rearrange("g c d -> c g d")).then_inc(s_rope, 16)
            for j in range(4):
                load_block(sp, phases["out2"], 0, j)
            sp.wait_ge(act_ready, ACT0["in2"] + 8)
            for g in range(4):
                if g:
                    sp.wait_ge(s_pool, g)
                sp.dma_start(rcnt[:, :], A["c_rcnt"][g:g + 1, :].broadcast_to([P, T])).then_inc(s_rcn, 16)
            for j in range(4, KD):
                load_block(sp, phases["out2"], 0, j)
            ffn("f3")
            for j in range(KD):
                sp.wait_ge(s_ob, j + 1)
                sp.dma_start(out[0].rearrange("(n p) d -> p n d", p=P)[:, :, j * P:(j + 1) * P],
                             ob[:, j % 2, :, :]).then_inc(s_out, 16)
                sp.wait_ge(s_out, 16 * (j + 1))

        @block.scalar
        def _(act):
            link = linker(act, act_chain)

            def hi_stream(ph, i, jj):
                ahead(split_hi, act, ph, i, jj)

            def silu_gate(ph, i, jj, t0):
                tile = t0 + 2 * i + jj // 2
                wait_block(act, ph, i, jj)
                act.wait_ge(value_done, tile + 1)
                act.activation(gate[:, (t0 + jj // 2) % 2, :], bank_of(ph, jj)[:, :], ACT.Silu).then_inc(gate_done, 1)

            def square_res(norm, j, ph=None):
                n = 8 * NORMS[norm][0] + j
                if ph:
                    act.wait_ge(bank_free, RAW + ph.base + j + 1)
                else:
                    act.wait_ge(normed, n - 8 + 1)
                act.wait_ge(sums_done, n + 1)
                act.activation(square[:, j % 2, :], res[:, j, :], ACT.Square).then_inc(square_done, 1)

            def norm_tail(norm, to_act=True):
                idx, centred, grow, brow = NORMS[norm]
                act.wait_ge(var_ready, idx + 1)
                link(act.activation(rstd[:, :], var[:, 1, :], ACT.Ln, bias=small[:, S_EPS6:S_EPS6 + 1] if not centred else small[:, S_EPS5:S_EPS5 + 1]))
                act.activation(rstd[:, :], rstd[:, :], ACT.Exp, scale=-0.5).then_inc(rstd_ready, 1)
                if not to_act:
                    return
                for k in range(KD):
                    act.wait_ge(normed, 8 * idx + k + 1)
                    src = res[:, k, :] if centred else hval[:, k % 2, :]
                    act.copy(ahi[:, k, :], src).then_inc(hi_act, 1)

            def ffn(name, norm):
                for part in range(len(PARTS)):
                    ph = phases[f"{name}_up{part}"]
                    t0 = part_tile0(ph.name)

                    def step(i, jj, ph=ph, t0=t0):
                        if jj % 2 == 0:
                            silu_gate(ph, i, jj, t0)
                        hi_stream(ph, i, jj)
                    each_block(act, ph, step)
                    ph = phases[f"{name}_down{part}"]
                    for j in range(KD):
                        hi_stream(ph, 0, j)
                        if norm and part == len(PARTS) - 1:
                            square_res(norm, j, ph)

            for b in range(2):
                split_hi(act, blocks[b][0], 0, blocks[b][1])
            for k in range(KD):
                act.wait_ge(s_xT, k + 1)
                act.copy(ahi[:, k, :], bank[4 + k % 4][:, :]).then_inc(s_xhi, 1)
            act.wait_ge(s_vecs, 2)
            act.activation(small[:, S_E0:S_E0 + 8], small[:, S_E0:S_E0 + 8], ACT.Exp).then_inc(s_lbe, 1)

            ffn("f1", "ln1")
            norm_tail("ln1")

            for kind, n in plan:
                if kind == "blk":
                    hi_stream(phases["in"], 0, n)
                elif kind == "sig":
                    wait_in(act, n)
                    link(act.activation(cum[:, n, :], mk[:, n, :], ACT.Sigmoid))
                    act.activation(mk[:, n, :], mk[:, n, :], ACT.Sigmoid, scale=-1.0).then_inc(s_sig, 1)
                elif kind == "forget":
                    act.wait_ge(s_fg, n + 1)
                    act.activation(cum[:, n, :], cum[:, n, :], ACT.Ln).then_inc(s_lf, 1)
                elif kind == "level":
                    if n in NTH:
                        e = NTH[n]
                        act.wait_ge(s_arg, e + 1)
                        act.activation(dec[:, e % 2, :], dec[:, e % 2, :], ACT.Exp).then_inc(s_dexp, 1)
                elif kind == "finish":
                    act.wait_ge(s_cum, n + 1)
                    if n:
                        act.wait_ge(s_on, n)
                    act.activation(eb[:, :], cum[:, n, :], ACT.Exp).then_inc(s_ebd, 1)
                    act.wait_ge(s_kd, n + 1)
                    act.activation(kend[:, :], kend[:, :], ACT.Exp).then_inc(s_kde, 1)
                    act.wait_ge(s_om, n + 1)
                    act.activation(osq[:, :], bank[6][:, :], ACT.Square).then_inc(s_osq, 1)
                    act.wait_ge(s_oss, n + 1)
                    link(act.activation(ors[:, :], bank[7][:, :], ACT.Ln, bias=small[:, S_EPS5:S_EPS5 + 1]))
                    act.activation(ors[:, :], ors[:, :], ACT.Exp, scale=-0.5).then_inc(s_ors, 1)
                elif kind == "silu":
                    wait_in(act, 12 + n)
                    act.activation(mg[:, n, :], mg[:, n, :], ACT.Silu).then_inc(s_act2, 1)
                elif kind == "gate":
                    act.wait_ge(s_prod, n + 1)
                    wait_block(act, phases["in"], 0, 23)
                    act.copy(ahi[:, n, :], mq[:, n, :]).then_inc(hi_act, 1)
                elif kind == "gelu":
                    wait_in(act, 20 + n)
                    act.activation(mv[:, n, :], mv[:, n, :], ACT.Gelu_apprx_tanh).then_inc(s_gv, 1)
                    act.activation(mu[:, n, :], mu[:, n, :], ACT.Gelu_apprx_tanh).then_inc(s_gv, 1)
                elif kind == "spatial":
                    act.wait_ge(s_sgv, n + 1)
                    link(act.activation(sgr[:, :], sgmv[:, :, 1], ACT.Ln, bias=small[:, S_EPS5:S_EPS5 + 1]))
                    act.activation(sgr[:, :], sgr[:, :], ACT.Exp, scale=-0.5).then_inc(s_sgr, 1)
                    act.wait_ge(s_so, 2 * n + 2)
                    act.copy(ahi[:, 4 + n, :], mu[:, n, :]).then_inc(hi_act, 1)

            for j in range(KD):
                hi_stream(phases["out"], 0, j)
                square_res("ln2", j, phases["out"])
            act.wait_ge(s_mv, 1)
            link(act.activation(mrs[:, :], mmv[:, :, 1], ACT.Ln, bias=small[:, S_EPS5:S_EPS5 + 1]))
            act.activation(mrs[:, :], mrs[:, :], ACT.Exp, scale=-0.5).then_inc(s_mr, 1)
            for k in range(KD):
                act.wait_ge(s_ma, k + 1)
                act.copy(mhi[:, k, :], mval[:, k % 2, :]).then_inc(s_mh, 1)
            norm_tail("ln2")
            for name in ("mk", "mv", "xq"):
                for j in range(KD):
                    hi_stream(phases[name], 0, j)
            def cross_exp(h):
                for t in range(TT):
                    act.wait_ge(s_nm, h + 1)
                    if t == 0 and h >= 2:
                        act.wait_ge(s_pT, 2 * (h - 1))
                    i = act.activation(px[:, h % 2, t, :], bank[2 * (h % 2) + t // 2][:, (t % 2) * MEM:(t % 2 + 1) * MEM],
                                       ACT.Exp, bias=small[:, S_NM + 4 * (h % 2) + t:S_NM + 4 * (h % 2) + t + 1],
                                       scale=(D // XH) ** -0.5,
                                       accum_out=small[:, S_SM + 4 * (h % 2) + t:S_SM + 4 * (h % 2) + t + 1])
                    i.then_inc(s_pe, 1)

            cross_exp(0)
            for h in range(XH):
                if h + 1 < XH:
                    cross_exp(h + 1)
                act.wait_ge(s_pT, 2 * h + 2)
                if h >= 2:
                    act.wait_ge(s_pv, 2 * (h - 1))
                act.copy(pxT[:, h % 2, 1, :], bank[5][:, :]).then_inc(s_pca, 1)
                for d in range(2):
                    act.wait_ge(s_pv, 2 * h + d + 1)
                    act.copy(ahi[:, 2 * h + d, :], bank[6 + d][:, :]).then_inc(s_ah, 1)
            for j in range(KD):
                hi_stream(phases["xo"], 0, j)
                square_res("ln3", j, phases["xo"])
            norm_tail("ln3")
            ffn("f2", "ln4")
            norm_tail("ln4", to_act=False)
            for j in range(KD):
                square_res("rms1", j)
            norm_tail("rms1")
            for j in range(10):
                hi_stream(phases["in2"], 0, j)
            for j in range(5):
                x = sq[:, j, :] if j < 4 else skv[:, 0, :]
                act.wait_ge(bank_free, RAW + phases["in2"].base + j + 1)
                if j:
                    act.wait_ge(s_hr, j)
                act.activation(r1[:, :], x, ACT.Square).then_inc(s_hsq, 1)
                act.wait_ge(s_hss, j + 1)
                link(act.activation(r2[:, :], bank[4][:, :], ACT.Ln, bias=small[:, S_EPS6:S_EPS6 + 1]))
                act.activation(r2[:, :], r2[:, :], ACT.Exp, scale=-0.5).then_inc(s_hrs, 1)
            for g in range(4):
                act.wait_ge(s_py, g + 1)
                act.copy(ahi[:, 4 + g, :], r3[:, :]).then_inc(s_pyh, 1)
            def self_exp(h):
                for t in range(TT):
                    n = TT * h + t
                    act.wait_ge(s_nm, XH + n + 1)
                    if t == 0 and h >= 2:
                        act.wait_ge(s_pT, 2 * XH + TT * (h - 1))
                    c = S_NM + n % 8
                    act.activation(ps[:, h % 2, t, :], bank[n % 3][:, :], ACT.Exp, bias=small[:, c:c + 1],
                                   scale=HD ** -0.5, accum_out=small[:, S_SM + n % 8:S_SM + n % 8 + 1]).then_inc(s_pe, 1)

            self_exp(0)
            for h in range(QH):
                if h + 1 < QH:
                    self_exp(h + 1)
                for st in (1, 3):
                    act.wait_ge(s_pT, 2 * XH + TT * h + st + 1)
                    if h >= 2:
                        act.wait_ge(s_pv, 2 * XH + h - 1)
                    act.copy(psT[:, h % 2, st, :], bank[3 + (TT * h + st) % 3][:, :]).then_inc(s_pca, 1)
                if h % 2 == 1:
                    act.wait_ge(s_pv, 2 * XH + h + 1)
                    act.copy(ahi[:, h // 2, :], bank[6 + (h // 2) % 2][:, :]).then_inc(s_ah, 1)
            for j in range(KD):
                hi_stream(phases["out2"], 0, j)
                square_res("rms2", j, phases["out2"])
            norm_tail("rms2")
            ffn("f3", None)

        @block.gpsimd
        def _(pool):
            link = linker(pool, pool_chain)

            def lo_stream(ph, i, jj):
                ahead(split_lo, pool, ph, i, jj)

            def add_sums(norm, j):
                idx, centred = NORMS[norm][:2]
                n = 8 * idx + j
                pool.wait_ge(square_done, n + 1)
                if j == 0:
                    if centred:
                        link(pool.tensor_copy(sum1[:, :], res[:, j, :]))
                    i = pool.tensor_copy(sum2[:, :], square[:, j % 2, :])
                else:
                    pool.wait_ge(sums_done, 2 + n)
                    if centred:
                        link(pool.tensor_tensor(sum1[:, :], sum1[:, :], res[:, j, :], ALU.add))
                    i = pool.tensor_tensor(sum2[:, :], sum2[:, :], square[:, j % 2, :], ALU.add)
                i.then_inc(sums_done, 1)

            def norm_tail(norm):
                idx, centred = NORMS[norm][:2]
                for k in range(KD):
                    pool.wait_ge(hi_act, HI0[norm] + k + 1)
                    src = res[:, k, :] if centred else hval[:, k % 2, :]
                    pool.tensor_tensor(alo[:, k, :], src, ahi[:, k, :], ALU.subtract).then_inc(act_ready, 1)

            def ffn(name, norm):
                for part in range(len(PARTS)):
                    ph = phases[f"{name}_up{part}"]
                    each_block(pool, ph, lambda i, jj, ph=ph: lo_stream(ph, i, jj))
                    ph = phases[f"{name}_down{part}"]
                    for j in range(KD):
                        lo_stream(ph, 0, j)
                        if norm and part == len(PARTS) - 1:
                            add_sums(norm, j)

            pool.sem_inc(lo_ready, RAW)
            pool.sem_inc(block_done, SPLIT)
            pool.sem_inc(bank_free, RAW)
            pool.sem_inc(value_done, 2)
            pool.sem_inc(hidden_ready, 2)
            pool.sem_inc(sums_done, 2)
            link(pool.memset(small[:, S_EPS5:S_EPS5 + 1], LN_EPS))
            link(pool.memset(small[:, S_EPS6:S_EPS6 + 1], RMS_EPS))
            pool.memset(wT[:, :, :], 0.0).then_inc(s_wTz, 1)
            for b in range(2):
                split_lo(pool, blocks[b][0], 0, blocks[b][1])
            ffn("f1", "ln1")
            norm_tail("ln1")
            zeroed = 0
            for kind, n in plan:
                if kind == "blk":
                    if n == 0:
                        wait_block(pool, phases["in"], 0, 0)
                        link(pool.memset(qt[:, :, :], 0.0))
                        pool.memset(kt[:, :, :], 0.0).then_inc(s_az, 1)
                        for h in range(2):
                            pool.memset(acc[:, h, :], 0.0).then_inc(s_az, 1)
                    lo_stream(phases["in"], 0, n)
                elif kind == "finish" and n + 2 < HG:
                    pool.wait_ge(s_om, n + 1)
                    pool.memset(acc[:, n % 2, :], 0.0).then_inc(s_az, 1)
                elif kind == "gate":
                    pool.wait_ge(hi_act, 8 + n + 1)
                    pool.tensor_tensor(alo[:, n, :], mq[:, n, :], ahi[:, n, :], ALU.subtract).then_inc(act_ready, 1)
                elif kind == "spatial":
                    pool.wait_ge(hi_act, 8 + 4 + n + 1)
                    pool.tensor_tensor(alo[:, 4 + n, :], mu[:, n, :], ahi[:, 4 + n, :], ALU.subtract).then_inc(act_ready, 1)
            for j in range(KD):
                lo_stream(phases["out"], 0, j)
                add_sums("ln2", j)
            for k in range(KD):
                pool.wait_ge(s_mh, k + 1)
                pool.tensor_tensor(mlo[:, k, :], mval[:, k % 2, :], mhi[:, k, :], ALU.subtract).then_inc(s_ml, 1)
            norm_tail("ln2")
            for name in ("mk", "mv", "xq"):
                for j in range(KD):
                    lo_stream(phases[name], 0, j)
            for j in range(KD):
                lo_stream(phases["xo"], 0, j)
                add_sums("ln3", j)
            norm_tail("ln3")
            ffn("f2", "ln4")
            for j in range(KD):
                add_sums("rms1", j)
            norm_tail("rms1")
            for j in range(10):
                lo_stream(phases["in2"], 0, j)
            for g in range(4):
                pool.wait_ge(bank_free, RAW + phases["in2"].base + 6 + g + 1)
                if g:
                    pool.wait_ge(s_pmm, g)
                src = su[:, g, :]
                bufs = [pa, pb]
                for lv in range(g + 1):
                    w = (1 << lv) // 2
                    reach = (1 << g) - (1 << lv)
                    lo, n = 8 - reach, T + 2 * reach
                    dst = bufs[lv % 2]
                    a0, a1 = (lo - 1, lo) if lv == 0 else (lo - w, lo + w)
                    link(pool.tensor_tensor(dst[:, lo:lo + n], src[:, a0:a0 + n], src[:, a1:a1 + n], ALU.add))
                    src = dst
                pool.wait_ge(s_rcn, 16 * (g + 1))
                link(pool.tensor_tensor(src[:, 8:8 + T], src[:, 8:8 + T], rcnt[:, :], ALU.mult))
                pool.tensor_tensor(su[:, g, 8:8 + T], src[:, 8:8 + T], su[:, g, 8:8 + T], ALU.subtract).then_inc(s_pool, 1)
            for j in range(KD):
                lo_stream(phases["out2"], 0, j)
                add_sums("rms2", j)
            norm_tail("rms2")
            ffn("f3", None)

        @block.vector
        def _(dve):
            link = linker(dve, dve_chain)

            def hidden(ph, i, jj, t0, scale):
                tile = t0 + 2 * i + jj // 2
                slot = (t0 + jj // 2) % 2
                at = 2 * i + jj // 2
                wait_block(dve, ph, i, jj)
                dve.wait_ge(gate_done, tile + 1)
                dve.wait_ge(hidden_ready, tile + 1)
                dve.scalar_tensor_tensor(out=hval[:, slot, :], in0=gate[:, slot, :], scalar=scale,
                                         in1=bank_of(ph, jj)[:, :], op0=ALU.mult, op1=ALU.mult).then_inc(value_done, 1)
                dve.wait_ge(value_done, 2 + tile + 1)
                dve.tensor_copy(hhi[:, bass.ds(at, 1), :].rearrange("p a t -> p (a t)"), hval[:, slot, :]).then_inc(bank_free, 2)
                dve.wait_ge(bank_free, RAW + ph.base + jj + 4 * i + 1)
                dve.tensor_tensor(hlo[:, bass.ds(at, 1), :].rearrange("p a t -> p (a t)"), hval[:, slot, :],
                                  hhi[:, bass.ds(at, 1), :].rearrange("p a t -> p (a t)"), ALU.subtract).then_inc(hidden_ready, 1)

            def add_res(ph, j, scale):
                wait_block(dve, ph, 0, j)
                dve.scalar_tensor_tensor(out=res[:, j, :], in0=res[:, j, :], scalar=scale,
                                         in1=bank_of(ph, j)[:, :], op0=ALU.mult, op1=ALU.add).then_inc(bank_free, 1)

            def norm_tail(norm):
                idx, centred, grow, brow = NORMS[norm]
                dve.wait_ge(stat_mm, idx + 1)
                if centred:
                    link(dve.tensor_copy(mean[:, :], bank[4][:, :]))
                    link(dve.tensor_tensor(var[:, 0, :], mean[:, :], mean[:, :], ALU.mult))
                    link(dve.tensor_tensor(var[:, 1, :], bank[5][:, :], var[:, 0, :], ALU.subtract))
                    dve.tensor_scalar(var[:, 1, :], var[:, 1, :], 0.0, None, ALU.max).then_inc(var_ready, 1)
                else:
                    dve.tensor_copy(var[:, 1, :], bank[5][:, :]).then_inc(var_ready, 1)
                dve.wait_ge(rstd_ready, idx + 1)
                for k in range(KD):
                    if centred:
                        link(dve.tensor_tensor(res[:, k, :], res[:, k, :], mean[:, :], ALU.subtract))
                        link(dve.tensor_tensor(res[:, k, :], res[:, k, :], rstd[:, :], ALU.mult))
                        i = dve.tensor_scalar(res[:, k, :], res[:, k, :], vcol(grow + k), vcol(brow + k), ALU.mult, ALU.add)
                    else:
                        if k >= 2:
                            dve.wait_ge(act_ready, LO0[norm] + k - 1)
                        i = dve.scalar_tensor_tensor(out=hval[:, k % 2, :], in0=res[:, k, :], scalar=vcol(grow + k),
                                                     in1=rstd[:, :], op0=ALU.mult, op1=ALU.mult)
                    i.then_inc(normed, 1)

            def ffn(name, alpha, scale, norm):
                for part in range(len(PARTS)):
                    ph = phases[f"{name}_up{part}"]
                    t0 = part_tile0(ph.name)

                    def step(i, jj, ph=ph, t0=t0):
                        if jj % 2:
                            hidden(ph, i, jj, t0, scale)
                    each_block(dve, ph, step)
                    ph = phases[f"{name}_down{part}"]
                    last = part == len(PARTS) - 1
                    for j in range(KD):
                        add_res(ph, j, alpha if part == 0 else 1.0)
                        if last and norm is None and j >= 1:
                            store_tile(j - 1)
                if norm is None:
                    store_tile(KD - 1)

            def store_tile(j):
                dve.wait_ge(s_oT, j + 1)
                if j >= 2:
                    dve.wait_ge(s_out, 16 * (j - 1))
                dve.tensor_copy(ob[:, j % 2, :, :], bank[4 + j % 2][:, :].rearrange("p (n f) -> p n f", f=P)).then_inc(s_ob, 1)

            for k in range(KD):
                dve.wait_ge(s_xhi, k + 1)
                link(dve.tensor_copy(res[:, k, :], bank[4 + k % 4][:, :]))
                dve.tensor_tensor(alo[:, k, :], bank[4 + k % 4][:, :], ahi[:, k, :], ALU.subtract).then_inc(act_ready, 1)
            dve.wait_ge(s_vT0, 1)
            dve.tensor_copy(vecs[:, 0:V_ROWS], bank[4][:, 0:V_ROWS]).then_inc(s_vecs, 1)
            dve.wait_ge(s_vecs, 1)
            link(dve.tensor_tensor(small[:, S_LB:S_LB + 4], vecs[:, V_LB:V_LB + 4], vecs[:, V_LB + 4:V_LB + 8], ALU.max))
            link(dve.tensor_tensor(small[:, S_E0:S_E0 + 4], vecs[:, V_LB:V_LB + 4], small[:, S_LB:S_LB + 4], ALU.subtract))
            dve.tensor_tensor(small[:, S_E1:S_E1 + 4], vecs[:, V_LB + 4:V_LB + 8], small[:, S_LB:S_LB + 4], ALU.subtract).then_inc(s_vecs, 1)
            dve.wait_ge(s_wsT, 1)
            dve.wait_ge(s_wTz, 1)
            dve.wait_ge(s_const, 48)
            dve.copy_predicated(wT[:, :, :], masks[:, len(LEVELS) + 1:len(LEVELS) + 2, :].broadcast_to([P, SG, P]),
                                bank[5][:, :].rearrange("p (g t) -> p g t", g=SG)).then_inc(s_wTr, 1)
            dve.wait_ge(s_lbe, 1)
            link(dve.tensor_tensor(small[:, S_OML:S_OML + 4], small[:, S_E0:S_E0 + 4], small[:, S_E1:S_E1 + 4], ALU.add))
            link(dve.reciprocal(small[:, S_OML:S_OML + 4], small[:, S_OML:S_OML + 4]))
            link(dve.tensor_tensor(small[:, S_LB:S_LB + 4], small[:, S_E0:S_E0 + 4], small[:, S_OML:S_OML + 4], ALU.mult))
            link(dve.tensor_scalar(small[:, S_OML:S_OML + 4], small[:, S_LB:S_LB + 4], -1.0, 1.0, ALU.mult, ALU.add))

            ffn("f1", ALPHA, 0.5, "ln1")
            norm_tail("ln1")

            def level_args(s):
                h, n = STEPS[s]
                e, lv = NTH[s], LEVELS[n]
                b, o = halves(cum[:, h, :], lv), halves(dec[:, e % 2, :], lv)
                c = 1 << lv
                ref = b[:, :, 0, c - 1:c].broadcast_to([P, T // (2 * c), c])
                if e >= 2:
                    dve.wait_ge(s_qk, e - 1)
                dve.tensor_tensor(o[:, :, 0, :], ref, b[:, :, 0, :], ALU.subtract)
                dve.tensor_tensor(o[:, :, 1, :], b[:, :, 1, :], ref, ALU.subtract).then_inc(s_arg, 1)

            def level_scale(s):
                h, n = STEPS[s]
                e, lv = NTH[s], LEVELS[n]
                d = halves(dec[:, e % 2, :], lv)
                dve.wait_ge(s_dexp, e + 1)
                if e >= 2:
                    dve.wait_ge(s_smm, SCALED[e - 2] + 1)
                else:
                    dve.wait_ge(s_az, 1)
                dve.tensor_tensor(halves(qt[:, e % 2, :], lv)[:, :, 1, :], halves(mq[:, h, :], lv)[:, :, 1, :],
                                  d[:, :, 1, :], ALU.mult)
                dve.tensor_tensor(halves(kt[:, e % 2, :], lv)[:, :, 0, :], halves(mk[:, h, :], lv)[:, :, 0, :],
                                  d[:, :, 0, :], ALU.mult).then_inc(s_qk, 1)

            def level_put(s):
                h, n = STEPS[s]
                dve.wait_ge(s_smm, s + 1)
                dve.wait_ge(s_az, 1 + h + 1)
                if s:
                    dve.wait_ge(s_put, s)
                dve.copy_predicated(acc[:, h % 2, :].rearrange("p (n t) -> p n t", t=P),
                                    masks[:, n:n + 1, :].broadcast_to([P, TT, P]),
                                    bank[4 + s % 2][:, :].rearrange("p (n t) -> p n t", t=P)).then_inc(s_put, 1)

            for kind, n in plan:
                if kind == "blk":
                    wait_block(dve, phases["in"], 0, n)
                    dst, at = IN_DST[n]
                    if 10 <= n < 12:
                        dve.wait_ge(s_ivT, n - 9)
                    dve.tensor_copy(dst[:, at, :], bank_of(phases["in"], n)[:, :]).then_inc(bank_free, 1)
                elif kind == "forget":
                    lb, oml = small[:, S_LB + n:S_LB + n + 1], small[:, S_OML + n:S_OML + n + 1]
                    dve.wait_ge(s_sig, n + 1)
                    link(dve.tensor_scalar(cum[:, n, :], cum[:, n, :], oml, lb, ALU.mult, ALU.add))
                    link(dve.tensor_scalar(cum[:, n, :], cum[:, n, :], 2.0 ** -60, None, ALU.max))
                    dve.tensor_scalar(mk[:, n, :], mk[:, n, :], oml, None, ALU.mult).then_inc(s_fg, 1)
                elif kind == "values":
                    if n == 0:
                        for h in range(HG):
                            dve.wait_ge(s_lf, h + 1)
                            dve.tensor_tensor_scan(cum[:, h, :], restart[:, :], cum[:, h, :], 0.0, ALU.mult, ALU.add).then_inc(s_cum, 1)
                    dve.wait_ge(s_ivT, n + 1)
                    dve.tensor_copy(vT[:, n, :, :], bank[6 + n % 2][:, :].rearrange("p (n f) -> p n f", f=P)).then_inc(s_ivc, 1)
                elif kind == "level":
                    if n in NTH:
                        if n == 0:
                            dve.wait_ge(s_cum, HG)
                        level_args(n)
                    if n >= 1 and (n - 1) in NTH:
                        level_scale(n - 1)
                    if n >= 2 and STEPS[n - 2][0] == STEPS[n][0]:
                        level_put(n - 2)
                    if STEPS[n][1] == len(LEVELS):
                        level_put(n - 1)
                        level_put(n)
                elif kind == "finish":
                    c, q, k = cum[:, n, :], mq[:, n, :], mk[:, n, :]
                    dve.wait_ge(s_ebd, n + 1)
                    link(dve.tensor_tensor(qe[:, :], q, eb[:, :], ALU.mult))
                    ct = c.rearrange("p (n t) -> p n t", t=P)
                    dve.tensor_tensor(kend[:, :].rearrange("p (n t) -> p n t", t=P), ct[:, 0:3, P - 1:P].broadcast_to([P, 3, P]),
                                      ct[:, 0:3, :], ALU.subtract).then_inc(s_kd, 1)
                    dve.wait_ge(s_kde, n + 1)
                    dve.tensor_tensor(kend[:, :], kend[:, :], k[:, 0:3 * P], ALU.mult).then_inc(s_ke, 1)
                    dve.wait_ge(s_keT, n + 1)
                    dve.tensor_copy(kendT[:, :], bank[6][:, 0:3 * P]).then_inc(s_kec, 1)
                    dve.wait_ge(s_um, n + 1)
                    link(dve.tensor_copy(state[:, 0, :], bank[7][:, 0:P]))
                    for j in range(1, 3):
                        i = dve.scalar_tensor_tensor(out=state[:, j, :], in0=state[:, j - 1, :],
                                                     scalar=eb[:, (j + 1) * P - 1:(j + 1) * P],
                                                     in1=bank[7][:, j * P:(j + 1) * P], op0=ALU.mult, op1=ALU.add)
                        if j == 1:
                            link(i)
                    i.then_inc(s_st, 1)
                    dve.wait_ge(s_ors, n + 1)
                    dve.scalar_tensor_tensor(out=q, in0=bank[6][:, :], scalar=vcol(V_HGN), in1=ors[:, :],
                                             op0=ALU.mult, op1=ALU.mult).then_inc(s_on, 1)
                elif kind == "gate":
                    dve.wait_ge(s_act2, n + 1)
                    dve.wait_ge(s_on, n + 1)
                    dve.tensor_tensor(mq[:, n, :], mq[:, n, :], mg[:, n, :], ALU.mult).then_inc(s_prod, 1)
                elif kind == "spatial":
                    pb_ = bank[4 + n % 2]
                    pt = pb_[:, :].rearrange("p (n f) -> p n f", f=P)
                    dve.wait_ge(s_gvT, n + 1)
                    for t in range(TT):
                        link(dve.bn_stats(sgst[:, t, :], pb_[:, t * P:(t + 1) * P]))
                    for t in range(TT):
                        i = dve.bn_aggr(sgmv[:, t, :], sgst[:, t, :])
                        if t < TT - 1:
                            link(i)
                    i.then_inc(s_sgv, 1)
                    dve.wait_ge(s_sgr, n + 1)
                    for t in range(TT):
                        link(dve.tensor_scalar(vn[:, n, t * P:(t + 1) * P], pb_[:, t * P:(t + 1) * P],
                                               sgmv[:, t, 0:1], sgr[:, t:t + 1], ALU.subtract, ALU.mult))
                    v3 = vn[:, n, :].rearrange("p (n f) -> p n f", f=P)

                    def row(r):
                        return sgb[:, r, n * P:(n + 1) * P].unsqueeze(1).broadcast_to([P, TT, P])
                    dve.wait_ge(s_rows, 48)
                    link(dve.tensor_tensor(v3, v3, row(0), ALU.mult))
                    dve.tensor_tensor(v3, v3, row(1), ALU.add).then_inc(s_vn, 1)
                    dve.wait_ge(s_sm, n + 1)
                    dve.tensor_tensor(mv[:, n, :].rearrange("p (n f) -> p n f", f=P),
                                      bank[6 + n % 2][:, :].rearrange("p (n f) -> p n f", f=P), row(2), ALU.add).then_inc(s_so, 1)
                    dve.wait_ge(s_so, 2 * n + 1)
                    dve.tensor_tensor(mu[:, n, :], mu[:, n, :], mv[:, n, :], ALU.mult).then_inc(s_so, 1)

            for j in range(KD):
                add_res(phases["out"], j, ALPHA)
                if j == 4:
                    dve.wait_ge(s_mem, 16)
                    for t in range(MT):
                        for hf in range(2):
                            link(dve.bn_stats(mst[:, 2 * t + hf, :], memin[:, t, hf * T:(hf + 1) * T]))
                    for t in range(MT):
                        link(dve.bn_aggr(mmv[:, t, :], mst[:, 2 * t:2 * t + 2, :].rearrange("p a b -> p (a b)")))
                    dve.sem_inc(s_mv, 1)
            dve.wait_ge(s_mr, 1)
            for t in range(MT):
                dve.tensor_scalar(memin[:, t, :], memin[:, t, :], mmv[:, t, 0:1], mrs[:, t:t + 1],
                                  ALU.subtract, ALU.mult).then_inc(s_mn, 1)
            for k in range(KD):
                dve.wait_ge(s_mT, k + 1)
                if k >= 2:
                    dve.wait_ge(s_ml, k - 1)
                dve.tensor_scalar(mval[:, k % 2, :], bank[6 + k % 2][:, 0:MEM], vcol(V_MEMG + k), vcol(V_MEMB + k),
                                  ALU.mult, ALU.add).then_inc(s_ma, 1)
            norm_tail("ln2")
            for j in range(KD):
                wait_block(dve, phases["mk"], 0, j)
                dve.tensor_copy(kx[:, j, :], bank_of(phases["mk"], j)[:, 0:MEM]).then_inc(bank_free, 1)
            for j in range(KD):
                wait_block(dve, phases["mv"], 0, j)
                if j >= 2:
                    dve.wait_ge(s_vxT, j - 1)
                dve.tensor_copy(vxt[:, j % 2, :], bank_of(phases["mv"], j)[:, 0:MEM]).then_inc(bank_free, 1)
                if j >= 1:
                    dve.wait_ge(s_vxT, j)
                    dve.tensor_copy(vx[:, :, (j - 1) * P:j * P], bank[4 + (j - 1) % 2][:, 0:MEM].rearrange("p (n f) -> p n f", f=P)).then_inc(s_kv, 1)
            dve.wait_ge(s_vxT, KD)
            dve.tensor_copy(vx[:, :, (KD - 1) * P:KD * P], bank[4 + (KD - 1) % 2][:, 0:MEM].rearrange("p (n f) -> p n f", f=P)).then_inc(s_kv, 1)
            for j in range(KD):
                wait_block(dve, phases["xq"], 0, j)
                dve.tensor_copy(qx[:, j, :], bank_of(phases["xq"], j)[:, :]).then_inc(bank_free, 1)
            def cross_max(h):
                m0 = S_MX + 4 * (h % 2)
                dve.wait_ge(s_sc, h + 1)
                for half in range(2):
                    link(dve.tensor_reduce(small[:, m0 + 2 * half:m0 + 2 * half + 2],
                                           bank[2 * (h % 2) + half][:, :].rearrange("p (n m) -> p n m", m=MEM), AX.X, ALU.max))
                n0 = S_NM + 4 * (h % 2)
                dve.tensor_scalar(small[:, n0:n0 + 4], small[:, m0:m0 + 4], -(D // XH) ** -0.5, None, ALU.mult).then_inc(s_nm, 1)

            cross_max(0)
            for h in range(XH):
                r0 = S_RI + 4 * (h % 2)
                dve.wait_ge(s_pe, TT * (h + 1))
                link(dve.reciprocal(small[:, r0:r0 + 4], small[:, S_SM + 4 * (h % 2):S_SM + 4 * (h % 2) + 4]))
                for t in range(TT):
                    dve.tensor_scalar(px[:, h % 2, t, :], px[:, h % 2, t, :], small[:, r0 + t:r0 + t + 1], None,
                                      ALU.mult).then_inc(s_pn, 1)
                if h + 1 < XH:
                    cross_max(h + 1)
                dve.wait_ge(s_pT, 2 * h + 1)
                if h >= 2:
                    dve.wait_ge(s_pv, 2 * (h - 1))
                dve.tensor_copy(pxT[:, h % 2, 0, :], bank[4][:, :]).then_inc(s_pcd, 1)
                for d in range(2):
                    dve.wait_ge(s_ah, 2 * h + d + 1)
                    dve.tensor_tensor(alo[:, 2 * h + d, :], bank[6 + d][:, :], ahi[:, 2 * h + d, :], ALU.subtract).then_inc(act_ready, 1)
            for j in range(KD):
                add_res(phases["xo"], j, ALPHA)
            norm_tail("ln3")
            ffn("f2", ALPHA, 0.5, "ln4")
            norm_tail("ln4")
            norm_tail("rms1")
            ph = phases["in2"]
            for j in range(10):
                wait_block(dve, ph, 0, j)
                if j == 6:
                    link(dve.memset(su[:, :, 0:8], 0.0))
                    link(dve.memset(su[:, :, 8 + T:16 + T], 0.0))
                dst = sq[:, j, :] if j < 4 else skv[:, j - 4, :] if j < 6 else su[:, j - 6, 8:8 + T]
                dve.tensor_copy(dst, bank_of(ph, j)[:, :]).then_inc(bank_free, 1)
            dve.wait_ge(s_rope, 32)
            for j in range(5):
                x = sq[:, j, :] if j < 4 else skv[:, 0, :]
                dve.wait_ge(s_hrs, j + 1)
                dve.scalar_tensor_tensor(out=x, in0=x, scalar=vcol(V_QN if j < 4 else V_KN), in1=r2[:, :],
                                         op0=ALU.mult, op1=ALU.mult).then_inc(s_hn, 1)
                dve.wait_ge(s_hrot, j + 1)
                link(dve.tensor_tensor(r3[:, :], bank[5][:, :], rope[:, 1, :], ALU.mult))
                link(dve.tensor_tensor(x, x, rope[:, 0, :], ALU.mult))
                dve.tensor_tensor(x, x, r3[:, :], ALU.add).then_inc(s_hr, 1)
                dve.wait_ge(s_hr, j + 1)
            for g in range(2):
                dve.wait_ge(s_dup, g + 1)
                dve.tensor_copy(kk[:, g, :], bank[6 + g][:, :]).then_inc(s_dupc, 1)
            dve.wait_ge(s_svT, 1)
            dve.tensor_copy(sv[:, :, :], bank[4][:, :].rearrange("p (n f) -> p n f", f=P)).then_inc(s_dupc, 1)
            for g in range(4):
                dve.wait_ge(s_pmm, g + 1)
                if g:
                    dve.wait_ge(act_ready, ACT0["out2"] + g)
                dve.tensor_scalar(r3[:, :], bank[4 + g % 2][:, :], vcol(V_POOLB + g), vcol(V_POOLS + g),
                                  ALU.add, ALU.mult).then_inc(s_py, 1)
                dve.wait_ge(s_pyh, g + 1)
                dve.tensor_tensor(alo[:, 4 + g, :], r3[:, :], ahi[:, 4 + g, :], ALU.subtract).then_inc(act_ready, 1)
            def self_max(h):
                for t in range(TT):
                    n = TT * h + t
                    c = n % 8
                    dve.wait_ge(s_sc, XH + n + 1)
                    link(dve.tensor_reduce(small[:, S_MX + c:S_MX + c + 1], bank[n % 3][:, :], AX.X, ALU.max))
                    dve.tensor_scalar(small[:, S_NM + c:S_NM + c + 1], small[:, S_MX + c:S_MX + c + 1], -HD ** -0.5, None,
                                      ALU.mult).then_inc(s_nm, 1)

            self_max(0)
            for h in range(QH):
                for t in range(TT):
                    n = TT * h + t
                    c = n % 8
                    dve.wait_ge(s_pe, TT * XH + n + 1)
                    link(dve.reciprocal(small[:, S_RI + c:S_RI + c + 1], small[:, S_SM + c:S_SM + c + 1]))
                    dve.tensor_scalar(ps[:, h % 2, t, :], ps[:, h % 2, t, :], small[:, S_RI + c:S_RI + c + 1], None,
                                      ALU.mult).then_inc(s_pn, 1)
                if h + 1 < QH:
                    self_max(h + 1)
                for st in (0, 2):
                    dve.wait_ge(s_pT, 2 * XH + TT * h + st + 1)
                    if h >= 2:
                        dve.wait_ge(s_pv, 2 * XH + h - 1)
                    dve.tensor_copy(psT[:, h % 2, st, :], bank[3 + (TT * h + st) % 3][:, :]).then_inc(s_pcd, 1)
                if h % 2 == 1:
                    dve.wait_ge(s_ah, 2 * XH + h // 2 + 1)
                    dve.tensor_tensor(alo[:, h // 2, :], bank[6 + (h // 2) % 2][:, :], ahi[:, h // 2, :],
                                      ALU.subtract).then_inc(act_ready, 1)
            for j in range(KD):
                add_res(phases["out2"], j, 1.0)
            norm_tail("rms2")
            ffn("f3", 1.0, 1.0, None)

        @block.tensor
        def _(pe):
            def linear(name, act0, xhi=None, xlo=None, width=T, ready=None, after=None):
                ph = phases[name]
                for j in range(ph.n):
                    r = ready if j == 0 else None
                    multiply(pe, ph, 0, j, ahi if xhi is None else xhi, alo if xlo is None else xlo, width, r)
                    if after:
                        after(j)

            def acts(base):
                return lambda k: (act_ready, base + k + 1)

            def stats(norm):
                idx, centred = NORMS[norm][:2]
                pe.wait_ge(sums_done, 2 + 8 * (idx + 1))
                if centred:
                    pe.matmul(bank[4][:, :], mats[:, C_MEAN, :], sum1[:, :], start=True, stop=True)
                pe.matmul(bank[5][:, :], mats[:, C_MEAN, :], sum2[:, :], start=True, stop=True).then_inc(stat_mm, 1)

            def ffn(name, norm):
                for part in range(len(PARTS)):
                    ph = phases[f"{name}_up{part}"]
                    if part == 0:
                        r = acts(ACT0[name])
                        multiply(pe, ph, 0, 0, ahi, alo, T, r)
                        for jj in range(1, 4):
                            multiply(pe, ph, 0, jj, ahi, alo)
                        start = 1
                    else:
                        start = 0
                    with pe.Fori(start, ph.n // 4) as i:
                        for jj in range(4):
                            multiply(pe, ph, i, jj, ahi, alo)
                    ph = phases[f"{name}_down{part}"]
                    t0 = part_tile0(ph.name)
                    for j in range(KD):
                        r = (lambda k: (hidden_ready, 2 + t0 + k + 1)) if j == 0 else None
                        multiply(pe, ph, 0, j, hhi, hlo, T, r)
                        if norm is None and part == len(PARTS) - 1 and j >= 1:
                            store_tile(ph, j - 1)
                if norm:
                    stats(norm)
                else:
                    store_tile(ph, KD - 1)

            def store_tile(ph, j):
                pe.wait_ge(bank_free, RAW + ph.base + j + 1)
                if j >= 2:
                    pe.wait_ge(s_ob, j - 1)
                for t in range(TT):
                    i = pe.transpose(bank[4 + j % 2][:, t * P:(t + 1) * P], res[:, j, t * P:(t + 1) * P], ident)
                i.then_inc(s_oT, 1)

            def four(o, src, s):
                for t in range(TT):
                    i = pe.transpose(o[:, t * P:(t + 1) * P], src[:, t * P:(t + 1) * P], ident)
                i.then_inc(s, 1)

            pe.wait_ge(s_const, 48)
            pe.wait_ge(s_x, 16)
            for k in range(KD):
                if k >= 4:
                    pe.wait_ge(act_ready, k - 3)
                for t in range(TT):
                    i = pe.transpose(bank[4 + k % 4][:, t * P:(t + 1) * P], xin[:, t, k * P:(k + 1) * P], ident)
                i.then_inc(s_xT, 1)
            pe.wait_ge(s_vec, 16 * 20)
            pe.wait_ge(act_ready, 5)
            pe.transpose(bank[4][:, 0:V_ROWS], vrow[0:V_ROWS, :], ident[0:V_ROWS, 0:V_ROWS]).then_inc(s_vT0, 1)
            pe.wait_ge(s_ws, 16)
            pe.wait_ge(act_ready, 6)
            for g in range(SG):
                i = pe.transpose(bank[5][:, g * P:(g + 1) * P], wsin[:, g, :], ident)
            i.then_inc(s_wsT, 1)
            ffn("f1", "ln1")

            def level_product(s):
                h, n = STEPS[s]
                if n < len(LEVELS):
                    e = NTH[s]
                    pe.wait_ge(s_qk, e + 1)
                    q, k = qt[:, e % 2, :], kt[:, e % 2, :]
                else:
                    q, k = mq[:, h, :], mk[:, h, :]
                if s >= 2:
                    pe.wait_ge(s_put, s - 1)
                for t in range(TT):
                    i = pe.matmul(bank[4 + s % 2][:, t * P:(t + 1) * P], k[:, t * P:(t + 1) * P], q[:, t * P:(t + 1) * P],
                                  start=True, stop=True)
                i.then_inc(s_smm, 1)

            ph = phases["in"]
            pe.wait_ge(var_ready, 1)
            for kind, n in plan:
                if kind == "blk":
                    multiply(pe, ph, 0, n, ahi, alo, T, acts(ACT0["in"]) if n == 0 else None)
                elif kind == "values":
                    wait_in(pe, 8 + n)
                    if n >= 2:
                        pe.wait_ge(s_ivc, n - 1)
                    four(bank[6 + n % 2], ivt[:, n % 2, :], s_ivT)
                elif kind == "level":
                    if n >= 1 and STEPS[n - 1][0] == STEPS[n][0]:
                        level_product(n - 1)
                    if STEPS[n][1] == len(LEVELS):
                        level_product(n)
                elif kind == "finish":
                    o, u = bank[6], bank[7]
                    pe.wait_ge(s_ke, n + 1)
                    pe.wait_ge(s_ivc, HG)
                    if n:
                        pe.wait_ge(s_on, n)
                    for t in range(3):
                        i = pe.transpose(o[:, t * P:(t + 1) * P], kend[:, t * P:(t + 1) * P], ident)
                    i.then_inc(s_keT, 1)
                    pe.wait_ge(s_kec, n + 1)
                    for t in range(3):
                        i = pe.matmul(u[:, t * P:(t + 1) * P], kendT[:, t * P:(t + 1) * P], vT[:, n, t, :], start=True, stop=True)
                    i.then_inc(s_um, 1)
                    pe.wait_ge(s_st, n + 1)
                    pe.wait_ge(s_put, (n + 1) * (len(LEVELS) + 1))
                    for t in range(TT):
                        ot = o[:, t * P:(t + 1) * P]
                        i = pe.matmul(ot, vT[:, n, t, :], acc[:, n % 2, t * P:(t + 1) * P], start=True, stop=(t == 0))
                        if t:
                            i = pe.matmul(ot, state[:, t - 1, :], qe[:, t * P:(t + 1) * P], start=False, stop=True)
                    i.then_inc(s_om, 1)
                    pe.wait_ge(s_osq, n + 1)
                    pe.matmul(u[:, :], mats[:, C_M128, :], osq[:, :], start=True, stop=True).then_inc(s_oss, 1)
                elif kind == "spatial":
                    pe.wait_ge(s_gv, 2 * n + 1)
                    if n >= 2:
                        pe.wait_ge(s_vn, n - 1)
                    four(bank[4 + n % 2], mv[:, n, :], s_gvT)
                    pe.wait_ge(s_vn, n + 1)
                    pe.wait_ge(s_wTr, 1)
                    if n == 0:
                        pe.wait_ge(s_on, HG)
                    else:
                        pe.wait_ge(s_so, 2 * n)
                    for t in range(TT):
                        i = pe.matmul(bank[6 + n % 2][:, t * P:(t + 1) * P], vn[:, n, t * P:(t + 1) * P], wT[:, n, :],
                                      start=True, stop=True)
                    i.then_inc(s_sm, 1)
            linear("out", None, ready=acts(ACT0["out"]))
            stats("ln2")
            pe.wait_ge(s_mn, MT)
            for k in range(KD):
                if k >= 2:
                    pe.wait_ge(s_ma, k - 1)
                for t in range(MT):
                    i = pe.transpose(bank[6 + k % 2][:, t * P:(t + 1) * P], memin[:, t, k * P:(k + 1) * P], ident)
                i.then_inc(s_mT, 1)
            linear("mk", None, mhi, mlo, MEM, ready=lambda k: (s_ml, k + 1))

            def turn_values(j):
                if j < 1:
                    return
                if j == 1:
                    pe.wait_ge(var_ready, 2)
                pe.wait_ge(bank_free, RAW + phases["mv"].base + j)
                if j >= 3:
                    pe.wait_ge(s_kv, j - 2)
                for t in range(MT):
                    i = pe.transpose(bank[4 + (j - 1) % 2][:, t * P:(t + 1) * P], vxt[:, (j - 1) % 2, t * P:(t + 1) * P], ident)
                i.then_inc(s_vxT, 1)
            linear("mv", None, mhi, mlo, MEM, after=turn_values)
            turn_values(KD)
            linear("xq", None, ready=acts(ACT0["xq"]))
            def cross_scores(h):
                pe.wait_ge(bank_free, RAW + phases["xq"].base + KD)
                if h >= 2:
                    pe.wait_ge(s_pe, TT * (h - 1))
                for t in range(TT):
                    for k in range(2):
                        i = pe.matmul(bank[2 * (h % 2) + t // 2][:, (t % 2) * MEM:(t % 2 + 1) * MEM],
                                      qx[:, 2 * h + k, t * P:(t + 1) * P], kx[:, 2 * h + k, :], start=(k == 0), stop=(k == 1))
                i.then_inc(s_sc, 1)

            cross_scores(0)
            for h in range(XH):
                if h + 1 < XH:
                    cross_scores(h + 1)
                pe.wait_ge(s_pn, TT * (h + 1))
                if h:
                    pe.wait_ge(s_pcd, h)
                    pe.wait_ge(s_pca, h)
                else:
                    pe.wait_ge(s_kv, KD)
                for m in range(MT):
                    for t in range(TT):
                        i = pe.transpose(bank[4 + m][:, t * P:(t + 1) * P], px[:, h % 2, t, m * P:(m + 1) * P], ident)
                    i.then_inc(s_pT, 1)
                pe.wait_ge(s_pcd, h + 1)
                pe.wait_ge(s_pca, h + 1)
                if h:
                    pe.wait_ge(act_ready, ACT0["xo"] + 2 * h)
                for d in range(2):
                    for m in range(MT):
                        i = pe.matmul(bank[6 + d][:, :], vx[:, m, (2 * h + d) * P:(2 * h + d + 1) * P], pxT[:, h % 2, m, :],
                                      start=(m == 0), stop=(m == MT - 1))
                    i.then_inc(s_pv, 1)
            linear("xo", None, ready=acts(ACT0["xo"]))
            stats("ln3")
            ffn("f2", "ln4")
            stats("rms1")
            linear("in2", None, ready=acts(ACT0["in2"]))
            for j in range(5):
                x = sq[:, j, :] if j < 4 else skv[:, 0, :]
                pe.wait_ge(s_hsq, j + 1)
                pe.matmul(bank[4][:, :], mats[:, C_HEAD, :], r1[:, :], start=True, stop=True).then_inc(s_hss, 1)
                pe.wait_ge(s_hn, j + 1)
                pe.matmul(bank[5][:, :], mats[:, C_ROT, :], x, start=True, stop=True).then_inc(s_hrot, 1)
            pe.wait_ge(s_hr, 5)
            for g in range(2):
                pe.matmul(bank[6 + g][:, :], mats[:, C_DUP0 + g, :], skv[:, 0, :], start=True, stop=True).then_inc(s_dup, 1)
            four(bank[4], skv[:, 1, :], s_svT)
            pe.wait_ge(s_dupc, 3)
            for g in range(4):
                pe.wait_ge(s_pool, g + 1)
                if g >= 2:
                    pe.wait_ge(s_py, g - 1)
                pe.matmul(bank[4 + g % 2][:, :], poolw[:, g, :], su[:, g, 8:8 + T], start=True, stop=True).then_inc(s_pmm, 1)

            def self_scores(h):
                p0 = HD * (h % 2)
                for t in range(TT):
                    n = TT * h + t
                    if n >= 3:
                        pe.wait_ge(s_pe, TT * XH + n - 2)
                    pe.matmul(bank[n % 3][:, :], sq[p0:p0 + HD, h // 2, t * P:(t + 1) * P], kk[p0:p0 + HD, h // 4, :],
                              start=True, stop=True).then_inc(s_sc, 1)

            pe.wait_ge(s_py, 4)
            self_scores(0)
            for h in range(QH):
                if h + 1 < QH:
                    self_scores(h + 1)
                p0 = HD * (h % 2)
                pe.wait_ge(s_pn, TT * XH + TT * (h + 1))
                for st in range(TT):
                    n = TT * h + st
                    if n >= 3:
                        m = n - 3
                        if m % 2:
                            pe.wait_ge(s_pca, XH + m // 2 + 1)
                        else:
                            pe.wait_ge(s_pcd, XH + m // 2 + 1)
                    for t in range(TT):
                        i = pe.transpose(bank[3 + n % 3][:, t * P:(t + 1) * P], ps[:, h % 2, t, st * P:(st + 1) * P], ident)
                    i.then_inc(s_pT, 1)
                pe.wait_ge(s_pcd, XH + 2 * (h + 1))
                pe.wait_ge(s_pca, XH + 2 * (h + 1))
                if h >= 4 and h % 2 == 0:
                    pe.wait_ge(act_ready, ACT0["out2"] + 4 + h // 2 - 1)
                for st in range(TT):
                    i = pe.matmul(bank[6 + (h // 2) % 2][p0:p0 + HD, :], sv[:, st, HD * (h // 4):HD * (h // 4) + HD],
                                  psT[:, h % 2, st, :], start=(st == 0), stop=(st == TT - 1))
                i.then_inc(s_pv, 1)
            linear("out2", None, ready=lambda k: (act_ready, ACT0["out2"] + 8))
            stats("rms2")
            ffn("f3", None)


def kernel(**inputs):
    import concourse.bacc as bacc
    from concourse.bass_utils import run_bass_kernel_spmd as run

    nc = bacc.Bacc("TRN2", target_bir_lowering=False, num_devices=1)
    arrays = {name: np.ascontiguousarray(a) for name, a in inputs.items()}
    arrays.update(shape_constants())
    aps = {}
    arrays = {f"in_{name}": a for name, a in arrays.items()}
    for name, a in arrays.items():
        aps[name[3:]] = nc.dram_tensor(name, a.shape, mybir.dt.from_np(a.dtype), kind="ExternalInput").ap()
    out = nc.dram_tensor("out_dram", (1, T, D), F32, kind="ExternalOutput").ap()
    build(nc, aps, out)
    return run(nc, [arrays], core_ids=[0]).results[0]["out_dram"]
```

```python
from contextlib import ExitStack

import numpy as np

import concourse.bass as bass
from concourse import mybir

F32 = mybir.dt.float32
F32R = mybir.dt.float32r
I32 = mybir.dt.int32
ACT = mybir.ActivationFunctionType
ALU = mybir.AluOpType
AX = mybir.AxisListType

P = 128
T = 512
D = 1024
KD = D // P
TT = T // P
F = 2816
MEM = 256
MT = MEM // P
HG = 4
SG = 4
XH = 4
QH = 8
HD = 64
GRID_W = 64
ALPHA = 2.0 ** 0.25
LN_EPS = 1e-5
RMS_EPS = 1e-6
PARTS = (8, 8, 6)
assert sum(PARTS) * P == F
RAW = 4
SPLIT = 2
MVAL = 4
MEM_AT = 5
LEVELS = (6, 5, 4, 3, 2, 1, 0)

V_LN1G, V_LN1B, V_LN2G, V_LN2B, V_MEMG, V_MEMB, V_LN3G, V_LN3B, V_LN4G, V_LN4B, V_N1, V_N2 = range(0, 96, 8)
V_POOLB, V_POOLS, V_HGN, V_LB, V_QN, V_KN, V_ROWS = 96, 100, 104, 105, 113, 114, 115

C_ID, C_MEAN, C_M128, C_HEAD, C_ROT, C_DUP0, C_DUP1, C_N = range(8)


def shape_constants():
    i = np.arange(P)
    mats = np.zeros((C_N, P, P), np.float32)
    mats[C_ID] = np.eye(P)
    mats[C_MEAN] = 1.0 / D
    mats[C_M128] = 1.0 / P
    mats[C_HEAD] = (i[:, None] // HD == i[None, :] // HD) / HD
    q = HD // 4
    for d in range(P):
        if (d // q) % 2 == 0:
            mats[C_ROT, d + q, d] = -1.0
        else:
            mats[C_ROT, d - q, d] = 1.0
    for g in range(2):
        for d in range(P):
            mats[C_DUP0 + g, g * HD + d % HD, d] = 1.0
    masks = np.zeros((len(LEVELS) + 2, P, P), np.int32)
    s, t = i[:, None], i[None, :]
    for n, lv in enumerate(LEVELS):
        masks[n] = (s >> (lv + 1) == t >> (lv + 1)) & (s >> lv & 1 == 0) & (t >> lv & 1 == 1)
    masks[len(LEVELS)] = s == t
    masks[len(LEVELS) + 1] = s <= t
    freq = (np.float32(10000.0) ** (-np.arange(q, dtype=np.float32) / np.float32(q))).astype(np.float32)
    tok = np.arange(T)
    row, col = (tok // GRID_W).astype(np.float32), (tok % GRID_W).astype(np.float32)
    ang = np.zeros((P, T), np.float32)
    for d in range(P):
        ang[d] = (row if (d % HD) < HD // 2 else col) * freq[d % q]
    rope = np.stack([np.cos(ang), np.sin(ang)]).astype(np.float32)
    restart = np.ones((1, T), np.float32)
    restart[0, ::P] = 0.0
    rcnt = np.zeros((4, T), np.float32)
    for g in range(4):
        w = 2 << g
        rcnt[g] = 1.0 / (np.clip(tok - w // 2 + w, 0, T) - np.clip(tok - w // 2, 0, T))
    return {"c_mats": mats, "c_masks": masks, "c_rope": rope, "c_restart": restart, "c_rcnt": rcnt}


def build(nc, A, out):
    ctx = ExitStack()
    with ctx:
        def sem(name):
            return ctx.enter_context(nc.semaphore(name))

        top = [-(-nc.sbuf_base // 32) * 32]

        def sb(name, shape, dt=F32, at=None):
            size = int(np.prod(shape[1:])) * 4
            off = top[0] if at is None else at
            assert off + size <= nc.sbuf_usable_end, (name, off + size - nc.sbuf_usable_end)
            if at is None:
                top[0] += -(-size // 32) * 32
            return nc.alloc_sbuf_tensor_at(name, list(shape), dt, offset=off)

        bank = [ctx.enter_context(nc.psum_tensor(f"bank{i}", [P, T], F32)) for i in range(8)]

        res = sb("res", [P, KD, T])
        ahi = sb("ahi", [P, KD, T], F32R)
        alo = sb("alo", [P, KD, T], F32R)
        wraw = sb("wraw", [P, RAW, KD * P])
        whi = sb("whi", [P, SPLIT, KD * P], F32R)
        wlo = sb("wlo", [P, SPLIT, KD * P], F32R)
        mats = sb("mats", [P, C_N, P])
        masks = sb("masks", [P, len(LEVELS) + 2, P], I32)
        restart = sb("restart", [P, T])
        vecs = sb("vecs", [P, P])
        wT = sb("wT", [P, SG, P])
        small = sb("small", [P, 64])
        sgst = sb("sgst", [P, 4, 6])
        sgmv = sb("sgmv", [P, 4, 2])
        sgr = sb("sgr", [P, 4])
        mst = sb("mst", [P, 4, 6])
        mmv = sb("mmv", [P, 2, 2])
        mrs = sb("mrs", [P, 2])
        arena = top[0]
        ARENA = nc.sbuf_usable_end - arena

        def region(start):
            at = [arena + start]

            def take(name, shape, dt=F32):
                t = sb(name, shape, dt, at=at[0])
                at[0] += int(np.prod(shape[1:])) * 4
                return t
            return take

        KB = 1024
        take = region(0)
        gate = take("gate", [P, 2, T])
        hval = take("hval", [P, 2, T])
        rstd = take("rstd", [P, T])
        mean = take("mean", [P, T])
        sum1 = take("sum1", [P, T])
        sum2 = take("sum2", [P, T])
        square = gate
        var = hval
        WORK = 16 * KB
        take = region(WORK)
        hhi = take("hhi", [P, max(PARTS), T], F32R)
        hlo = take("hlo", [P, max(PARTS), T], F32R)
        take = region(WORK)
        xin = take("xin", [P, TT, D])
        take = region(WORK + 32 * KB)
        vrow = take("vrow", [P, P])
        wsin = take("wsin", [P, SG, P])
        take = region(WORK)
        mk = take("mk", [P, HG, T])
        mq = take("mq", [P, HG, T])
        mg = take("mg", [P, HG, T])
        mu = take("mu", [P, SG, T])
        mv = take("mv", [P, SG, T])
        cum = take("cum", [P, HG, T])
        vT = take("vT", [P, HG, TT, P])
        ivt = take("ivt", [P, 2, T])
        acc = take("acc", [P, 2, T])
        DEC = 4
        dec = take("dec", [P, DEC, T])
        qt = take("qt", [P, 2, T])
        kt = take("kt", [P, 2, T])
        sgb = take("sgb", [P, 3, T])
        vn = cum
        take = region(0)
        eb = take("eb", [P, T])
        qe = take("qe", [P, T])
        kend = take("kend", [P, 3 * P])
        kendT = take("kendT", [P, 3 * P])
        state = take("state", [P, 3, P])
        osq = take("osq", [P, T])
        ors = take("ors", [P, T])
        take = region(WORK)
        memin = take("memin", [P, MT, D])
        mhi = take("mhi", [P, KD, MEM], F32R)
        mlo = take("mlo", [P, KD, MEM], F32R)
        mval = take("mval", [P, MVAL, MEM])
        kx = take("kx", [P, KD, MEM])
        vx = take("vx", [P, MT, D])
        vxt = take("vxt", [P, 2, MEM])
        take = region(WORK + 48 * KB)
        qx = take("qx", [P, KD, T])
        take = region(WORK)
        px = take("px", [P, 2, TT, MEM])
        pxT = take("pxT", [P, 2, MT, T])
        take = region(WORK)
        sq = take("sq", [P, 4, T])
        skv = take("skv", [P, 2, T])
        su = take("su", [P, 4, T + 16])
        kk = take("kk", [P, 2, T])
        sv = take("sv", [P, TT, P])
        ps = take("ps", [P, 2, TT, T])
        psT = take("psT", [P, 2, TT, T])
        rope = take("rope", [P, 2, T])
        poolw = take("poolw", [P, 4, P])
        rcnt = take("rcnt", [P, 2, T])
        po = take("po", [P, 2, T])
        take = region(0)
        r1 = take("r1", [P, 2, T])
        r2 = take("r2", [P, 2, T])
        r3 = take("r3", [P, T])
        pa = take("pa", [P, T + 16])
        pb = take("pb", [P, T + 16])
        take = region(WORK + 32 * KB)
        ob = take("ob", [P, 2, TT, P])
        assert ARENA >= WORK + 86 * KB, ARENA

        ident = mats[:, C_ID, :]

        def vcol(row):
            return vecs[:, row:row + 1]

        S_LB, S_OML, S_E0, S_E1, S_EPS5, S_EPS6, S_MX, S_NM, S_SM, S_RI = 0, 4, 8, 12, 16, 17, 20, 28, 36, 44

        class Phase:
            def __init__(self, name, kind, base, K, n, src):
                self.name, self.kind, self.base, self.K, self.n, self.src = name, kind, base, K, n, src

        phases, blocks = {}, []

        def add(name, kind, K, n, src):
            ph = Phase(name, kind, len(blocks), K, n, src)
            phases[name] = ph
            blocks.extend((ph, j) for j in range(n))

        def cols(w, k0, K, col):
            return w.rearrange("(k p) f -> p k f", p=P)[:, k0:k0 + K, bass.ds(col * P, P)]

        def add_ffn(name, wg, wu, wd):
            t0 = 0
            for part, n in enumerate(PARTS):
                def up(tile, odd, t0=t0):
                    return cols(wu if odd else wg, 0, KD, tile + t0)
                add(f"{name}_up{part}", "up", KD, 2 * n, up)
                add(f"{name}_down{part}", "down", n, KD, lambda j, t0=t0, n=n: cols(wd, t0, n, j))
                t0 += n

        POOL_ORDER = (3, 2, 1, 0)
        IN2_ORDER = [4, 0, 1, 2, 3] + [6 + g for g in POOL_ORDER] + [5]
        add_ffn("f1", A["ffn1_w_gate"][0], A["ffn1_w_up"][0], A["ffn1_w_down"][0])
        add("in", "lin", KD, 24, lambda j: cols(A["w_in"][0], 0, KD, IN_ORDER[j]))
        add("out", "lin", KD, KD, lambda j: cols(A["w_out"][0], 0, KD, j))
        add("mk", "lin", KD, KD, lambda j: cols(A["xa_w_k"][0], 0, KD, j))
        add("mv", "lin", KD, KD, lambda j: cols(A["xa_w_v"][0], 0, KD, j))
        add("xq", "lin", KD, KD, lambda j: cols(A["xa_w_q"][0], 0, KD, j))
        add("xo", "lin", KD, KD, lambda j: cols(A["xa_w_o"][0], 0, KD, j))
        add_ffn("f2", A["ffn2_w_gate"][0], A["ffn2_w_up"][0], A["ffn2_w_down"][0])
        add("in2", "lin", KD, 10, lambda j: cols(A["w_in_2"][0], 0, KD, IN2_ORDER[j]))
        add("out2", "lin", KD, KD, lambda j: cols(A["w_out_2"][0], 0, KD, j))
        add_ffn("f3", A["w_gate_2"][0], A["w_up_2"][0], A["w_down_2"][0])
        TILE0 = {"f1": 0, "f2": F // P, "f3": 2 * (F // P)}

        def part_tile0(name):
            return TILE0[name[:2]] + sum(PARTS[:int(name[-1])])

        raw_ready = [sem(f"raw_ready{i}") for i in range(RAW)]
        hi_ready = sem("hi_ready")
        lo_ready = sem("lo_ready")
        block_done = sem("block_done")
        bank_free = sem("bank_free")
        gate_done = sem("gate_done")
        value_done = sem("value_done")
        hidden_ready = sem("hidden_ready")
        act_dve = sem("operand_tile_by_dve")
        act_pool = sem("operand_tile_by_pool")
        square_done = sem("square_done")
        sums_done = sem("sums_done")
        stat_mean = sem("stat_mean")
        stat_sq = sem("stat_sq")
        mean_sq = sem("mean_squared")
        var_ready = sem("var_ready")
        rstd_ready = sem("rstd_ready")
        scaled = sem("scaled")
        normed = sem("normed")
        hi_act = sem("hi_act")
        lo_act = sem("lo_act")
        dve_chain = sem("dve_chain")
        act_chain = sem("act_chain")
        pool_chain = sem("pool_chain")

        def linker(eng, s):
            n = [0]

            def link(ins):
                n[0] += 1
                ins.then_inc(s, 1)
                eng.wait_ge(s, n[0])
            return link

        def slot_of(ph, jj, n):
            return (ph.base + jj) % n

        def each_block(eng, ph, step):
            loops = (ph.n - 4) // 4
            done = 0
            if loops >= 2:
                with eng.Fori(0, loops) as i:
                    for jj in range(4):
                        step(i, jj)
                done = 4 * loops
            for j in range(done, ph.n):
                step(0, j)

        def load_block(eng, ph, i, jj):
            b = ph.base + jj + 4 * i
            eng.wait_ge(lo_ready, b + 1)
            src = ph.src(2 * i + jj // 2, jj % 2) if ph.kind == "up" else ph.src(jj)
            slot = slot_of(ph, jj, RAW)
            dst = wraw[:, slot, 0:ph.K * P].rearrange("p (k f) -> p k f", f=P)
            eng.dma_start(dst, src).then_inc(raw_ready[slot], 16)

        def split_hi(eng, ph, i, jj):
            b = ph.base + jj + 4 * i
            n = ph.K * P
            slot, raw = slot_of(ph, jj, SPLIT), slot_of(ph, jj, RAW)
            eng.wait_ge(raw_ready[raw], 16 * ((ph.base + jj) // RAW + 1) + 16 * i)
            eng.wait_ge(block_done, b + 1)
            eng.copy(whi[:, slot, 0:n], wraw[:, raw, 0:n]).then_inc(hi_ready, 1)

        def split_lo(eng, ph, i, jj):
            b = ph.base + jj + 4 * i
            n = ph.K * P
            slot, raw = slot_of(ph, jj, SPLIT), slot_of(ph, jj, RAW)
            eng.wait_ge(hi_ready, b + 1)
            eng.tensor_tensor(wlo[:, slot, 0:n], wraw[:, raw, 0:n], whi[:, slot, 0:n],
                              ALU.subtract).then_inc(lo_ready, 1)

        def ahead(split, eng, ph, i, jj):
            if isinstance(i, int):
                b = ph.base + jj + 2
                if b < len(blocks):
                    split(eng, blocks[b][0], 0, blocks[b][1])
            else:
                split(eng, ph, i, jj + 2)

        def multiply(eng, ph, i, jj, xhi, xlo, width=T, ready=None):
            b = ph.base + jj + 4 * i
            slot = slot_of(ph, jj, SPLIT)
            o = bank[slot_of(ph, jj, RAW)][:, 0:width]
            eng.wait_ge(hi_ready, b + 1)
            eng.wait_ge(bank_free, b + 1)
            for k in range(ph.K):
                if ready is not None:
                    eng.wait_ge(*ready(k))
                w = whi[:, slot, k * P:(k + 1) * P]
                eng.matmul(o, w, xhi[:, k, :], start=(k == 0), stop=False)
                eng.matmul(o, w, xlo[:, k, :], start=False, stop=False)
            eng.wait_ge(lo_ready, RAW + b + 1)
            for k in range(ph.K):
                mm = eng.matmul(o, wlo[:, slot, k * P:(k + 1) * P], xhi[:, k, :],
                                start=False, stop=(k == ph.K - 1))
            mm.then_inc(block_done, 1)

        def multiply_two(eng, ph, xhi, xlo, width, ready, before=None, order=None):
            eng.wait_ge(hi_ready, ph.base + 2)
            eng.wait_ge(bank_free, ph.base + 2)
            eng.wait_ge(lo_ready, RAW + ph.base + 2)
            for n, k in enumerate(order or range(ph.K)):
                if before:
                    before(n)
                eng.wait_ge(*ready(n))
                for j in range(2):
                    slot = slot_of(ph, j, SPLIT)
                    o = bank[slot_of(ph, j, RAW)][:, 0:width]
                    w, wl = whi[:, slot, k * P:(k + 1) * P], wlo[:, slot, k * P:(k + 1) * P]
                    eng.matmul(o, w, xhi[:, k, :], start=(n == 0), stop=False)
                    eng.matmul(o, w, xlo[:, k, :], start=False, stop=False)
                    mm = eng.matmul(o, wl, xhi[:, k, :], start=False, stop=(n == ph.K - 1))
                    if n == ph.K - 1:
                        mm.then_inc(block_done, 1)

        def bank_of(ph, jj):
            return bank[slot_of(ph, jj, RAW)]

        def wait_block(eng, ph, i, jj):
            eng.wait_ge(block_done, SPLIT + ph.base + jj + 4 * i + 1)

        NORMS = {"ln1": (0, True, V_LN1G, V_LN1B), "ln2": (1, True, V_LN2G, V_LN2B),
                 "ln3": (2, True, V_LN3G, V_LN3B), "ln4": (3, True, V_LN4G, V_LN4B),
                 "rms1": (4, False, V_N1, None), "rms2": (5, False, V_N2, None)}
        POOL, DVE = 0, 1
        MAKERS = {"f1": [DVE] * KD, "in": [POOL] * KD, "out": [POOL, DVE] * (KD // 2), "xq": [DVE] * KD, "xo": [DVE] * KD,
                  "f2": [POOL] * KD, "in2": [POOL, DVE] * (KD // 2), "out2": [DVE] * KD, "f3": [POOL, DVE] * (KD // 2)}
        OPERAND = {"ln1": "in", "ln2": "xq", "ln3": "f2", "rms1": "in2", "rms2": "f3"}

        def operand(layer, k):
            n = [0, 0]
            for name, makers in MAKERS.items():
                for i, m in enumerate(makers):
                    n[m] += 1
                    if name == layer and i == k:
                        return (act_pool, act_dve)[m], n[m]

        def by(layer, k):
            return MAKERS[layer][k]

        HI0 = {"ln1": 0, "ln2": 16, "ln3": 24, "rms1": 32, "rms2": 40}
        SUM_STEPS = KD - 2

        s_ident = sem("identity_loaded")
        s_x = [sem(f"x_loaded{i}") for i in range(2)]
        s_mem, s_const, s_vec, s_ws, s_rows = (sem(n) for n in
                                                    ("mem_loaded", "consts_loaded", "vectors_loaded",
                                                     "spatial_loaded", "rows_loaded"))
        s_xT = sem("x_transposed")
        s_xhi = sem("x_hi")
        s_vT0 = sem("vectors_transposed")
        s_vecs = sem("vectors_ready")
        s_lbe = sem("bound_exps")
        s_wsT = sem("spatial_transposed")
        s_wTz = sem("spatial_zeroed")
        s_wTr = sem("spatial_ready")
        s_out = sem("out_stored")
        s_oT = sem("out_transposed")
        s_ob = sem("out_copied")

        s_sig = sem("gates_sigmoid")
        s_fg = sem("forget_ready")
        s_lf = sem("log_forget")
        s_cum = sem("cum_ready")
        s_ivT = sem("values_transposed")
        s_ivc = sem("values_copied")
        s_arg = sem("decay_args")
        s_dexp = sem("decays")
        s_qk = sem("scaled_qk")
        s_smm = sem("score_products")
        s_put = sem("scores_put")
        s_az = sem("scores_zeroed")
        s_ebd = sem("exp_cum")
        s_kd = sem("key_decay_args")
        s_kde = sem("key_decays")
        s_ke = sem("end_keys")
        s_keT = sem("end_keys_transposed")
        s_kec = sem("end_keys_copied")
        s_um = sem("state_products")
        s_st = sem("states_ready")
        s_om = sem("outputs_product")
        s_osq = sem("outputs_squared")
        s_oss = sem("outputs_square_sum")
        s_ors = sem("outputs_rstd")
        s_on = sem("outputs_normed")
        s_act2 = sem("gates_activated")
        s_prod = sem("gated")
        s_gv = sem("gelu_done")
        s_gvT = sem("gelu_transposed")
        s_sgv = sem("spatial_var")
        s_sgr = sem("spatial_rstd")
        s_vn = sem("spatial_normed")
        s_sm = sem("spatial_products")
        s_so = sem("spatial_biased")
        s_mul = sem("spatial_gated")
        s_mv = sem("mem_var")
        s_mr = sem("mem_rstd")
        s_mn = sem("mem_normed")
        s_mT = sem("mem_transposed")
        s_ma = sem("mem_affine")
        s_mh = sem("mem_hi")
        s_ml = sem("mem_lo")
        s_vxT = sem("mem_values_transposed")
        s_kv = sem("mem_kv_copied")
        s_sc = sem("scores")
        s_nm = sem("score_maxima")
        s_pe = sem("probabilities")
        s_pn = sem("probabilities_normed")
        s_pT = sem("probabilities_transposed")
        s_pcd = sem("probabilities_copied_dve")
        s_pca = sem("probabilities_copied_act")
        s_pv = sem("attended")
        s_ah = sem("attended_hi")
        s_rope = sem("rope_loaded")
        s_hsq = sem("head_squares")
        s_hss = sem("head_square_sums")
        s_hrs = sem("head_rstd")
        s_hn = sem("head_normed")
        s_hrot = sem("head_rotated")
        s_hr = sem("head_roped")
        s_dup = sem("keys_doubled")
        s_dupc = sem("keys_copied")
        s_svT = sem("self_values_transposed")
        s_pad = sem("pool_pads")
        s_pool = sem("pooled")
        s_rcn = [sem(f"counts_loaded{i}") for i in range(2)]
        s_pmm = sem("pool_products")
        s_py = sem("pool_out")
        s_pyh = sem("pool_out_hi")

        STEPS = [(h, n) for h in range(HG) for n in range(len(LEVELS) + 1)]
        SCALED = [s for s, (h, n) in enumerate(STEPS) if n < len(LEVELS)]
        NTH = {s: e for e, s in enumerate(SCALED)}
        Q0, FZ0, IV0, G0, U0, V0 = range(0, 24, 4)
        IN_ORDER = ([FZ0 + h for h in range(HG)] + [Q0, IV0, Q0 + 1, IV0 + 1, V0, V0 + 1, V0 + 2, Q0 + 2, IV0 + 2,
                                                    Q0 + 3, IV0 + 3, V0 + 3]
                    + [U0 + g for g in range(SG)] + [G0 + h for h in range(HG)])
        at_block = {c: n for n, c in enumerate(IN_ORDER)}
        plan = [[] for _ in range(24)]
        for h in range(HG):
            plan[1 + h] += [("forget", h)]
        plan[4] += [("logs", 0)]
        for h in range(HG):
            g0 = 5 + 4 * h
            if h >= 1:
                plan[g0 + 1] += [("take_values", h)]
        for h in range(HG):
            g0 = 5 + 4 * h
            for n in range(len(LEVELS) + 1):
                s = (len(LEVELS) + 1) * h + n
                plan[g0 + n // 2 + 1] += [("put", s)]
            plan[g0 + 4] += [("outputs", h)]
            plan[g0 + 5] += [("power", h)]
            plan[g0 + 6] += [("normed", h)]
            for n in range(len(LEVELS) + 1):
                plan[g0 + n // 2] += [("level", (len(LEVELS) + 1) * h + n)]
            plan[g0 + 2] += [("ends", h)]
            plan[g0 + 3] += [("update", h)]
            plan[g0 if h else g0 + 1] += [("values", h)]
            if h == 0:
                plan[g0 + 2] += [("take_values", h)]
        plan[11] += [("gelu", 0), ("gelu", 1), ("gelu", 2)]
        for g, (at, b) in enumerate(((11, 6), (15, 6), (19, 6), (21, 4))):
            if g == SG - 1:
                plan[at] += [("gelu", n) for n in range(3, 8)]
            plan[at] += [("turn", g)]
            plan[at + 1] += [("centre", g)]
            plan[at + 2].insert(0, ("bias", g))
        plan[22] += [("spatial", g) for g in range(3)]
        plan[23] += [("spatial", 3)] + [("silu", h) for h in range(3)] + [("gate", h) for h in range(3)]
        SPATIAL_BANK = (6, 6, 6, 4)
        DST = {Q0: mq, FZ0: mk, G0: mg, U0: mu, V0: mv}
        IN_DST = [ivt[:, c % 2, :] if c // 4 * 4 == IV0 else DST[c // 4 * 4][:, c % 4, :] for c in IN_ORDER]
        OUT_TILES = [4, 5, 6, 7, 0, 1, 2, 3]

        def wait_in(eng, j):
            eng.wait_ge(bank_free, RAW + phases["in"].base + at_block[j] + 1)

        def mixed(k):
            return mq[:, k, :] if k < HG else mu[:, k - HG, :]

        def wait_mixed(eng, k):
            if k < HG:
                eng.wait_ge(s_prod, k + 1)
            else:
                eng.wait_ge(s_mul, k - HG + 1)

        def halves(t, lv):
            return t.rearrange("p (n two c) -> p n two c", two=2, c=1 << lv)

        def in2_dst(j):
            return skv[:, 0, :] if j == 0 else sq[:, j - 1, :] if j < 5 else su[:, j - 5, 8:8 + T] if j < 9 else skv[:, 1, :]

        block = ctx.enter_context(nc.Block())

        @block.sync
        def _(sp):
            def vec_rows(row, ap, n):
                sp.dma_start(vrow[row:row + n, :], ap).then_inc(s_vec, 16)

            sp.dma_start(mats[:, C_ID, :], A["c_mats"][C_ID]).then_inc(s_ident, 16)
            xv = A["x"][0].rearrange("(n p) d -> p n d", p=P)
            for half in range(2):
                sp.dma_start(xin[:, :, half * T:(half + 1) * T], xv[:, :, half * T:(half + 1) * T]).then_inc(s_x[half], 16)
                for j in range(2):
                    load_block(sp, phases["f1_up0"], 0, 2 * half + j)
            sp.dma_start(mats[:, 1:C_N, :], A["c_mats"][1:C_N].rearrange("n p f -> p n f")).then_inc(s_const, 16)
            for row, name in ((V_LN1G, "ln1_g"), (V_LN1B, "ln1_b"), (V_LN2G, "ln2_g"), (V_LN2B, "ln2_b"),
                              (V_MEMG, "mem_ln_g"), (V_MEMB, "mem_ln_b"), (V_LN3G, "ln3_g"), (V_LN3B, "ln3_b"),
                              (V_LN4G, "ln4_g"), (V_LN4B, "ln4_b"), (V_N1, "norm1_g_2"), (V_N2, "norm2_g_2")):
                vec_rows(row, A[name].rearrange("o (k p) -> (o k) p", p=P), KD)
            vec_rows(V_POOLB, A["pool_b_2"][0], 4)
            vec_rows(V_POOLS, A["pool_scale_2"].rearrange("o (k p) -> (o k) p", p=P), 4)
            vec_rows(V_HGN, A["hg_norm_g"], 1)
            vec_rows(V_LB, A["hg_lb_logits"].rearrange("l h d -> (l h) d"), 8)
            for row, name in ((V_QN, "q_norm_g_2"), (V_KN, "k_norm_g_2")):
                for half in range(2):
                    sp.dma_start(vrow[row:row + 1, half * HD:(half + 1) * HD], A[name]).then_inc(s_vec, 16)
            sp.dma_start(masks[:, :, :], A["c_masks"].rearrange("n p f -> p n f")).then_inc(s_const, 16)
            sp.dma_start(restart[:, :], A["c_restart"].broadcast_to([P, T])).then_inc(s_const, 16)
            sp.dma_start(wsin[:, :, :], A["sg_w_s"][0].rearrange("g t s -> t g s")).then_inc(s_ws, 16)

            def stream(name):
                ph = phases[name]
                if ph.kind == "up":
                    with sp.Fori(1 if ph.base == 0 else 0, ph.n // 4) as i:
                        for jj in range(4):
                            load_block(sp, ph, i, jj)
                    return
                for j in range(ph.n):
                    load_block(sp, ph, 0, j)

            def ffn(name):
                for part in range(len(PARTS)):
                    stream(f"{name}_up{part}")
                    stream(f"{name}_down{part}")

            ffn("f1")
            for j in range(4):
                load_block(sp, phases["in"], 0, j)
            wait_block(sp, phases["in"], 0, 0)
            for n, ap in enumerate((A["sg_ln_g"].rearrange("o g c -> o (g c)"), A["sg_ln_b"].rearrange("o g c -> o (g c)"),
                                    A["sg_b_s"].rearrange("o g c -> o (g c)"))):
                sp.dma_start(sgb[:, n, :], ap.broadcast_to([P, T])).then_inc(s_rows, 16)
            for j in range(4, 24):
                load_block(sp, phases["in"], 0, j)
            for j in range(4):
                load_block(sp, phases["out"], 0, j)
            sp.wait_ge(*operand("out", KD - 1))
            sp.dma_start(memin[:, :, :], A["mem"][0].rearrange("(n p) d -> p n d", p=P)).then_inc(s_mem, 16)
            for j in range(4, KD):
                load_block(sp, phases["out"], 0, j)
            for name in ("mk", "mv", "xq", "xo"):
                stream(name)
            ffn("f2")
            stream("in2")
            wait_block(sp, phases["in2"], 0, 0)
            sp.dma_start(rope[:, :, :], A["c_rope"].rearrange("n p t -> p n t")).then_inc(s_rope, 16)
            sp.dma_start(poolw[:, :, :], A["pool_w_2"][0].rearrange("g c d -> c g d")).then_inc(s_rope, 16)
            for j in range(4):
                load_block(sp, phases["out2"], 0, j)
            for n, g in enumerate(POOL_ORDER):
                if n >= 2:
                    sp.wait_ge(s_pool, n - 1)
                sp.dma_start(rcnt[:, n % 2, :], A["c_rcnt"][g:g + 1, :].broadcast_to([P, T])).then_inc(s_rcn[n % 2], 16)
            for j in range(4, KD):
                load_block(sp, phases["out2"], 0, j)
            ffn("f3")
            for j in range(KD):
                sp.wait_ge(s_ob, j + 1)
                sp.dma_start(out[0].rearrange("(n p) d -> p n d", p=P)[:, :, j * P:(j + 1) * P],
                             ob[:, j % 2, :, :]).then_inc(s_out, 16)
                sp.wait_ge(s_out, 16 * (j + 1))

        @block.scalar
        def _(act):
            link = linker(act, act_chain)

            def hi_stream(ph, i, jj):
                ahead(split_hi, act, ph, i, jj)

            def silu_gate(ph, i, jj, t0):
                tile = t0 + 2 * i + jj // 2
                wait_block(act, ph, i, jj)
                act.wait_ge(value_done, tile + 1)
                act.activation(gate[:, (t0 + jj // 2) % 2, :], bank_of(ph, jj)[:, :], ACT.Silu).then_inc(gate_done, 1)

            def square_res(norm, j, ph=None):
                n = 8 * NORMS[norm][0] + j
                if ph:
                    act.wait_ge(bank_free, RAW + ph.base + j + 1)
                else:
                    act.wait_ge(normed, n - 8 + 1)
                if j >= 2:
                    act.wait_ge(sums_done, SUM_STEPS * NORMS[norm][0] + max(1, j - 2))
                act.activation(square[:, j % 2, :], res[:, j, :], ACT.Square).then_inc(square_done, 1)

            def use_logs():
                act.preload_act_table_set("natural_log_exp_and_others")

            def norm_tail(norm, between=None):
                idx, centred, grow, brow = NORMS[norm]
                if centred:
                    act.wait_ge(stat_mean, idx + 1)
                    act.activation(var[:, 0, :], bank[4][:, :], ACT.Square).then_inc(mean_sq, 1)
                    act.wait_ge(var_ready, idx + 1)
                else:
                    act.wait_ge(stat_sq, idx + 1)
                eps = S_EPS5 if centred else S_EPS6
                src = var[:, 1, :] if centred else bank[5][:, :]
                link(act.activation(rstd[:, :], src, ACT.Ln, bias=small[:, eps:eps + 1]))
                act.activation(rstd[:, :], rstd[:, :], ACT.Exp, scale=-0.5).then_inc(rstd_ready, 1)
                for k in range(KD):
                    act.wait_ge(scaled, 8 * idx + k + 1)
                    if centred:
                        g, b = vcol(grow + k), vcol(brow + k)
                        if norm in OPERAND:
                            act.activation(ahi[:, k, :], res[:, k, :], ACT.Identity, bias=b, scale=g).then_inc(hi_act, 1)
                        act.activation(res[:, k, :], res[:, k, :], ACT.Identity, bias=b, scale=g).then_inc(normed, 1)
                        if norm == "ln4":
                            square_res("rms1", k)
                    else:
                        act.copy(ahi[:, k, :], hval[:, k % 2, :]).then_inc(hi_act, 1)
                    if between:
                        between(k)

            def ffn(name, norm, once=None):
                for part in range(len(PARTS)):
                    ph = phases[f"{name}_up{part}"]
                    t0 = part_tile0(ph.name)

                    def step(i, jj, ph=ph, t0=t0):
                        if jj % 2 == 0:
                            silu_gate(ph, i, jj, t0)
                        hi_stream(ph, i, jj)
                    each_block(act, ph, step)
                    if once and part == 0:
                        once()
                    ph = phases[f"{name}_down{part}"]
                    if norm and part == len(PARTS) - 1:
                        use_logs()
                    for j in range(KD):
                        hi_stream(ph, 0, j)
                        if norm and part == len(PARTS) - 1:
                            square_res(norm, j, ph)

            for b in range(2):
                split_hi(act, blocks[b][0], 0, blocks[b][1])
            for k in range(KD):
                act.wait_ge(s_xT, k + 1)
                act.copy(ahi[:, k, :], bank[4 + k % 4][:, :])
                act.copy(res[:, k, :], bank[4 + k % 4][:, :]).then_inc(s_xhi, 1)

            def bound_exps():
                act.wait_ge(s_vecs, 2)
                act.activation(small[:, S_E0:S_E0 + 8], small[:, S_E0:S_E0 + 8], ACT.Exp).then_inc(s_lbe, 1)

            ffn("f1", "ln1", bound_exps)
            norm_tail("ln1")

            def mixer(kind, n):
                if kind == "forget":
                    wait_in(act, FZ0 + n)
                    link(act.activation(cum[:, n, :], mk[:, n, :], ACT.Sigmoid))
                    act.activation(mk[:, n, :], mk[:, n, :], ACT.Sigmoid, scale=-1.0).then_inc(s_sig, 1)
                elif kind == "logs":
                    for h in range(HG):
                        act.wait_ge(s_fg, h + 1)
                        act.activation(cum[:, h, :], cum[:, h, :], ACT.Ln).then_inc(s_lf, 1)
                elif kind == "level" and n in NTH:
                    e = NTH[n]
                    act.wait_ge(s_arg, e + 1)
                    act.activation(dec[:, e % DEC, :], dec[:, e % DEC, :], ACT.Exp).then_inc(s_dexp, 1)
                elif kind == "ends":
                    if n == 0:
                        act.wait_ge(s_cum, 1)
                    else:
                        act.wait_ge(s_on, n)
                    act.activation(eb[:, :], cum[:, n, :], ACT.Exp).then_inc(s_ebd, 1)
                    act.wait_ge(s_kd, n + 1)
                    act.activation(kend[:, :], kend[:, :], ACT.Exp).then_inc(s_kde, 1)
                elif kind == "power":
                    act.wait_ge(s_om, n + 1)
                    act.activation(osq[:, :], bank[6][:, :], ACT.Square).then_inc(s_osq, 1)
                elif kind == "normed":
                    act.wait_ge(s_oss, n + 1)
                    link(act.activation(ors[:, :], bank[7][:, :], ACT.Ln, bias=small[:, S_EPS5:S_EPS5 + 1]))
                    act.activation(ors[:, :], ors[:, :], ACT.Exp, scale=-0.5).then_inc(s_ors, 1)
                elif kind == "gelu":
                    wait_in(act, V0 + n if n < SG else U0 + n - SG)
                    x = mv[:, n, :] if n < SG else mu[:, n - SG, :]
                    act.activation(x, x, ACT.Gelu_apprx_tanh).then_inc(s_gv, 1)
                elif kind == "centre":
                    act.wait_ge(s_sgv, n + 1)
                    link(act.activation(sgr[:, :], sgmv[:, :, 1], ACT.Ln, bias=small[:, S_EPS5:S_EPS5 + 1]))
                    act.activation(sgr[:, :], sgr[:, :], ACT.Exp, scale=-0.5).then_inc(s_sgr, 1)
                elif kind == "silu":
                    wait_in(act, G0 + n)
                    act.activation(mg[:, n, :], mg[:, n, :], ACT.Silu).then_inc(s_act2, 1)

            for n, tasks in enumerate(plan):
                for task in tasks:
                    mixer(*task)
                hi_stream(phases["in"], 0, n)
            wait_block(act, phases["in"], 0, 23)
            for n, k in enumerate(OUT_TILES):
                if n == 2:
                    mixer("silu", 3)
                wait_mixed(act, k)
                act.copy(ahi[:, k, :], mixed(k)).then_inc(hi_act, 1)

            use_logs()
            for j in range(KD):
                hi_stream(phases["out"], 0, j)
                square_res("ln2", j, phases["out"])
                if j == MEM_AT:
                    act.wait_ge(s_mv, 1)
                    link(act.activation(mrs[:, :], mmv[:, :, 1], ACT.Ln, bias=small[:, S_EPS5:S_EPS5 + 1]))
                    act.activation(mrs[:, :], mrs[:, :], ACT.Exp, scale=-0.5).then_inc(s_mr, 1)
                if j == MEM_AT + 1:
                    for k in range(KD):
                        act.wait_ge(s_ma, k + 1)
                        act.copy(mhi[:, k, :], mval[:, k % MVAL, :]).then_inc(s_mh, 1)
            norm_tail("ln2", lambda k: hi_stream(phases["mk"], 0, k))
            for name in ("mv", "xq"):
                for j in range(KD):
                    hi_stream(phases[name], 0, j)
            def cross_exp(h):
                for t in range(TT):
                    act.wait_ge(s_nm, h + 1)
                    if t == 0 and h >= 2:
                        act.wait_ge(s_pT, 2 * (h - 1))
                    i = act.activation(px[:, h % 2, t, :], bank[2 * (h % 2) + t // 2][:, (t % 2) * MEM:(t % 2 + 1) * MEM],
                                       ACT.Exp, bias=small[:, S_NM + 4 * (h % 2) + t:S_NM + 4 * (h % 2) + t + 1],
                                       scale=(D // XH) ** -0.5,
                                       accum_out=small[:, S_SM + 4 * (h % 2) + t:S_SM + 4 * (h % 2) + t + 1])
                    i.then_inc(s_pe, 1)

            cross_exp(0)
            for h in range(XH):
                if h + 1 < XH:
                    cross_exp(h + 1)
                act.wait_ge(s_pT, 2 * h + 2)
                if h >= 2:
                    act.wait_ge(s_pv, 2 * (h - 1))
                act.copy(pxT[:, h % 2, 1, :], bank[5][:, :]).then_inc(s_pca, 1)
                for d in range(2):
                    act.wait_ge(s_pv, 2 * h + d + 1)
                    act.copy(ahi[:, 2 * h + d, :], bank[6 + d][:, :]).then_inc(s_ah, 1)
            for j in range(KD):
                hi_stream(phases["xo"], 0, j)
                square_res("ln3", j, phases["xo"])
            norm_tail("ln3")
            ffn("f2", "ln4")
            norm_tail("ln4")
            norm_tail("rms1")
            for j in range(10):
                hi_stream(phases["in2"], 0, j)
            for j in range(5):
                x = in2_dst(j)
                act.wait_ge(bank_free, RAW + phases["in2"].base + j + 1)
                if j:
                    act.wait_ge(s_hr, j)
                act.activation(r1[:, 0, :], x, ACT.Square).then_inc(s_hsq, 1)
                act.wait_ge(s_hss, j + 1)
                link(act.activation(r2[:, 0, :], bank[4][:, :], ACT.Ln, bias=small[:, S_EPS6:S_EPS6 + 1]))
                act.activation(r2[:, 0, :], r2[:, 0, :], ACT.Exp, scale=-0.5).then_inc(s_hrs, 1)
            for n, g in enumerate(POOL_ORDER):
                act.wait_ge(s_py, n + 1)
                act.copy(ahi[:, 4 + g, :], po[:, n % 2, :]).then_inc(s_pyh, 1)
            def self_exp(h):
                for t in range(TT):
                    n = TT * h + t
                    act.wait_ge(s_nm, XH + n + 1)
                    if t == 0 and h >= 2:
                        act.wait_ge(s_pT, 2 * XH + TT * (h - 1))
                    c = S_NM + n % 8
                    act.activation(ps[:, h % 2, t, :], bank[n % 3][:, :], ACT.Exp, bias=small[:, c:c + 1],
                                   scale=HD ** -0.5, accum_out=small[:, S_SM + n % 8:S_SM + n % 8 + 1]).then_inc(s_pe, 1)

            self_exp(0)
            for h in range(QH):
                if h + 1 < QH:
                    self_exp(h + 1)
                for st in (1, 3):
                    act.wait_ge(s_pT, 2 * XH + TT * h + st + 1)
                    if h >= 2:
                        act.wait_ge(s_pv, 2 * XH + h - 1)
                    act.copy(psT[:, h % 2, st, :], bank[3 + (TT * h + st) % 3][:, :]).then_inc(s_pca, 1)
                if h % 2 == 1:
                    act.wait_ge(s_pv, 2 * XH + h + 1)
                    act.copy(ahi[:, h // 2, :], bank[6 + (h // 2) % 2][:, :]).then_inc(s_ah, 1)
            for j in range(KD):
                hi_stream(phases["out2"], 0, j)
                square_res("rms2", j, phases["out2"])
            norm_tail("rms2")
            ffn("f3", None)

        @block.gpsimd
        def _(pool):
            link = linker(pool, pool_chain)

            def lo_stream(ph, i, jj):
                ahead(split_lo, pool, ph, i, jj)

            def norm_tail(norm, between=None):
                idx, centred = NORMS[norm][:2]
                for k in range(KD):
                    if by(OPERAND[norm], k) == POOL:
                        if centred:
                            pool.wait_ge(normed, 8 * idx + k + 1)
                        else:
                            pool.wait_ge(hi_act, HI0[norm] + k + 1)
                        src = res[:, k, :] if centred else hval[:, k % 2, :]
                        pool.tensor_tensor(alo[:, k, :], src, ahi[:, k, :], ALU.subtract).then_inc(act_pool, 1)
                    if between:
                        between(k)

            def ffn(name):
                for part in range(len(PARTS)):
                    ph = phases[f"{name}_up{part}"]
                    each_block(pool, ph, lambda i, jj, ph=ph: lo_stream(ph, i, jj))
                    ph = phases[f"{name}_down{part}"]
                    for j in range(KD):
                        lo_stream(ph, 0, j)

            pool.sem_inc(lo_ready, RAW)
            pool.sem_inc(block_done, SPLIT)
            pool.sem_inc(bank_free, RAW)
            pool.sem_inc(value_done, 2)
            pool.sem_inc(hidden_ready, 2)
            link(pool.memset(small[:, S_EPS5:S_EPS5 + 1], LN_EPS))
            link(pool.memset(small[:, S_EPS6:S_EPS6 + 1], RMS_EPS))
            pool.memset(wT[:, :, :], 0.0).then_inc(s_wTz, 1)
            for b in range(2):
                split_lo(pool, blocks[b][0], 0, blocks[b][1])
            ffn("f1")
            norm_tail("ln1")
            def level_args(s):
                h, n = STEPS[s]
                e, lv = NTH[s], LEVELS[n]
                b, o = halves(cum[:, h, :], lv), halves(dec[:, e % DEC, :], lv)
                c = 1 << lv
                ref = b[:, :, 0, c - 1:c].broadcast_to([P, T // (2 * c), c])
                pool.wait_ge(s_cum, h + 1)
                if e >= DEC:
                    pool.wait_ge(s_qk, e - DEC + 1)
                pool.tensor_tensor(o[:, :, 0, :], ref, b[:, :, 0, :], ALU.subtract)
                pool.tensor_tensor(o[:, :, 1, :], b[:, :, 1, :], ref, ALU.subtract).then_inc(s_arg, 1)

            for n, tasks in enumerate(plan):
                if n == 1:
                    wait_block(pool, phases["in"], 0, 0)
                    link(pool.memset(qt[:, :, :], 0.0))
                    pool.memset(kt[:, :, :], 0.0).then_inc(s_az, 1)
                    for h in range(2):
                        pool.memset(acc[:, h, :], 0.0).then_inc(s_az, 1)
                lo_stream(phases["in"], 0, n)
                for kind, s in plan[n + 1] if n + 1 < len(plan) else []:
                    if kind == "level" and s in NTH:
                        level_args(s)
                    if kind == "power" and s + 2 < HG:
                        pool.wait_ge(s_om, s + 1)
                        pool.memset(acc[:, s % 2, :], 0.0).then_inc(s_az, 1)
            for n, k in enumerate(OUT_TILES):
                if by("out", n) == POOL:
                    pool.wait_ge(hi_act, 8 + n + 1)
                    pool.tensor_tensor(alo[:, k, :], mixed(k), ahi[:, k, :], ALU.subtract).then_inc(act_pool, 1)
            for j in range(KD):
                lo_stream(phases["out"], 0, j)
                if j == MEM_AT + 1:
                    for k in range(KD):
                        pool.wait_ge(s_mh, k + 1)
                        pool.tensor_tensor(mlo[:, k, :], mval[:, k % MVAL, :], mhi[:, k, :], ALU.subtract).then_inc(s_ml, 1)
            norm_tail("ln2", lambda k: lo_stream(phases["mk"], 0, k))
            for name in ("mv", "xq", "xo"):
                for j in range(KD):
                    lo_stream(phases[name], 0, j)
            norm_tail("ln3")
            ffn("f2")
            norm_tail("rms1")
            for j in range(10):
                lo_stream(phases["in2"], 0, j)
            for n, g in enumerate(POOL_ORDER):
                pool.wait_ge(bank_free, RAW + phases["in2"].base + 5 + n + 1)
                if n:
                    pool.wait_ge(s_pool, n)
                src = su[:, n, :]
                bufs = [pa, pb]
                for lv in range(g + 1):
                    w = (1 << lv) // 2
                    reach = (1 << g) - (1 << lv)
                    lo, wide = 8 - reach, T + 2 * reach
                    dst = bufs[lv % 2]
                    a0, a1 = (lo - 1, lo) if lv == 0 else (lo - w, lo + w)
                    link(pool.tensor_tensor(dst[:, lo:lo + wide], src[:, a0:a0 + wide], src[:, a1:a1 + wide], ALU.add))
                    src = dst
                pool.wait_ge(s_rcn[n % 2], 16 * (n // 2 + 1))
                link(pool.tensor_tensor(src[:, 8:8 + T], src[:, 8:8 + T], rcnt[:, n % 2, :], ALU.mult))
                pool.tensor_tensor(su[:, n, 8:8 + T], src[:, 8:8 + T], su[:, n, 8:8 + T], ALU.subtract).then_inc(s_pool, 1)
            for j in range(KD):
                lo_stream(phases["out2"], 0, j)
            norm_tail("rms2")
            ffn("f3")

        @block.vector
        def _(dve):
            link = linker(dve, dve_chain)

            def hidden(ph, i, jj, t0, scale):
                tile = t0 + 2 * i + jj // 2
                slot = (t0 + jj // 2) % 2
                at = 2 * i + jj // 2
                wait_block(dve, ph, i, jj)
                dve.wait_ge(gate_done, tile + 1)
                dve.wait_ge(hidden_ready, tile + 1)
                dve.scalar_tensor_tensor(out=hval[:, slot, :], in0=gate[:, slot, :], scalar=scale,
                                         in1=bank_of(ph, jj)[:, :], op0=ALU.mult, op1=ALU.mult).then_inc(value_done, 1)
                dve.wait_ge(value_done, 2 + tile + 1)
                dve.tensor_copy(hhi[:, bass.ds(at, 1), :].rearrange("p a t -> p (a t)"), hval[:, slot, :]).then_inc(bank_free, 2)
                dve.wait_ge(bank_free, RAW + ph.base + jj + 4 * i + 1)
                dve.tensor_tensor(hlo[:, bass.ds(at, 1), :].rearrange("p a t -> p (a t)"), hval[:, slot, :],
                                  hhi[:, bass.ds(at, 1), :].rearrange("p a t -> p (a t)"), ALU.subtract).then_inc(hidden_ready, 1)

            def add_res(ph, j, scale):
                wait_block(dve, ph, 0, j)
                dve.scalar_tensor_tensor(out=res[:, j, :], in0=res[:, j, :], scalar=scale,
                                         in1=bank_of(ph, j)[:, :], op0=ALU.mult, op1=ALU.add).then_inc(bank_free, 1)

            def add_sums(norm, j):
                idx, centred = NORMS[norm][:2]
                if not 1 <= j <= SUM_STEPS:
                    return
                dve.wait_ge(square_done, 8 * idx + j + 1)
                if j > 1:
                    dve.wait_ge(sums_done, SUM_STEPS * idx + j - 1)
                last = (res[:, 0, :], square[:, 0, :]) if j == 1 else (sum1[:, :], sum2[:, :])
                if centred:
                    dve.tensor_tensor(sum1[:, :], last[0], res[:, j, :], ALU.add)
                dve.tensor_tensor(sum2[:, :], last[1], square[:, j % 2, :], ALU.add).then_inc(sums_done, 1)

            def norm_tail(norm, between=None):
                idx, centred, grow, brow = NORMS[norm]
                layer = OPERAND.get(norm)
                if centred:
                    dve.wait_ge(stat_sq, idx + 1)
                    dve.wait_ge(mean_sq, idx + 1)
                    link(dve.tensor_tensor(var[:, 1, :], bank[5][:, :], var[:, 0, :], ALU.subtract))
                    dve.tensor_scalar(var[:, 1, :], var[:, 1, :], 0.0, None, ALU.max).then_inc(var_ready, 1)
                    link(dve.tensor_copy(mean[:, :], bank[4][:, :]))
                    link(dve.tensor_tensor(res[:, 0, :], res[:, 0, :], mean[:, :], ALU.subtract))
                dve.wait_ge(rstd_ready, idx + 1)

                def lo(k):
                    if k >= 0 and layer and by(layer, k) == DVE:
                        dve.wait_ge(*((normed, 8 * idx + k + 1) if centred else (hi_act, HI0[norm] + k + 1)))
                        src = res[:, k, :] if centred else hval[:, k % 2, :]
                        dve.tensor_tensor(alo[:, k, :], src, ahi[:, k, :], ALU.subtract).then_inc(act_dve, 1)
                for k in range(KD):
                    if centred:
                        if k:
                            link(dve.tensor_tensor(res[:, k, :], res[:, k, :], mean[:, :], ALU.subtract))
                        dve.tensor_tensor(res[:, k, :], res[:, k, :], rstd[:, :], ALU.mult).then_inc(scaled, 1)
                        if norm == "ln4":
                            add_sums("rms1", k - 2)
                    else:
                        if k >= 2:
                            dve.wait_ge(*operand(layer, k - 2))
                        dve.scalar_tensor_tensor(out=hval[:, k % 2, :], in0=res[:, k, :], scalar=vcol(grow + k),
                                                 in1=rstd[:, :], op0=ALU.mult, op1=ALU.mult).then_inc(scaled, 1)
                    lo(k - 1)
                    if between:
                        between(k)
                if norm == "ln4":
                    add_sums("rms1", KD - 2)
                lo(KD - 1)

            def ffn(name, alpha, scale, norm, once=None):
                for part in range(len(PARTS)):
                    ph = phases[f"{name}_up{part}"]
                    t0 = part_tile0(ph.name)

                    def step(i, jj, ph=ph, t0=t0):
                        if jj % 2:
                            hidden(ph, i, jj, t0, scale)
                    each_block(dve, ph, step)
                    if once and part == 0:
                        once()
                    ph = phases[f"{name}_down{part}"]
                    last = part == len(PARTS) - 1
                    for j in range(KD):
                        if last and norm:
                            add_sums(norm, j - 1)
                        add_res(ph, j, alpha if part == 0 else 1.0)
                        if last and norm is None and j >= 1:
                            store_tile(j - 1)
                if norm is None:
                    store_tile(KD - 1)

            def store_tile(j):
                dve.wait_ge(s_oT, j + 1)
                if j >= 2:
                    dve.wait_ge(s_out, 16 * (j - 1))
                dve.tensor_copy(ob[:, j % 2, :, :], bank[4 + j % 2][:, :].rearrange("p (n f) -> p n f", f=P)).then_inc(s_ob, 1)

            for k in range(KD):
                dve.wait_ge(s_xhi, k + 1)
                dve.tensor_tensor(alo[:, k, :], res[:, k, :], ahi[:, k, :], ALU.subtract).then_inc(act_dve, 1)

            def vectors():
                dve.wait_ge(s_vT0, 1)
                link(dve.tensor_copy(vecs[:, 0:V_ROWS], bank[4][:, 0:V_ROWS]))
                link(dve.tensor_tensor(small[:, S_LB:S_LB + 4], vecs[:, V_LB:V_LB + 4], vecs[:, V_LB + 4:V_LB + 8], ALU.max))
                dve.tensor_tensor(small[:, S_E0:S_E0 + 4], vecs[:, V_LB:V_LB + 4], small[:, S_LB:S_LB + 4], ALU.subtract).then_inc(s_vecs, 1)
                dve.tensor_tensor(small[:, S_E1:S_E1 + 4], vecs[:, V_LB + 4:V_LB + 8], small[:, S_LB:S_LB + 4], ALU.subtract).then_inc(s_vecs, 1)
                dve.wait_ge(s_wsT, 1)
                dve.wait_ge(s_wTz, 1)
                dve.wait_ge(s_const, 48)
                dve.copy_predicated(wT[:, :, :], masks[:, len(LEVELS) + 1:len(LEVELS) + 2, :].broadcast_to([P, SG, P]),
                                    bank[5][:, :].rearrange("p (g t) -> p g t", g=SG)).then_inc(s_wTr, 1)
                dve.wait_ge(s_lbe, 1)
                link(dve.tensor_tensor(small[:, S_OML:S_OML + 4], small[:, S_E0:S_E0 + 4], small[:, S_E1:S_E1 + 4], ALU.add))
                link(dve.reciprocal(small[:, S_OML:S_OML + 4], small[:, S_OML:S_OML + 4]))
                link(dve.tensor_tensor(small[:, S_LB:S_LB + 4], small[:, S_E0:S_E0 + 4], small[:, S_OML:S_OML + 4], ALU.mult))
                link(dve.tensor_scalar(small[:, S_OML:S_OML + 4], small[:, S_LB:S_LB + 4], -1.0, 1.0, ALU.mult, ALU.add))

            ffn("f1", ALPHA, 0.5, "ln1", vectors)
            norm_tail("ln1")

            def level_scale(s):
                h, n = STEPS[s]
                e, lv = NTH[s], LEVELS[n]
                d = halves(dec[:, e % DEC, :], lv)
                dve.wait_ge(s_dexp, e + 1)
                if e >= 2:
                    dve.wait_ge(s_smm, SCALED[e - 2] + 1)
                else:
                    dve.wait_ge(s_az, 1)
                dve.tensor_tensor(halves(qt[:, e % 2, :], lv)[:, :, 1, :], halves(mq[:, h, :], lv)[:, :, 1, :],
                                  d[:, :, 1, :], ALU.mult)
                dve.tensor_tensor(halves(kt[:, e % 2, :], lv)[:, :, 0, :], halves(mk[:, h, :], lv)[:, :, 0, :],
                                  d[:, :, 0, :], ALU.mult).then_inc(s_qk, 1)

            def level_put(s):
                h, n = STEPS[s]
                dve.wait_ge(s_smm, s + 1)
                dve.wait_ge(s_az, 1 + h + 1)
                if s:
                    dve.wait_ge(s_put, s)
                dve.copy_predicated(acc[:, h % 2, :].rearrange("p (n t) -> p n t", t=P),
                                    masks[:, n:n + 1, :].broadcast_to([P, TT, P]),
                                    bank[4 + s % 2][:, :].rearrange("p (n t) -> p n t", t=P)).then_inc(s_put, 1)

            def mixer(kind, n):
                if kind == "forget":
                    lb, oml = small[:, S_LB + n:S_LB + n + 1], small[:, S_OML + n:S_OML + n + 1]
                    dve.wait_ge(s_sig, n + 1)
                    link(dve.tensor_scalar(cum[:, n, :], cum[:, n, :], oml, lb, ALU.mult, ALU.add))
                    link(dve.tensor_scalar(cum[:, n, :], cum[:, n, :], 2.0 ** -60, None, ALU.max))
                    dve.tensor_scalar(mk[:, n, :], mk[:, n, :], oml, None, ALU.mult).then_inc(s_fg, 1)
                elif kind == "logs":
                    for h in range(HG):
                        dve.wait_ge(s_lf, h + 1)
                        dve.tensor_tensor_scan(cum[:, h, :], restart[:, :], cum[:, h, :], 0.0, ALU.mult, ALU.add).then_inc(s_cum, 1)
                elif kind == "take_values":
                    dve.wait_ge(s_ivT, n + 1)
                    dve.tensor_copy(vT[:, n, :, :], bank[7][:, :].rearrange("p (n f) -> p n f", f=P)).then_inc(s_ivc, 1)
                elif kind == "level" and n in NTH:
                    if STEPS[n][1] == 0:
                        wait_in(dve, Q0 + STEPS[n][0])
                    level_scale(n)
                elif kind == "put":
                    level_put(n)
                elif kind == "ends":
                    c, q, k = cum[:, n, :], mq[:, n, :], mk[:, n, :]
                    ct = c.rearrange("p (n t) -> p n t", t=P)
                    if n:
                        dve.wait_ge(s_keT, n)
                    dve.tensor_tensor(kend[:, :].rearrange("p (n t) -> p n t", t=P), ct[:, 0:3, P - 1:P].broadcast_to([P, 3, P]),
                                      ct[:, 0:3, :], ALU.subtract).then_inc(s_kd, 1)
                    dve.wait_ge(s_ebd, n + 1)
                    link(dve.tensor_tensor(qe[:, :], q, eb[:, :], ALU.mult))
                    dve.wait_ge(s_kde, n + 1)
                    dve.tensor_tensor(kend[:, :], kend[:, :], k[:, 0:3 * P], ALU.mult).then_inc(s_ke, 1)
                elif kind == "update":
                    dve.wait_ge(s_keT, n + 1)
                    dve.tensor_copy(kendT[:, :], bank[7][:, 0:3 * P]).then_inc(s_kec, 1)
                elif kind == "outputs":
                    dve.wait_ge(s_um, n + 1)
                    link(dve.tensor_copy(state[:, 0, :], bank[7][:, 0:P]))
                    for j in range(1, 3):
                        i = dve.scalar_tensor_tensor(out=state[:, j, :], in0=state[:, j - 1, :],
                                                     scalar=eb[:, (j + 1) * P - 1:(j + 1) * P],
                                                     in1=bank[7][:, j * P:(j + 1) * P], op0=ALU.mult, op1=ALU.add)
                        if j == 1:
                            link(i)
                    i.then_inc(s_st, 1)
                elif kind == "normed":
                    dve.wait_ge(s_ors, n + 1)
                    dve.scalar_tensor_tensor(out=mq[:, n, :], in0=bank[6][:, :], scalar=vcol(V_HGN), in1=ors[:, :],
                                             op0=ALU.mult, op1=ALU.mult).then_inc(s_on, 1)
                elif kind == "gate":
                    dve.wait_ge(s_act2, n + 1)
                    dve.wait_ge(s_on, n + 1)
                    dve.tensor_tensor(mq[:, n, :], mq[:, n, :], mg[:, n, :], ALU.mult).then_inc(s_prod, 1)
                elif kind == "centre":
                    pb_ = bank[SPATIAL_BANK[n]]
                    dve.wait_ge(s_gvT, n + 1)
                    for t in range(TT):
                        link(dve.bn_stats(sgst[:, t, :], pb_[:, t * P:(t + 1) * P]))
                    for t in range(TT):
                        i = dve.bn_aggr(sgmv[:, t, :], sgst[:, t, :])
                        if t < TT - 1:
                            link(i)
                    i.then_inc(s_sgv, 1)
                    dve.wait_ge(s_sgr, n + 1)
                    for t in range(TT):
                        link(dve.tensor_scalar(vn[:, n, t * P:(t + 1) * P], pb_[:, t * P:(t + 1) * P],
                                               sgmv[:, t, 0:1], sgr[:, t:t + 1], ALU.subtract, ALU.mult))
                    v3 = vn[:, n, :].rearrange("p (n f) -> p n f", f=P)
                    dve.wait_ge(s_rows, 48)
                    link(dve.tensor_tensor(v3, v3, row(0, n), ALU.mult))
                    dve.tensor_tensor(v3, v3, row(1, n), ALU.add).then_inc(s_vn, 1)
                elif kind == "bias":
                    dve.wait_ge(s_sm, n + 1)
                    dve.tensor_tensor(mv[:, n, :].rearrange("p (n f) -> p n f", f=P),
                                      bank[SPATIAL_BANK[n]][:, :].rearrange("p (n f) -> p n f", f=P), row(2, n), ALU.add).then_inc(s_so, 1)
                elif kind == "spatial":
                    dve.wait_ge(s_gv, 4 + n + 1)
                    dve.wait_ge(s_so, n + 1)
                    dve.tensor_tensor(mu[:, n, :], mu[:, n, :], mv[:, n, :], ALU.mult).then_inc(s_mul, 1)

            def row(r, g):
                return sgb[:, r, g * P:(g + 1) * P].unsqueeze(1).broadcast_to([P, TT, P])

            for n, tasks in enumerate(plan):
                for task in tasks:
                    mixer(*task)
                if IN_ORDER[n] in (IV0 + 2, IV0 + 3):
                    dve.wait_ge(s_ivT, IN_ORDER[n] - IV0 - 1)
                wait_block(dve, phases["in"], 0, n)
                dve.tensor_copy(IN_DST[n], bank_of(phases["in"], n)[:, :]).then_inc(bank_free, 1)
            for n, k in enumerate(OUT_TILES):
                if n == 3:
                    mixer("gate", 3)
                if by("out", n) == DVE:
                    dve.wait_ge(hi_act, 8 + n + 1)
                    dve.tensor_tensor(alo[:, k, :], mixed(k), ahi[:, k, :], ALU.subtract).then_inc(act_dve, 1)
            for j in range(KD):
                add_sums("ln2", j - 1)
                add_res(phases["out"], j, ALPHA)
                if j == MEM_AT - 1:
                    dve.wait_ge(s_mem, 16)
                    for t in range(MT):
                        for hf in range(2):
                            link(dve.bn_stats(mst[:, 2 * t + hf, :], memin[:, t, hf * T:(hf + 1) * T]))
                    for t in range(MT):
                        link(dve.bn_aggr(mmv[:, t, :], mst[:, 2 * t:2 * t + 2, :].rearrange("p a b -> p (a b)")))
                    dve.sem_inc(s_mv, 1)
                if j == MEM_AT:
                    dve.wait_ge(s_mr, 1)
                    for t in range(MT):
                        dve.tensor_scalar(memin[:, t, :], memin[:, t, :], mmv[:, t, 0:1], mrs[:, t:t + 1],
                                          ALU.subtract, ALU.mult).then_inc(s_mn, 1)
                if j == MEM_AT + 1:
                    for k in range(KD):
                        dve.wait_ge(s_mT, k // 2 + 1)
                        if k >= MVAL:
                            dve.wait_ge(s_ml, k - MVAL + 1)
                        dve.tensor_scalar(mval[:, k % MVAL, :], bank[4 + k // 2][:, (k % 2) * MEM:(k % 2 + 1) * MEM],
                                          vcol(V_MEMG + k), vcol(V_MEMB + k), ALU.mult, ALU.add).then_inc(s_ma, 1)

            def mem_key(j):
                wait_block(dve, phases["mk"], 0, j)
                dve.tensor_copy(kx[:, j, :], bank_of(phases["mk"], j)[:, 0:MEM]).then_inc(bank_free, 1)
            norm_tail("ln2", mem_key)
            for j in range(KD):
                wait_block(dve, phases["mv"], 0, j)
                if j >= 2:
                    dve.wait_ge(s_vxT, j - 1)
                dve.tensor_copy(vxt[:, j % 2, :], bank_of(phases["mv"], j)[:, 0:MEM]).then_inc(bank_free, 1)
                if j >= 1:
                    dve.wait_ge(s_vxT, j)
                    dve.tensor_copy(vx[:, :, (j - 1) * P:j * P], bank[4 + (j - 1) % 2][:, 0:MEM].rearrange("p (n f) -> p n f", f=P)).then_inc(s_kv, 1)
            dve.wait_ge(s_vxT, KD)
            dve.tensor_copy(vx[:, :, (KD - 1) * P:KD * P], bank[4 + (KD - 1) % 2][:, 0:MEM].rearrange("p (n f) -> p n f", f=P)).then_inc(s_kv, 1)
            for j in range(KD):
                wait_block(dve, phases["xq"], 0, j)
                dve.tensor_copy(qx[:, j, :], bank_of(phases["xq"], j)[:, :]).then_inc(bank_free, 1)
            def cross_max(h):
                m0 = S_MX + 4 * (h % 2)
                dve.wait_ge(s_sc, h + 1)
                for half in range(2):
                    link(dve.tensor_reduce(small[:, m0 + 2 * half:m0 + 2 * half + 2],
                                           bank[2 * (h % 2) + half][:, :].rearrange("p (n m) -> p n m", m=MEM), AX.X, ALU.max))
                n0 = S_NM + 4 * (h % 2)
                dve.tensor_scalar(small[:, n0:n0 + 4], small[:, m0:m0 + 4], -(D // XH) ** -0.5, None, ALU.mult).then_inc(s_nm, 1)

            cross_max(0)
            for h in range(XH):
                r0 = S_RI + 4 * (h % 2)
                dve.wait_ge(s_pe, TT * (h + 1))
                link(dve.reciprocal(small[:, r0:r0 + 4], small[:, S_SM + 4 * (h % 2):S_SM + 4 * (h % 2) + 4]))
                for t in range(TT):
                    dve.tensor_scalar(px[:, h % 2, t, :], px[:, h % 2, t, :], small[:, r0 + t:r0 + t + 1], None,
                                      ALU.mult).then_inc(s_pn, 1)
                if h + 1 < XH:
                    cross_max(h + 1)
                dve.wait_ge(s_pT, 2 * h + 1)
                if h >= 2:
                    dve.wait_ge(s_pv, 2 * (h - 1))
                dve.tensor_copy(pxT[:, h % 2, 0, :], bank[4][:, :]).then_inc(s_pcd, 1)
                for d in range(2):
                    dve.wait_ge(s_ah, 2 * h + d + 1)
                    dve.tensor_tensor(alo[:, 2 * h + d, :], bank[6 + d][:, :], ahi[:, 2 * h + d, :], ALU.subtract).then_inc(act_dve, 1)
            for j in range(KD):
                add_sums("ln3", j - 1)
                add_res(phases["xo"], j, ALPHA)
            norm_tail("ln3")
            ffn("f2", ALPHA, 0.5, "ln4")
            norm_tail("ln4")
            norm_tail("rms1")
            ph = phases["in2"]
            for j in range(10):
                wait_block(dve, ph, 0, j)
                if j == 5:
                    link(dve.memset(su[:, :, 0:8], 0.0))
                    link(dve.memset(su[:, :, 8 + T:16 + T], 0.0))
                dst = in2_dst(j)
                dve.tensor_copy(dst, bank_of(ph, j)[:, :]).then_inc(bank_free, 1)
            dve.wait_ge(s_rope, 32)
            for j in range(5):
                x = in2_dst(j)
                dve.wait_ge(s_hrs, j + 1)
                dve.scalar_tensor_tensor(out=x, in0=x, scalar=vcol(V_QN if j else V_KN), in1=r2[:, 0, :],
                                         op0=ALU.mult, op1=ALU.mult).then_inc(s_hn, 1)
                dve.wait_ge(s_hrot, j + 1)
                link(dve.tensor_tensor(r3[:, :], bank[5][:, :], rope[:, 1, :], ALU.mult))
                link(dve.tensor_tensor(x, x, rope[:, 0, :], ALU.mult))
                dve.tensor_tensor(x, x, r3[:, :], ALU.add).then_inc(s_hr, 1)
                dve.wait_ge(s_hr, j + 1)
            for g in range(2):
                dve.wait_ge(s_dup, g + 1)
                dve.tensor_copy(kk[:, g, :], bank[6 + g][:, :]).then_inc(s_dupc, 1)
            dve.wait_ge(s_svT, 1)
            dve.tensor_copy(sv[:, :, :], bank[4][:, :].rearrange("p (n f) -> p n f", f=P)).then_inc(s_dupc, 1)
            for n, g in enumerate(POOL_ORDER):
                dve.wait_ge(s_pmm, n + 1)
                dve.tensor_scalar(po[:, n % 2, :], bank[4 + n % 2][:, :], vcol(V_POOLB + g), vcol(V_POOLS + g),
                                  ALU.add, ALU.mult).then_inc(s_py, 1)
                dve.wait_ge(s_pyh, n + 1)
                dve.tensor_tensor(alo[:, 4 + g, :], po[:, n % 2, :], ahi[:, 4 + g, :], ALU.subtract).then_inc(act_dve, 1)
            def self_max(h):
                for t in range(TT):
                    n = TT * h + t
                    c = n % 8
                    dve.wait_ge(s_sc, XH + n + 1)
                    link(dve.tensor_reduce(small[:, S_MX + c:S_MX + c + 1], bank[n % 3][:, :], AX.X, ALU.max))
                    dve.tensor_scalar(small[:, S_NM + c:S_NM + c + 1], small[:, S_MX + c:S_MX + c + 1], -HD ** -0.5, None,
                                      ALU.mult).then_inc(s_nm, 1)

            self_max(0)
            for h in range(QH):
                for t in range(TT):
                    n = TT * h + t
                    c = n % 8
                    dve.wait_ge(s_pe, TT * XH + n + 1)
                    link(dve.reciprocal(small[:, S_RI + c:S_RI + c + 1], small[:, S_SM + c:S_SM + c + 1]))
                    dve.tensor_scalar(ps[:, h % 2, t, :], ps[:, h % 2, t, :], small[:, S_RI + c:S_RI + c + 1], None,
                                      ALU.mult).then_inc(s_pn, 1)
                if h + 1 < QH:
                    self_max(h + 1)
                for st in (0, 2):
                    dve.wait_ge(s_pT, 2 * XH + TT * h + st + 1)
                    if h >= 2:
                        dve.wait_ge(s_pv, 2 * XH + h - 1)
                    dve.tensor_copy(psT[:, h % 2, st, :], bank[3 + (TT * h + st) % 3][:, :]).then_inc(s_pcd, 1)
                if h % 2 == 1:
                    dve.wait_ge(s_ah, 2 * XH + h // 2 + 1)
                    dve.tensor_tensor(alo[:, h // 2, :], bank[6 + (h // 2) % 2][:, :], ahi[:, h // 2, :],
                                      ALU.subtract).then_inc(act_dve, 1)
            for j in range(KD):
                add_sums("rms2", j - 1)
                add_res(phases["out2"], j, 1.0)
            norm_tail("rms2")
            ffn("f3", 1.0, 1.0, None)

        @block.tensor
        def _(pe):
            def linear(name, ready=None, xhi=ahi, xlo=alo, width=T, after=None, order=None):
                ph = phases[name]
                multiply_two(pe, ph, xhi, xlo, width, ready or made(name), order=order)
                for j in range(ph.n):
                    if j >= 2:
                        multiply(pe, ph, 0, j, xhi, xlo, width)
                    if j >= 1 and after:
                        after(j)

            def made(layer):
                return lambda k: operand(layer, k)

            def stats(norm, ph=None):
                idx, centred = NORMS[norm][:2]
                last = KD - 1
                pe.wait_ge(sums_done, SUM_STEPS * (idx + 1))
                if centred:
                    pe.matmul(bank[4][:, :], mats[:, C_MEAN, :], sum1[:, :], start=True, stop=False)
                pe.matmul(bank[5][:, :], mats[:, C_MEAN, :], sum2[:, :], start=True, stop=False)
                if centred:
                    pe.wait_ge(bank_free, RAW + ph.base + last + 1)
                    pe.matmul(bank[4][:, :], mats[:, C_MEAN, :], res[:, last, :], start=False, stop=True).then_inc(stat_mean, 1)
                pe.wait_ge(square_done, 8 * (idx + 1))
                pe.matmul(bank[5][:, :], mats[:, C_MEAN, :], square[:, last % 2, :], start=False, stop=True).then_inc(stat_sq, 1)

            def ffn(name, norm, once=None, before=None):
                for part in range(len(PARTS)):
                    ph = phases[f"{name}_up{part}"]
                    if part == 0:
                        multiply_two(pe, ph, ahi, alo, T, made(name), before)
                        for jj in range(2, 4):
                            multiply(pe, ph, 0, jj, ahi, alo)
                        start = 1
                    else:
                        start = 0
                    with pe.Fori(start, ph.n // 4) as i:
                        for jj in range(4):
                            multiply(pe, ph, i, jj, ahi, alo)
                    if once and part == 0:
                        once()
                    ph = phases[f"{name}_down{part}"]
                    t0 = part_tile0(ph.name)
                    for j in range(KD):
                        r = (lambda k: (hidden_ready, 2 + t0 + k + 1)) if j == 0 else None
                        multiply(pe, ph, 0, j, hhi, hlo, T, r)
                        if norm is None and part == len(PARTS) - 1 and j >= 1:
                            store_tile(ph, j - 1)
                if norm:
                    stats(norm, ph)
                else:
                    store_tile(ph, KD - 1)

            def store_tile(ph, j):
                pe.wait_ge(bank_free, RAW + ph.base + j + 1)
                if j >= 2:
                    pe.wait_ge(s_ob, j - 1)
                for t in range(TT):
                    i = pe.transpose(bank[4 + j % 2][:, t * P:(t + 1) * P], res[:, j, t * P:(t + 1) * P], ident)
                i.then_inc(s_oT, 1)

            def four(o, src, s):
                for t in range(TT):
                    i = pe.transpose(o[:, t * P:(t + 1) * P], src[:, t * P:(t + 1) * P], ident)
                i.then_inc(s, 1)

            def turn_x(k):
                pe.wait_ge(s_x[k // 4], 16)
                if k >= 4:
                    pe.wait_ge(s_xhi, k - 3)
                for t in range(TT):
                    i = pe.transpose(bank[4 + k % 4][:, t * P:(t + 1) * P], xin[:, t, k * P:(k + 1) * P], ident)
                i.then_inc(s_xT, 1)

            def turn_vectors():
                pe.wait_ge(s_const, 48)
                pe.wait_ge(s_vec, 16 * 20)
                pe.transpose(bank[4][:, 0:V_ROWS], vrow[0:V_ROWS, :], ident[0:V_ROWS, 0:V_ROWS]).then_inc(s_vT0, 1)
                pe.wait_ge(s_ws, 16)
                for g in range(SG):
                    i = pe.transpose(bank[5][:, g * P:(g + 1) * P], wsin[:, g, :], ident)
                i.then_inc(s_wsT, 1)

            pe.wait_ge(s_ident, 16)
            for k in range(4):
                turn_x(k)
            ffn("f1", "ln1", turn_vectors, lambda k: turn_x(k + 4) if k < 4 else None)

            def level_product(s):
                h, n = STEPS[s]
                if n < len(LEVELS):
                    e = NTH[s]
                    pe.wait_ge(s_qk, e + 1)
                    q, k = qt[:, e % 2, :], kt[:, e % 2, :]
                else:
                    q, k = mq[:, h, :], mk[:, h, :]
                if s >= 2:
                    pe.wait_ge(s_put, s - 1)
                for t in range(TT):
                    i = pe.matmul(bank[4 + s % 2][:, t * P:(t + 1) * P], k[:, t * P:(t + 1) * P], q[:, t * P:(t + 1) * P],
                                  start=True, stop=True)
                i.then_inc(s_smm, 1)

            ph = phases["in"]
            def mixer(kind, n):
                o, u = bank[6], bank[7]
                if kind == "values":
                    wait_in(pe, IV0 + n)
                    if n:
                        pe.wait_ge(s_st, n)
                    four(u, ivt[:, n % 2, :], s_ivT)
                elif kind == "level":
                    level_product(n)
                elif kind == "ends":
                    pe.wait_ge(s_ke, n + 1)
                    if n:
                        pe.wait_ge(s_ors, n)
                    if n == 0:
                        pe.wait_ge(s_ivc, 1)
                    for t in range(3):
                        i = pe.transpose(u[:, t * P:(t + 1) * P], kend[:, t * P:(t + 1) * P], ident)
                    i.then_inc(s_keT, 1)
                elif kind == "update":
                    pe.wait_ge(s_kec, n + 1)
                    pe.wait_ge(s_ivc, n + 1)
                    for t in range(3):
                        i = pe.matmul(u[:, t * P:(t + 1) * P], kendT[:, t * P:(t + 1) * P], vT[:, n, t, :], start=True, stop=True)
                    i.then_inc(s_um, 1)
                elif kind == "outputs":
                    pe.wait_ge(s_st, n + 1)
                    pe.wait_ge(s_put, (n + 1) * (len(LEVELS) + 1))
                    if n:
                        pe.wait_ge(s_so, n)
                    for t in range(TT):
                        ot = o[:, t * P:(t + 1) * P]
                        i = pe.matmul(ot, vT[:, n, t, :], acc[:, n % 2, t * P:(t + 1) * P], start=True, stop=(t == 0))
                        if t:
                            i = pe.matmul(ot, state[:, t - 1, :], qe[:, t * P:(t + 1) * P], start=False, stop=True)
                    i.then_inc(s_om, 1)
                elif kind == "power":
                    if n + 1 < HG:
                        pe.wait_ge(s_ivc, n + 2)
                    pe.wait_ge(s_osq, n + 1)
                    pe.matmul(u[:, :], mats[:, C_M128, :], osq[:, :], start=True, stop=True).then_inc(s_oss, 1)
                elif kind == "turn":
                    pe.wait_ge(s_gv, n + 1)
                    if SPATIAL_BANK[n] == 6:
                        pe.wait_ge(s_on, n + 1)
                    else:
                        pe.wait_ge(s_put, len(STEPS))
                    four(bank[SPATIAL_BANK[n]], mv[:, n, :], s_gvT)
                elif kind == "centre":
                    pe.wait_ge(s_vn, n + 1)
                    pe.wait_ge(s_wTr, 1)
                    for t in range(TT):
                        i = pe.matmul(bank[SPATIAL_BANK[n]][:, t * P:(t + 1) * P], vn[:, n, t * P:(t + 1) * P], wT[:, n, :],
                                      start=True, stop=True)
                    i.then_inc(s_sm, 1)

            multiply_two(pe, ph, ahi, alo, T, made("in"))
            for n, tasks in enumerate(plan):
                if n >= 2:
                    multiply(pe, ph, 0, n, ahi, alo)
                for task in tasks:
                    mixer(*task)

            def turn_memory(j):
                if j == MEM_AT:
                    pe.wait_ge(s_mn, MT)
                    for k in range(KD):
                        for t in range(MT):
                            at = (k % 2) * MEM + t * P
                            i = pe.transpose(bank[4 + k // 2][:, at:at + P], memin[:, t, k * P:(k + 1) * P], ident)
                        if k % 2:
                            i.then_inc(s_mT, 1)
            linear("out", after=turn_memory, order=OUT_TILES)

            def stats_ln2(j):
                if j == 1:
                    pe.wait_ge(s_ma, KD)
                    stats("ln2", phases["out"])
            linear("mk", lambda k: (s_ml, k + 1), mhi, mlo, MEM, after=stats_ln2)

            def turn_values(j):
                if j < 1:
                    return
                if j == 1:
                    pe.wait_ge(var_ready, 2)
                pe.wait_ge(bank_free, RAW + phases["mv"].base + j)
                if j >= 3:
                    pe.wait_ge(s_kv, j - 2)
                for t in range(MT):
                    i = pe.transpose(bank[4 + (j - 1) % 2][:, t * P:(t + 1) * P], vxt[:, (j - 1) % 2, t * P:(t + 1) * P], ident)
                i.then_inc(s_vxT, 1)
            linear("mv", lambda k: (s_ml, KD), mhi, mlo, MEM, after=turn_values)
            turn_values(KD)
            linear("xq")
            def cross_scores(h):
                pe.wait_ge(bank_free, RAW + phases["xq"].base + KD)
                if h >= 2:
                    pe.wait_ge(s_pe, TT * (h - 1))
                for t in range(TT):
                    for k in range(2):
                        i = pe.matmul(bank[2 * (h % 2) + t // 2][:, (t % 2) * MEM:(t % 2 + 1) * MEM],
                                      qx[:, 2 * h + k, t * P:(t + 1) * P], kx[:, 2 * h + k, :], start=(k == 0), stop=(k == 1))
                i.then_inc(s_sc, 1)

            cross_scores(0)
            for h in range(XH):
                if h + 1 < XH:
                    cross_scores(h + 1)
                pe.wait_ge(s_pn, TT * (h + 1))
                if h:
                    pe.wait_ge(s_pcd, h)
                    pe.wait_ge(s_pca, h)
                else:
                    pe.wait_ge(s_kv, KD)
                for m in range(MT):
                    for t in range(TT):
                        i = pe.transpose(bank[4 + m][:, t * P:(t + 1) * P], px[:, h % 2, t, m * P:(m + 1) * P], ident)
                    i.then_inc(s_pT, 1)
                pe.wait_ge(s_pcd, h + 1)
                pe.wait_ge(s_pca, h + 1)
                if h:
                    pe.wait_ge(*operand("xo", 2 * h - 1))
                for d in range(2):
                    for m in range(MT):
                        i = pe.matmul(bank[6 + d][:, :], vx[:, m, (2 * h + d) * P:(2 * h + d + 1) * P], pxT[:, h % 2, m, :],
                                      start=(m == 0), stop=(m == MT - 1))
                    i.then_inc(s_pv, 1)
            linear("xo")
            stats("ln3", phases["xo"])
            ffn("f2", "ln4")
            stats("rms1")
            linear("in2")
            for j in range(5):
                x = in2_dst(j)
                pe.wait_ge(s_hsq, j + 1)
                pe.matmul(bank[4][:, :], mats[:, C_HEAD, :], r1[:, 0, :], start=True, stop=True).then_inc(s_hss, 1)
                pe.wait_ge(s_hn, j + 1)
                pe.matmul(bank[5][:, :], mats[:, C_ROT, :], x, start=True, stop=True).then_inc(s_hrot, 1)
            pe.wait_ge(s_hr, 5)
            for g in range(2):
                pe.matmul(bank[6 + g][:, :], mats[:, C_DUP0 + g, :], skv[:, 0, :], start=True, stop=True).then_inc(s_dup, 1)
            four(bank[4], skv[:, 1, :], s_svT)
            pe.wait_ge(s_dupc, 3)
            for n, g in enumerate(POOL_ORDER):
                pe.wait_ge(s_pool, n + 1)
                if n >= 2:
                    pe.wait_ge(s_py, n - 1)
                pe.matmul(bank[4 + n % 2][:, :], poolw[:, g, :], su[:, n, 8:8 + T], start=True, stop=True).then_inc(s_pmm, 1)

            def self_scores(h):
                p0 = HD * (h % 2)
                for t in range(TT):
                    n = TT * h + t
                    if n >= 3:
                        pe.wait_ge(s_pe, TT * XH + n - 2)
                    pe.matmul(bank[n % 3][:, :], sq[p0:p0 + HD, h // 2, t * P:(t + 1) * P], kk[p0:p0 + HD, h // 4, :],
                              start=True, stop=True).then_inc(s_sc, 1)

            pe.wait_ge(s_py, 4)
            self_scores(0)
            for h in range(QH):
                if h + 1 < QH:
                    self_scores(h + 1)
                p0 = HD * (h % 2)
                pe.wait_ge(s_pn, TT * XH + TT * (h + 1))
                for st in range(TT):
                    n = TT * h + st
                    if n >= 3:
                        m = n - 3
                        if m % 2:
                            pe.wait_ge(s_pca, XH + m // 2 + 1)
                        else:
                            pe.wait_ge(s_pcd, XH + m // 2 + 1)
                    for t in range(TT):
                        i = pe.transpose(bank[3 + n % 3][:, t * P:(t + 1) * P], ps[:, h % 2, t, st * P:(st + 1) * P], ident)
                    i.then_inc(s_pT, 1)
                pe.wait_ge(s_pcd, XH + 2 * (h + 1))
                pe.wait_ge(s_pca, XH + 2 * (h + 1))
                if h >= 4 and h % 2 == 0:
                    pe.wait_ge(*operand("out2", 4 + h // 2 - 2))
                for st in range(TT):
                    i = pe.matmul(bank[6 + (h // 2) % 2][p0:p0 + HD, :], sv[:, st, HD * (h // 4):HD * (h // 4) + HD],
                                  psT[:, h % 2, st, :], start=(st == 0), stop=(st == TT - 1))
                i.then_inc(s_pv, 1)
            linear("out2", order=[4 + g for g in POOL_ORDER] + list(range(4)))
            stats("rms2")
            ffn("f3", None)


def kernel(**inputs):
    import concourse.bacc as bacc
    from concourse.bass_utils import run_bass_kernel_spmd as run

    nc = bacc.Bacc("TRN2", target_bir_lowering=False, num_devices=1)
    arrays = {name: np.ascontiguousarray(a) for name, a in inputs.items()}
    arrays.update(shape_constants())
    aps = {}
    arrays = {f"in_{name}": a for name, a in arrays.items()}
    for name, a in arrays.items():
        aps[name[3:]] = nc.dram_tensor(name, a.shape, mybir.dt.from_np(a.dtype), kind="ExternalInput").ap()
    out = nc.dram_tensor("out_dram", (1, T, D), F32, kind="ExternalOutput").ap()
    build(nc, aps, out)
    return run(nc, [arrays], core_ids=[0]).results[0]["out_dram"]
```

```python
from contextlib import ExitStack

import numpy as np

import concourse.bass as bass
from concourse import mybir

F32 = mybir.dt.float32
F32R = mybir.dt.float32r
I32 = mybir.dt.int32
ACT = mybir.ActivationFunctionType
ALU = mybir.AluOpType
AX = mybir.AxisListType

P = 128
T = 512
D = 1024
KD = D // P
TT = T // P
F = 2816
MEM = 256
MT = MEM // P
HG = 4
SG = 4
XH = 4
QH = 8
HD = 64
GRID_W = 64
ALPHA = 2.0 ** 0.25
LN_EPS = 1e-5
RMS_EPS = 1e-6
PARTS = (8, 8, 6)
assert sum(PARTS) * P == F
RAW = 4
SPLIT = 4
AHEAD = 3
MVAL = 4
MEM_AT = 5
LEVELS = (6, 5, 4, 3, 2, 1, 0)

V_LN1G, V_LN1B, V_LN2G, V_LN2B, V_MEMG, V_MEMB, V_LN3G, V_LN3B, V_LN4G, V_LN4B, V_N1, V_N2 = range(0, 96, 8)
V_POOLB, V_POOLS, V_HGN, V_LB, V_QN, V_KN, V_ROWS = 96, 100, 104, 105, 113, 114, 115

C_ID, C_MEAN, C_M128, C_HEAD, C_ROT, C_DUP0, C_DUP1, C_N = range(8)


def shape_constants():
    i = np.arange(P)
    mats = np.zeros((C_N, P, P), np.float32)
    mats[C_ID] = np.eye(P)
    mats[C_MEAN] = 1.0 / D
    mats[C_M128] = 1.0 / P
    mats[C_HEAD] = (i[:, None] // HD == i[None, :] // HD) / HD
    q = HD // 4
    for d in range(P):
        if (d // q) % 2 == 0:
            mats[C_ROT, d + q, d] = -1.0
        else:
            mats[C_ROT, d - q, d] = 1.0
    for g in range(2):
        for d in range(P):
            mats[C_DUP0 + g, g * HD + d % HD, d] = 1.0
    masks = np.zeros((len(LEVELS) + 2, P, P), np.int32)
    s, t = i[:, None], i[None, :]
    for n, lv in enumerate(LEVELS):
        masks[n] = (s >> (lv + 1) == t >> (lv + 1)) & (s >> lv & 1 == 0) & (t >> lv & 1 == 1)
        masks[n, :, :P // 2] = masks[n][:, (i >> lv & 1) == 1]
        masks[n, :, P // 2:] = 0
    masks[len(LEVELS)] = s == t
    masks[len(LEVELS) + 1] = s <= t
    freq = (np.float32(10000.0) ** (-np.arange(q, dtype=np.float32) / np.float32(q))).astype(np.float32)
    tok = np.arange(T)
    row, col = (tok // GRID_W).astype(np.float32), (tok % GRID_W).astype(np.float32)
    ang = np.zeros((P, T), np.float32)
    for d in range(P):
        ang[d] = (row if (d % HD) < HD // 2 else col) * freq[d % q]
    rope = np.stack([np.cos(ang), np.sin(ang)]).astype(np.float32)
    restart = np.ones((1, T), np.float32)
    restart[0, ::P] = 0.0
    rcnt = np.zeros((4, T), np.float32)
    for g in range(4):
        w = 2 << g
        rcnt[g] = 1.0 / (np.clip(tok - w // 2 + w, 0, T) - np.clip(tok - w // 2, 0, T))
    return {"c_mats": mats, "c_masks": masks, "c_rope": rope, "c_restart": restart, "c_rcnt": rcnt}


def build(nc, A, out):
    ctx = ExitStack()
    with ctx:
        def sem(name):
            return ctx.enter_context(nc.semaphore(name))

        top = [-(-nc.sbuf_base // 32) * 32]

        def sb(name, shape, dt=F32, at=None):
            size = int(np.prod(shape[1:])) * 4
            off = top[0] if at is None else at
            assert off + size <= nc.sbuf_usable_end, (name, off + size - nc.sbuf_usable_end)
            if at is None:
                top[0] += -(-size // 32) * 32
            return nc.alloc_sbuf_tensor_at(name, list(shape), dt, offset=off)

        bank = [ctx.enter_context(nc.psum_tensor(f"bank{i}", [P, T], F32)) for i in range(8)]

        res = sb("res", [P, KD, T])
        ahi = sb("ahi", [P, KD, T], F32R)
        alo = sb("alo", [P, KD, T], F32R)
        wraw = sb("wraw", [P, RAW, KD * P])
        whi = sb("whi", [P, SPLIT, KD * P], F32R)
        wlo = sb("wlo", [P, SPLIT, KD * P], F32R)
        mats = sb("mats", [P, C_N, P])
        masks = sb("masks", [P, len(LEVELS) + 2, P], I32)
        restart = sb("restart", [P, T])
        vecs = sb("vecs", [P, P])
        wT = sb("wT", [P, SG, P])
        small = sb("small", [P, 64])
        sgst = sb("sgst", [P, 4, 6])
        sgmv = sb("sgmv", [P, 4, 2])
        sgr = sb("sgr", [P, 4])
        mst = sb("mst", [P, 4, 6])
        mmv = sb("mmv", [P, 2, 2])
        mrs = sb("mrs", [P, 2])
        arena = top[0]
        ARENA = nc.sbuf_usable_end - arena

        def region(start):
            at = [arena + start]

            def take(name, shape, dt=F32):
                t = sb(name, shape, dt, at=at[0])
                at[0] += int(np.prod(shape[1:])) * 4
                return t
            return take

        KB = 1024
        take = region(0)
        gate = take("gate", [P, 2, T])
        hval = take("hval", [P, 2, T])
        rstd = take("rstd", [P, T])
        mean = take("mean", [P, T])
        sum1 = take("sum1", [P, T])
        sum2 = take("sum2", [P, T])
        square = gate
        var = hval
        WORK = 16 * KB
        take = region(WORK)
        hhi = take("hhi", [P, max(PARTS), T], F32R)
        hlo = take("hlo", [P, max(PARTS), T], F32R)
        take = region(WORK)
        xin = take("xin", [P, TT, D])
        take = region(WORK + 32 * KB)
        vrow = take("vrow", [P, P])
        wsin = take("wsin", [P, SG, P])
        take = region(WORK)
        mk = take("mk", [P, HG, T])
        mq = take("mq", [P, HG, T])
        mg = take("mg", [P, HG, T])
        mu = take("mu", [P, SG, T])
        mv = take("mv", [P, SG, T])
        cum = take("cum", [P, HG, T])
        vT = take("vT", [P, HG, TT, P])
        ivt = take("ivt", [P, 2, T])
        acc = take("acc", [P, 2, T])
        DEC = 3
        dec = take("dec", [P, DEC, T])
        qt = take("qt", [P, 2, T // 2])
        kt = take("kt", [P, 2, T])
        sgb = take("sgb", [P, 3, T])
        vn = cum
        take = region(0)
        eb = take("eb", [P, T])
        qe = take("qe", [P, T])
        kend = take("kend", [P, 3 * P])
        kendT = take("kendT", [P, 3 * P])
        state = take("state", [P, 3, P])
        osq = take("osq", [P, T])
        ors = take("ors", [P, T])
        take = region(WORK)
        memin = take("memin", [P, MT, D])
        mhi = take("mhi", [P, KD, MEM], F32R)
        mlo = take("mlo", [P, KD, MEM], F32R)
        mval = take("mval", [P, MVAL, MEM])
        kx = take("kx", [P, KD, MEM])
        vx = take("vx", [P, MT, D])
        vxt = take("vxt", [P, 2, MEM])
        take = region(WORK + 48 * KB)
        qx = take("qx", [P, KD, T])
        take = region(WORK)
        px = take("px", [P, 2, TT, MEM])
        pxT = take("pxT", [P, 2, MT, T])
        take = region(WORK)
        sst = take("sst", [P, QH, T], F32R)
        skv = take("skv", [P, 2, T])
        su = take("su", [P, 4, T + 16])
        khi = take("khi", [P, 2, T], F32R)
        klo = take("klo", [P, 2, T], F32R)
        sv = take("sv", [P, TT, P])
        ps = take("ps", [P, 2, TT, T])
        psT = take("psT", [P, 2, TT, T])
        sq = psT[:, 0, :, :]
        rope = take("rope", [P, 2, T])
        poolw = take("poolw", [P, 4, P])
        rcnt = take("rcnt", [P, 2, T])
        po = rope
        take = region(0)
        r1 = take("r1", [P, 2, T])
        r2 = take("r2", [P, 2, T])
        r3 = take("r3", [P, T])
        pa = take("pa", [P, T + 16])
        pb = take("pb", [P, T + 16])
        take = region(WORK + 32 * KB)
        ob = take("ob", [P, 2, TT, P])
        assert ARENA >= WORK + 82 * KB, ARENA

        ident = mats[:, C_ID, :]

        def vcol(row):
            return vecs[:, row:row + 1]

        S_LB, S_OML, S_E0, S_E1, S_EPS5, S_EPS6, S_NM, S_SM, S_RI = 0, 4, 8, 12, 16, 17, 20, 28, 36

        class Phase:
            def __init__(self, name, kind, base, K, n, src):
                self.name, self.kind, self.base, self.K, self.n, self.src = name, kind, base, K, n, src

        phases, blocks = {}, []

        def add(name, kind, K, n, src):
            ph = Phase(name, kind, len(blocks), K, n, src)
            phases[name] = ph
            blocks.extend((ph, j) for j in range(n))

        def cols(w, k0, K, col):
            return w.rearrange("(k p) f -> p k f", p=P)[:, k0:k0 + K, bass.ds(col * P, P)]

        def add_ffn(name, wg, wu, wd):
            t0 = 0
            for part, n in enumerate(PARTS):
                def up(tile, odd, t0=t0):
                    return cols(wu if odd else wg, 0, KD, tile + t0)
                add(f"{name}_up{part}", "up", KD, 2 * n, up)
                add(f"{name}_down{part}", "down", n, KD, lambda j, t0=t0, n=n: cols(wd, t0, n, j))
                t0 += n

        POOL_ORDER = (3, 2, 1, 0)
        IN2_ORDER = [4, 0, 1, 2, 3, 5] + [6 + g for g in POOL_ORDER]
        add_ffn("f1", A["ffn1_w_gate"][0], A["ffn1_w_up"][0], A["ffn1_w_down"][0])
        add("in", "lin", KD, 24, lambda j: cols(A["w_in"][0], 0, KD, IN_ORDER[j]))
        add("out", "lin", KD, KD, lambda j: cols(A["w_out"][0], 0, KD, j))
        add("mk", "lin", KD, KD, lambda j: cols(A["xa_w_k"][0], 0, KD, j))
        add("mv", "lin", KD, KD, lambda j: cols(A["xa_w_v"][0], 0, KD, j))
        add("xq", "lin", KD, KD, lambda j: cols(A["xa_w_q"][0], 0, KD, j))
        add("xo", "lin", KD, KD, lambda j: cols(A["xa_w_o"][0], 0, KD, j))
        add_ffn("f2", A["ffn2_w_gate"][0], A["ffn2_w_up"][0], A["ffn2_w_down"][0])
        add("in2", "lin", KD, 10, lambda j: cols(A["w_in_2"][0], 0, KD, IN2_ORDER[j]))
        add("out2", "lin", KD, KD, lambda j: cols(A["w_out_2"][0], 0, KD, j))
        add_ffn("f3", A["w_gate_2"][0], A["w_up_2"][0], A["w_down_2"][0])
        TILE0 = {"f1": 0, "f2": F // P, "f3": 2 * (F // P)}

        def part_tile0(name):
            return TILE0[name[:2]] + sum(PARTS[:int(name[-1])])

        raw_ready = [sem(f"raw_ready{i}") for i in range(RAW)]
        hi_ready = sem("hi_ready")
        lo_ready = [sem(f"lo_ready{i}") for i in range(2)]
        block_done = sem("block_done")
        bank_free = sem("bank_free")
        gate_done = sem("gate_done")
        value_done = sem("value_done")
        hidden_ready = sem("hidden_ready")
        act_dve = sem("operand_tile_by_dve")
        act_pool = sem("operand_tile_by_pool")
        square_done = sem("square_done")
        sums_done = sem("sums_done")
        stat_mean = sem("stat_mean")
        stat_sq = sem("stat_sq")
        rms1_sum = sem("rms1_squares_added")
        mean_sq = sem("mean_squared")
        var_ready = sem("var_ready")
        rstd_ready = sem("rstd_ready")
        mean_ready = sem("mean_ready")
        s_mid = sem("centred_by_pool")
        scaled = sem("scaled")
        normed = sem("normed")
        hi_act = sem("hi_act")
        dve_chain = sem("dve_chain")
        act_chain = sem("act_chain")
        pool_chain = sem("pool_chain")

        def linker(eng, s):
            n = [0]

            def link(ins):
                n[0] += 1
                ins.then_inc(s, 1)
                eng.wait_ge(s, n[0])
            return link

        def slot_of(ph, jj, n):
            return (ph.base + jj) % n

        def each_block(eng, ph, step):
            loops = (ph.n - 4) // 4
            done = 0
            if loops >= 2:
                with eng.Fori(0, loops) as i:
                    for jj in range(4):
                        step(i, jj)
                done = 4 * loops
            for j in range(done, ph.n):
                step(0, j)

        def load_block(eng, ph, i, jj):
            eng.wait_ge(lo_ready[slot_of(ph, jj, 2)], (ph.base + jj) // 2 + 1 + 2 * i)
            src = ph.src(2 * i + jj // 2, jj % 2) if ph.kind == "up" else ph.src(jj)
            slot = slot_of(ph, jj, RAW)
            dst = wraw[:, slot, 0:ph.K * P].rearrange("p (k f) -> p k f", f=P)
            eng.dma_start(dst, src).then_inc(raw_ready[slot], 16)

        def split_hi(eng, ph, i, jj):
            b = ph.base + jj + 4 * i
            n = ph.K * P
            slot, raw = slot_of(ph, jj, SPLIT), slot_of(ph, jj, RAW)
            eng.wait_ge(raw_ready[raw], 16 * ((ph.base + jj) // RAW + 1) + 16 * i)
            eng.wait_ge(block_done, b + 1)
            eng.copy(whi[:, slot, 0:n], wraw[:, raw, 0:n]).then_inc(hi_ready, 1)

        def split_lo(eng, ph, i, jj):
            b = ph.base + jj + 4 * i
            n = ph.K * P
            slot, raw = slot_of(ph, jj, SPLIT), slot_of(ph, jj, RAW)
            even_odd = lo_ready[slot_of(ph, jj, 2)]
            if isinstance(i, int) and b >= 2 and lo_owner(b) != lo_owner(b - 2):
                eng.wait_ge(even_odd, RAW // 2 + b // 2)
            eng.wait_ge(hi_ready, b + 1)
            eng.tensor_tensor(wlo[:, slot, 0:n], wraw[:, raw, 0:n], whi[:, slot, 0:n],
                              ALU.subtract).then_inc(even_odd, 1)

        def wait_lo(eng, ph, i, jj):
            eng.wait_ge(lo_ready[slot_of(ph, jj, 2)], RAW // 2 + (ph.base + jj) // 2 + 1 + 2 * i)

        def lo_owner(b):
            return DVE if b == 1 or (b % 2 and blocks[b][0].name in DVE_SPLITS) else POOL

        def ahead(split, eng, ph, i, jj, owner=None):
            if isinstance(i, int):
                b = ph.base + jj + AHEAD
                if b < len(blocks) and (owner is None or lo_owner(b) == owner):
                    split(eng, blocks[b][0], 0, blocks[b][1])
            elif owner != DVE:
                split(eng, ph, i, jj + AHEAD)

        def multiply(eng, ph, i, jj, xhi, xlo, width=T, ready=None):
            b = ph.base + jj + 4 * i
            slot = slot_of(ph, jj, SPLIT)
            o = bank[slot_of(ph, jj, RAW)][:, 0:width]
            eng.wait_ge(hi_ready, b + 1)
            eng.wait_ge(bank_free, b + 1)
            for k in range(ph.K):
                if ready is not None:
                    eng.wait_ge(*ready(k))
                w = whi[:, slot, k * P:(k + 1) * P]
                eng.matmul(o, w, xhi[:, k, :], start=(k == 0), stop=False)
                eng.matmul(o, w, xlo[:, k, :], start=False, stop=False)
            wait_lo(eng, ph, i, jj)
            for k in range(ph.K):
                mm = eng.matmul(o, wlo[:, slot, k * P:(k + 1) * P], xhi[:, k, :],
                                start=False, stop=(k == ph.K - 1))
            mm.then_inc(block_done, 1)

        def multiply_two(eng, ph, xhi, xlo, width, ready, before=None, order=None):
            eng.wait_ge(hi_ready, ph.base + 2)
            eng.wait_ge(bank_free, ph.base + 2)
            for j in range(2):
                wait_lo(eng, ph, 0, j)
            for n, k in enumerate(order or range(ph.K)):
                if before:
                    before(n)
                hi = HI_OF.get(ph.name.split("_")[0])
                if ph.base == 0:
                    eng.wait_ge(s_xhi, n + 1)
                elif hi is None:
                    eng.wait_ge(*ready(n))
                else:
                    eng.wait_ge(hi_act, hi + n + 1)
                for j in range(2):
                    slot = slot_of(ph, j, SPLIT)
                    o = bank[slot_of(ph, j, RAW)][:, 0:width]
                    eng.matmul(o, whi[:, slot, k * P:(k + 1) * P], xhi[:, k, :], start=(n == 0), stop=False)
                    eng.matmul(o, wlo[:, slot, k * P:(k + 1) * P], xhi[:, k, :], start=False, stop=False)
                eng.wait_ge(*ready(n))
                for j in range(2):
                    slot = slot_of(ph, j, SPLIT)
                    o = bank[slot_of(ph, j, RAW)][:, 0:width]
                    mm = eng.matmul(o, whi[:, slot, k * P:(k + 1) * P], xlo[:, k, :], start=False, stop=(n == ph.K - 1))
                    if n == ph.K - 1:
                        mm.then_inc(block_done, 1)

        def bank_of(ph, jj):
            return bank[slot_of(ph, jj, RAW)]

        def wait_block(eng, ph, i, jj):
            eng.wait_ge(block_done, SPLIT + ph.base + jj + 4 * i + 1)

        DVE_SPLITS = ("out", "mk", "mv", "xq", "xo", "in2", "out2")

        NORMS = {"ln1": (0, True, V_LN1G, V_LN1B), "ln2": (1, True, V_LN2G, V_LN2B),
                 "ln3": (2, True, V_LN3G, V_LN3B), "ln4": (3, True, V_LN4G, V_LN4B),
                 "rms1": (4, False, V_N1, None), "rms2": (5, False, V_N2, None)}
        POOL, DVE = 0, 1
        MAKERS = {"f1": [DVE] * KD, "in": [DVE] + [POOL] * (KD - 1), "out": [DVE, POOL] * (KD // 2), "xq": [DVE] * KD, "xo": [DVE] * KD,
                  "f2": [DVE] + [POOL] * (KD - 1), "in2": [DVE, POOL] * (KD // 2), "out2": [DVE] * KD, "f3": [DVE, POOL] * (KD // 2)}
        OPERAND = {"ln1": "in", "ln2": "xq", "ln3": "f2", "rms1": "in2", "rms2": "f3"}

        def operand(layer, k):
            n = [0, 0]
            for name, makers in MAKERS.items():
                for i, m in enumerate(makers):
                    n[m] += 1
                    if name == layer and i == k:
                        return (act_pool, act_dve)[m], n[m]

        def by(layer, k):
            return MAKERS[layer][k]

        HI0 = {"ln1": 0, "ln2": 16, "ln3": 24, "rms1": 32, "rms2": 40}
        HI_OF = {"in": 0, "out": 8, "xq": 16, "f2": 24, "in2": 32, "f3": 40}
        SUM_STEPS = KD - 2

        def steps_before(norm):
            idx = NORMS[norm][0]
            return SUM_STEPS * (idx - (idx > NORMS["rms1"][0]))
        POOL_SUB = (2, 4, 6)

        s_ident = sem("identity_loaded")
        s_x = [sem(f"x_loaded{i}") for i in range(4)]
        s_mem, s_const, s_vec, s_ws, s_rows = (sem(n) for n in
                                                    ("mem_loaded", "consts_loaded", "vectors_loaded",
                                                     "spatial_loaded", "rows_loaded"))
        s_xT = sem("x_transposed")
        s_xhi = sem("x_hi")
        s_vT0 = sem("vectors_transposed")
        s_vecs = sem("vectors_ready")
        s_lbe = sem("bound_exps")
        s_wsT = sem("spatial_transposed")
        s_wTz = sem("spatial_zeroed")
        s_wTr = sem("spatial_ready")
        s_out = sem("out_stored")
        s_oT = sem("out_transposed")
        s_ob = sem("out_copied")

        s_sig = sem("gates_sigmoid")
        s_fg = sem("forget_ready")
        s_lf = sem("log_forget")
        s_cum = sem("cum_ready")
        s_ivT = sem("values_transposed")
        s_ivc = sem("values_copied")
        s_arg = sem("decay_args")
        s_dexp = sem("decays")
        s_qk = sem("scaled_qk")
        s_smm = sem("score_products")
        s_put = sem("scores_put")
        s_az = sem("scores_zeroed")
        s_ebd = sem("exp_cum")
        s_kd = sem("key_decay_args")
        s_kde = sem("key_decays")
        s_ke = sem("end_keys")
        s_keT = sem("end_keys_transposed")
        s_kec = sem("end_keys_copied")
        s_um = sem("state_products")
        s_st = sem("states_ready")
        s_om = sem("outputs_product")
        s_osq = sem("outputs_squared")
        s_oss = sem("outputs_square_sum")
        s_ors = sem("outputs_rstd")
        s_on = sem("outputs_normed")
        s_act2 = sem("gates_activated")
        s_prod = sem("gated")
        s_gv = sem("gelu_done")
        s_gvT = sem("gelu_transposed")
        s_sgv = sem("spatial_var")
        s_sgr = sem("spatial_rstd")
        s_vn = sem("spatial_normed")
        s_sm = sem("spatial_products")
        s_so = sem("spatial_biased")
        s_mul = sem("spatial_gated")
        s_mv = sem("mem_var")
        s_mr = sem("mem_rstd")
        s_mn = sem("mem_normed")
        s_mT = sem("mem_transposed")
        s_ma = sem("mem_affine")
        s_mh = sem("mem_hi")
        s_ml = sem("mem_lo")
        s_vxT = sem("mem_values_transposed")
        s_kv = sem("mem_kv_copied")
        s_sc = sem("scores")
        s_nm = sem("score_maxima")
        s_pe = sem("probabilities")
        s_pn = sem("probabilities_normed")
        s_pT = sem("probabilities_transposed")
        s_pcd = sem("probabilities_copied_dve")
        s_pca = sem("probabilities_copied_act")
        s_pv = sem("attended")
        s_ah = sem("attended_hi")
        s_rope = sem("rope_loaded")
        s_hsq = sem("head_squares")
        s_hss = sem("head_square_sums")
        s_hrs = sem("head_rstd")
        s_hn = sem("head_normed")
        s_hrot = sem("head_rotated")
        s_hr = sem("head_roped")
        s_sth = sem("queries_hi_stacked")
        s_stl = sem("queries_lo_stacked")
        s_kh = sem("keys_hi")
        s_dup = sem("keys_doubled")
        s_dupc = sem("keys_copied")
        s_svT = sem("self_values_transposed")
        s_pool = sem("pooled")
        s_rcn = [sem(f"counts_loaded{i}") for i in range(2)]
        s_pmm = sem("pool_products")
        s_py = sem("pool_out")
        s_pyh = sem("pool_out_hi")

        STEPS = [(h, n) for h in range(HG) for n in range(len(LEVELS) + 1)]
        SCALED = [s for s, (h, n) in enumerate(STEPS) if n < len(LEVELS)]
        NTH = {s: e for e, s in enumerate(SCALED)}
        Q0, FZ0, IV0, G0, U0, V0 = range(0, 24, 4)
        IN_ORDER = ([FZ0 + h for h in range(HG)] + [Q0, IV0, Q0 + 1, IV0 + 1, V0, V0 + 1, V0 + 2, Q0 + 2, IV0 + 2,
                                                    Q0 + 3, IV0 + 3, V0 + 3]
                    + [U0 + g for g in range(SG)] + [G0 + h for h in range(HG)])
        at_block = {c: n for n, c in enumerate(IN_ORDER)}
        plan = [[] for _ in range(24)]
        for h in range(HG):
            plan[1 + h] += [("forget", h)]
        plan[4] += [("logs", 0)]
        for h in range(HG):
            g0 = 5 + 4 * h
            if h >= 1:
                plan[g0 + 1] += [("take_values", h)]
        for h in range(HG):
            g0 = 5 + 4 * h
            for n in range(len(LEVELS) + 1):
                s = (len(LEVELS) + 1) * h + n
                plan[g0 + n // 2 + 1] += [("put", s)]
            plan[g0 + 4] += [("outputs", h)]
            plan[g0 + 5] += [("power", h)]
            plan[g0 + 6] += [("normed", h)]
            for n in range(len(LEVELS) + 1):
                plan[g0 + n // 2] += [("level", (len(LEVELS) + 1) * h + n)]
            plan[g0 + 2] += [("ends", h)]
            plan[g0 + 3] += [("update", h)]
            plan[g0 if h else g0 + 1] += [("values", h)]
            if h == 0:
                plan[g0 + 2] += [("take_values", h)]
        plan[11] += [("gelu", 0), ("gelu", 1), ("gelu", 2)]
        for g, (at, b) in enumerate(((11, 6), (15, 6), (19, 6), (21, 4))):
            if g == SG - 1:
                plan[at] += [("gelu", n) for n in range(3, 8)]
            plan[at] += [("turn", g)]
            plan[at + 1] += [("centre", g)]
            plan[at + 2].insert(0, ("mix", g))
            plan[at + 2] += [("bias", g)]
            for n in [n for n, (kind, h) in enumerate(plan[at + 2]) if kind == "outputs"]:
                plan[at + 2].append(plan[at + 2].pop(n))
        plan[22] += [("spatial", g) for g in range(3)]
        plan[23] = ([t for t in plan[23] if t[0] != "bias"] + [("silu", h) for h in range(3)]
                    + [("gate", h) for h in range(3)])
        SPATIAL_BANK = (6, 6, 6, 4)
        DST = {Q0: mq, FZ0: mk, G0: mg, U0: mu, V0: mv}
        IN_DST = [ivt[:, c % 2, :] if c // 4 * 4 == IV0 else DST[c // 4 * 4][:, c % 4, :] for c in IN_ORDER]
        OUT_TILES = [4, 5, 6, 0, 1, 2, 7, 3]

        def wait_in(eng, j):
            eng.wait_ge(bank_free, RAW + phases["in"].base + at_block[j] + 1)

        def mixed(k):
            return mq[:, k, :] if k < HG else mu[:, k - HG, :]

        def wait_mixed(eng, k):
            if k < HG:
                eng.wait_ge(s_prod, k + 1)
            else:
                eng.wait_ge(s_mul, k - HG + 1)

        def halves(t, lv):
            return t.rearrange("p (n two c) -> p n two c", two=2, c=1 << lv)

        def in2_dst(j):
            return skv[:, 0, :] if j == 0 else sq[:, j - 1, :] if j < 5 else skv[:, 1, :] if j == 5 else su[:, j - 6, 8:8 + T]

        plan2 = [[] for _ in range(10)]
        for j in range(5):
            plan2[j + 3].insert(0, ("rope", j))
            plan2[j + 2].append(("rstd", j))
            plan2[j + 1].append(("square", j))
        for j in range(1, 5):
            plan2[j + 4].append(("stack", j))
        plan2[6] += [("turn_v", 0)]
        plan2[7] += [("take_v", 0), ("double", 0)]
        plan2[8] += [("take_k", 0)]
        POOL_AT = 2
        OUT2_TILES = [0, 7, 1, 6, 5, 2, 4, 3]

        def last_block_in(ph, b):
            return max(j for j in range(ph.n) if slot_of(ph, j, RAW) == b)

        block = ctx.enter_context(nc.Block())

        @block.sync
        def _(sp):
            def vec_rows(row, ap, n):
                sp.dma_start(vrow[row:row + n, :], ap).then_inc(s_vec, 16)

            sp.dma_start(mats[:, C_ID, :], A["c_mats"][C_ID]).then_inc(s_ident, 16)
            xv = A["x"][0].rearrange("(n p) d -> p n d", p=P)
            for j in range(2):
                load_block(sp, phases["f1_up0"], 0, j)
            for part in range(4):
                at = slice(part * D // 4, (part + 1) * D // 4)
                sp.dma_start(xin[:, :, at], xv[:, :, at]).then_inc(s_x[part], 16)
            for j in range(2, RAW):
                load_block(sp, phases["f1_up0"], 0, j)
            sp.dma_start(mats[:, 1:C_N, :], A["c_mats"][1:C_N].rearrange("n p f -> p n f")).then_inc(s_const, 16)
            for row, name in ((V_LN1G, "ln1_g"), (V_LN1B, "ln1_b"), (V_LN2G, "ln2_g"), (V_LN2B, "ln2_b"),
                              (V_MEMG, "mem_ln_g"), (V_MEMB, "mem_ln_b"), (V_LN3G, "ln3_g"), (V_LN3B, "ln3_b"),
                              (V_LN4G, "ln4_g"), (V_LN4B, "ln4_b"), (V_N1, "norm1_g_2"), (V_N2, "norm2_g_2")):
                vec_rows(row, A[name].rearrange("o (k p) -> (o k) p", p=P), KD)
            vec_rows(V_POOLB, A["pool_b_2"][0], 4)
            vec_rows(V_POOLS, A["pool_scale_2"].rearrange("o (k p) -> (o k) p", p=P), 4)
            vec_rows(V_HGN, A["hg_norm_g"], 1)
            vec_rows(V_LB, A["hg_lb_logits"].rearrange("l h d -> (l h) d"), 8)
            for row, name in ((V_QN, "q_norm_g_2"), (V_KN, "k_norm_g_2")):
                for half in range(2):
                    sp.dma_start(vrow[row:row + 1, half * HD:(half + 1) * HD], A[name]).then_inc(s_vec, 16)
            sp.dma_start(masks[:, :, :], A["c_masks"].rearrange("n p f -> p n f")).then_inc(s_const, 16)
            sp.dma_start(restart[:, :], A["c_restart"].broadcast_to([P, T])).then_inc(s_const, 16)
            sp.dma_start(wsin[:, :, :], A["sg_w_s"][0].rearrange("g t s -> t g s")).then_inc(s_ws, 16)

            def stream(name):
                ph = phases[name]
                if ph.kind == "up":
                    with sp.Fori(1 if ph.base == 0 else 0, ph.n // 4) as i:
                        for jj in range(4):
                            load_block(sp, ph, i, jj)
                    return
                for j in range(ph.n):
                    load_block(sp, ph, 0, j)

            def ffn(name, once=None):
                for part in range(len(PARTS)):
                    stream(f"{name}_up{part}")
                    if once and part == 0:
                        once()
                    stream(f"{name}_down{part}")

            ffn("f1")
            for j in range(4):
                load_block(sp, phases["in"], 0, j)
            wait_block(sp, phases["in"], 0, 0)
            for n, ap in enumerate((A["sg_ln_g"].rearrange("o g c -> o (g c)"), A["sg_ln_b"].rearrange("o g c -> o (g c)"),
                                    A["sg_b_s"].rearrange("o g c -> o (g c)"))):
                sp.dma_start(sgb[:, n, :], ap.broadcast_to([P, T])).then_inc(s_rows, 16)
            for j in range(4, 24):
                load_block(sp, phases["in"], 0, j)
            for j in range(4):
                load_block(sp, phases["out"], 0, j)
            sp.wait_ge(*operand("out", KD - 1))
            sp.dma_start(memin[:, :, :], A["mem"][0].rearrange("(n p) d -> p n d", p=P)).then_inc(s_mem, 16)
            for j in range(4, KD):
                load_block(sp, phases["out"], 0, j)
            for name in ("mk", "mv", "xq", "xo"):
                stream(name)
            def tables():
                wait_block(sp, phases["xo"], 0, KD - 1)
                sp.dma_start(rope[:, :, :], A["c_rope"].rearrange("n p t -> p n t")).then_inc(s_rope, 16)
                sp.dma_start(poolw[:, :, :], A["pool_w_2"][0].rearrange("g c d -> c g d")).then_inc(s_rope, 16)
                for n in range(2):
                    load_counts(n)

            def load_counts(n):
                if n >= 2:
                    sp.wait_ge(s_pool, n - 1)
                sp.dma_start(rcnt[:, n % 2, :],
                             A["c_rcnt"][POOL_ORDER[n]:POOL_ORDER[n] + 1, :].broadcast_to([P, T])).then_inc(s_rcn[n % 2], 16)

            ffn("f2", tables)
            stream("in2")
            for j in range(4):
                load_block(sp, phases["out2"], 0, j)
            for n in range(2, 4):
                load_counts(n)
            for j in range(4, KD):
                load_block(sp, phases["out2"], 0, j)
            ffn("f3")
            for j in range(KD):
                sp.wait_ge(s_ob, j + 1)
                sp.dma_start(out[0].rearrange("(n p) d -> p n d", p=P)[:, :, j * P:(j + 1) * P],
                             ob[:, j % 2, :, :]).then_inc(s_out, 16)
                sp.wait_ge(s_out, 16 * (j + 1))

        @block.scalar
        def _(act):
            link = linker(act, act_chain)

            def hi_stream(ph, i, jj):
                ahead(split_hi, act, ph, i, jj)

            def silu_gate(ph, i, jj, t0):
                tile = t0 + 2 * i + jj // 2
                wait_block(act, ph, i, jj)
                act.wait_ge(value_done, tile + 1)
                act.activation(gate[:, (t0 + jj // 2) % 2, :], bank_of(ph, jj)[:, :], ACT.Silu).then_inc(gate_done, 1)

            def square_res(norm, j, ph=None):
                n = 8 * NORMS[norm][0] + j
                if ph:
                    act.wait_ge(bank_free, RAW + ph.base + j + 1)
                else:
                    act.wait_ge(normed, n - 8 + 1)
                if norm == "rms1" and j >= 2:
                    act.wait_ge(rms1_sum, j - 1)
                elif j >= 2:
                    act.wait_ge(sums_done, steps_before(norm) + max(1, j - 2))
                act.activation(square[:, j % 2, :], res[:, j, :], ACT.Square).then_inc(square_done, 1)

            def use_logs():
                act.preload_act_table_set("natural_log_exp_and_others")

            def norm_tail(norm, between=None):
                idx, centred, grow, brow = NORMS[norm]
                if centred:
                    act.wait_ge(stat_mean, idx + 1)
                    act.activation(var[:, 0, :], bank[4][:, :], ACT.Square).then_inc(mean_sq, 1)
                    act.wait_ge(var_ready, idx + 1)
                else:
                    act.wait_ge(stat_sq, idx + 1)
                eps = S_EPS5 if centred else S_EPS6
                src = var[:, 1, :] if centred else bank[5][:, :]
                link(act.activation(rstd[:, :], src, ACT.Ln, bias=small[:, eps:eps + 1]))
                act.activation(rstd[:, :], rstd[:, :], ACT.Exp, scale=-0.5).then_inc(rstd_ready, 1)
                for k in range(KD):
                    act.wait_ge(scaled, 8 * idx + k + 1)
                    if centred:
                        g, b = vcol(grow + k), vcol(brow + k)
                        if norm in OPERAND:
                            act.activation(ahi[:, k, :], res[:, k, :], ACT.Identity, bias=b, scale=g).then_inc(hi_act, 1)
                        act.activation(res[:, k, :], res[:, k, :], ACT.Identity, bias=b, scale=g).then_inc(normed, 1)
                        if norm == "ln4":
                            square_res("rms1", k)
                    else:
                        act.copy(ahi[:, k, :], hval[:, k % 2, :]).then_inc(hi_act, 1)
                    if between:
                        between(k)

            def ffn(name, norm, once=None):
                for part in range(len(PARTS)):
                    ph = phases[f"{name}_up{part}"]
                    t0 = part_tile0(ph.name)

                    def step(i, jj, ph=ph, t0=t0):
                        if jj % 2 == 0:
                            silu_gate(ph, i, jj, t0)
                        hi_stream(ph, i, jj)
                    each_block(act, ph, step)
                    if once and part == 0:
                        once()
                    ph = phases[f"{name}_down{part}"]
                    if norm and part == len(PARTS) - 1:
                        use_logs()
                    for j in range(KD):
                        hi_stream(ph, 0, j)
                        if norm and part == len(PARTS) - 1:
                            square_res(norm, j, ph)

            for b in range(2):
                split_hi(act, blocks[b][0], 0, blocks[b][1])
            for k in range(KD):
                act.wait_ge(s_xT, k + 1)
                act.copy(ahi[:, k, :], bank[4 + k % 4][:, :])
                act.copy(res[:, k, :], bank[4 + k % 4][:, :]).then_inc(s_xhi, 1)
                if k == 4:
                    split_hi(act, blocks[2][0], 0, blocks[2][1])

            def bound_exps():
                act.wait_ge(s_vecs, 2)
                act.activation(small[:, S_E0:S_E0 + 8], small[:, S_E0:S_E0 + 8], ACT.Exp).then_inc(s_lbe, 1)

            ffn("f1", "ln1", bound_exps)
            norm_tail("ln1")

            def mixer(kind, n):
                if kind == "forget":
                    wait_in(act, FZ0 + n)
                    link(act.activation(cum[:, n, :], mk[:, n, :], ACT.Sigmoid))
                    act.activation(mk[:, n, :], mk[:, n, :], ACT.Sigmoid, scale=-1.0).then_inc(s_sig, 1)
                elif kind == "logs":
                    for h in range(HG):
                        act.wait_ge(s_fg, h + 1)
                        act.activation(cum[:, h, :], cum[:, h, :], ACT.Ln).then_inc(s_lf, 1)
                elif kind == "level" and n in NTH:
                    e = NTH[n]
                    act.wait_ge(s_arg, e + 1)
                    act.activation(dec[:, e % DEC, :], dec[:, e % DEC, :], ACT.Exp).then_inc(s_dexp, 1)
                elif kind == "ends":
                    if n == 0:
                        act.wait_ge(s_cum, 1)
                    else:
                        act.wait_ge(s_on, n)
                    act.activation(eb[:, :], cum[:, n, :], ACT.Exp).then_inc(s_ebd, 1)
                    act.wait_ge(s_kd, n + 1)
                    act.activation(kend[:, :], kend[:, :], ACT.Exp).then_inc(s_kde, 1)
                elif kind == "power":
                    act.wait_ge(s_om, n + 1)
                    act.activation(osq[:, :], bank[6][:, :], ACT.Square).then_inc(s_osq, 1)
                elif kind == "normed":
                    act.wait_ge(s_oss, n + 1)
                    link(act.activation(ors[:, :], bank[7][:, :], ACT.Ln, bias=small[:, S_EPS5:S_EPS5 + 1]))
                    act.activation(ors[:, :], ors[:, :], ACT.Exp, scale=-0.5).then_inc(s_ors, 1)
                elif kind == "gelu":
                    wait_in(act, V0 + n if n < SG else U0 + n - SG)
                    x = mv[:, n, :] if n < SG else mu[:, n - SG, :]
                    act.activation(x, x, ACT.Gelu_apprx_tanh).then_inc(s_gv, 1)
                elif kind == "centre":
                    act.wait_ge(s_sgv, n + 1)
                    link(act.activation(sgr[:, :], sgmv[:, :, 1], ACT.Ln, bias=small[:, S_EPS5:S_EPS5 + 1]))
                    act.activation(sgr[:, :], sgr[:, :], ACT.Exp, scale=-0.5).then_inc(s_sgr, 1)
                elif kind == "silu":
                    wait_in(act, G0 + n)
                    act.activation(mg[:, n, :], mg[:, n, :], ACT.Silu).then_inc(s_act2, 1)

            for n, tasks in enumerate(plan):
                for task in tasks:
                    mixer(*task)
                hi_stream(phases["in"], 0, n)
            wait_block(act, phases["in"], 0, 23)
            for n, k in enumerate(OUT_TILES):
                if n == 4:
                    mixer("silu", 3)
                wait_mixed(act, k)
                act.copy(ahi[:, k, :], mixed(k)).then_inc(hi_act, 1)

            use_logs()
            for j in range(KD):
                hi_stream(phases["out"], 0, j)
                square_res("ln2", j, phases["out"])
                if j == MEM_AT:
                    act.wait_ge(s_mv, 1)
                    link(act.activation(mrs[:, :], mmv[:, :, 1], ACT.Ln, bias=small[:, S_EPS5:S_EPS5 + 1]))
                    act.activation(mrs[:, :], mrs[:, :], ACT.Exp, scale=-0.5).then_inc(s_mr, 1)
                if j == MEM_AT + 1:
                    for k in range(KD):
                        act.wait_ge(s_ma, k + 1)
                        act.copy(mhi[:, k, :], mval[:, k % MVAL, :]).then_inc(s_mh, 1)
            for j in range(3):
                hi_stream(phases["mk"], 0, j)
            norm_tail("ln2", lambda k: hi_stream(phases["mk"], 0, k + 3) if k + 3 < KD else None)
            for name in ("mv", "xq"):
                for j in range(KD):
                    hi_stream(phases[name], 0, j)
            def cross_exp(h):
                for t in range(TT):
                    act.wait_ge(s_nm, 2 * h + 2)
                    if t == 0 and h >= 2:
                        act.wait_ge(s_pT, 2 * (h - 1))
                    i = act.activation(px[:, h % 2, t, :], bank[2 * (h % 2) + t // 2][:, (t % 2) * MEM:(t % 2 + 1) * MEM],
                                       ACT.Exp, bias=small[:, S_NM + 4 * (h % 2) + t:S_NM + 4 * (h % 2) + t + 1],
                                       accum_out=small[:, S_SM + 4 * (h % 2) + t:S_SM + 4 * (h % 2) + t + 1])
                    i.then_inc(s_pe, 1)

            def attended_hi(h):
                for d in range(2):
                    act.wait_ge(s_pv, 2 * h + d + 1)
                    act.copy(ahi[:, 2 * h + d, :], bank[6 + d][:, :]).then_inc(s_ah, 1)

            cross_exp(0)
            for h in range(XH):
                if h >= 2:
                    attended_hi(h - 2)
                if h + 1 < XH:
                    cross_exp(h + 1)
                act.wait_ge(s_pT, 2 * h + 2)
                if h >= 2:
                    act.wait_ge(s_pv, 2 * (h - 1))
                act.copy(pxT[:, h % 2, 1, :], bank[5][:, :]).then_inc(s_pca, 1)
            attended_hi(XH - 2)
            attended_hi(XH - 1)
            for j in range(KD):
                hi_stream(phases["xo"], 0, j)
                square_res("ln3", j, phases["xo"])
            norm_tail("ln3")
            ffn("f2", "ln4")
            norm_tail("ln4")
            norm_tail("rms1")
            def prepare(kind, j):
                if kind == "square":
                    act.wait_ge(bank_free, RAW + phases["in2"].base + j + 1)
                    act.activation(r1[:, j % 2, :], in2_dst(j), ACT.Square).then_inc(s_hsq, 1)
                elif kind == "rstd":
                    act.wait_ge(s_hss, j + 1)
                    link(act.activation(r2[:, j % 2, :], bank[4 + j % 2][:, :], ACT.Ln, bias=small[:, S_EPS6:S_EPS6 + 1]))
                    act.activation(r2[:, j % 2, :], r2[:, j % 2, :], ACT.Exp, scale=-0.5).then_inc(s_hrs, 1)
                elif kind == "stack":
                    act.wait_ge(s_hr, j + 1)
                    for n in range(2):
                        own = slice(HD * n, HD * n + HD)
                        act.copy(sst[own, 2 * (j - 1) + n, :], in2_dst(j)[own, :]).then_inc(s_sth, 1)
                elif kind == "take_k":
                    for g in range(2):
                        act.wait_ge(s_dup, g + 1)
                        act.copy(khi[:, g, :], bank[(4, 7)[g]][:, :]).then_inc(s_kh, 1)

            for j, tasks in enumerate(plan2):
                for task in tasks:
                    prepare(*task)
                hi_stream(phases["in2"], 0, j)

            def self_exp(h, t):
                n = TT * h + t
                if h >= QH:
                    return
                act.wait_ge(s_nm, 2 * XH + n + 1)
                if t == 0 and h >= 2:
                    act.wait_ge(s_pT, 2 * XH + TT * (h - 1))
                c = S_NM + n % 8
                act.activation(ps[:, h % 2, t, :], bank[n % 3][:, :], ACT.Exp, bias=small[:, c:c + 1],
                               accum_out=small[:, S_SM + n % 8:S_SM + n % 8 + 1]).then_inc(s_pe, 1)

            def take_transposed(h, st):
                act.wait_ge(s_pT, 2 * XH + TT * h + st + 1)
                if h >= 2:
                    act.wait_ge(s_pv, 2 * XH + h - 1)
                act.copy(psT[:, h % 2, st, :], bank[3 + st % 2][:, :]).then_inc(s_pca, 1)

            def attended_hi(h):
                if h % 2:
                    act.wait_ge(s_pv, 2 * XH + h + 1)
                    act.copy(ahi[:, h // 2, :], bank[6 + (h // 2) % 2][:, :]).then_inc(s_ah, 1)

            for t in range(TT):
                self_exp(0, t)
            for h in range(QH):
                if h >= 2:
                    attended_hi(h - 2)
                self_exp(h + 1, 0)
                self_exp(h + 1, 1)
                if 0 <= h - POOL_AT - 1 < 4:
                    n = h - POOL_AT - 1
                    act.wait_ge(s_py, n + 1)
                    act.copy(ahi[:, 4 + POOL_ORDER[n], :], po[:, n % 2, :]).then_inc(s_pyh, 1)
                take_transposed(h, 1)
                self_exp(h + 1, 2)
                self_exp(h + 1, 3)
                take_transposed(h, 2)
                take_transposed(h, 3)
            attended_hi(QH - 1)
            for j in range(KD):
                hi_stream(phases["out2"], 0, j)
                square_res("rms2", j, phases["out2"])
            norm_tail("rms2")
            ffn("f3", None)

        @block.gpsimd
        def _(pool):
            link = linker(pool, pool_chain)

            def lo_stream(ph, i, jj):
                ahead(split_lo, pool, ph, i, jj, POOL)

            def norm_tail(norm, between=None):
                idx, centred = NORMS[norm][:2]
                for k in range(KD):
                    if by(OPERAND[norm], k) == POOL:
                        if centred:
                            pool.wait_ge(normed, 8 * idx + k + 1)
                        else:
                            pool.wait_ge(hi_act, HI0[norm] + k + 1)
                        src = res[:, k, :] if centred else hval[:, k % 2, :]
                        pool.tensor_tensor(alo[:, k, :], src, ahi[:, k, :], ALU.subtract).then_inc(act_pool, 1)
                    if between:
                        between(k)

            def ffn(name):
                for part in range(len(PARTS)):
                    ph = phases[f"{name}_up{part}"]
                    each_block(pool, ph, lambda i, jj, ph=ph: lo_stream(ph, i, jj))
                    ph = phases[f"{name}_down{part}"]
                    for j in range(KD):
                        lo_stream(ph, 0, j)

            for i in range(2):
                pool.sem_inc(lo_ready[i], RAW // 2)
            pool.sem_inc(block_done, SPLIT)
            pool.sem_inc(bank_free, RAW)
            pool.sem_inc(value_done, 2)
            pool.sem_inc(hidden_ready, 2)
            link(pool.memset(small[:, S_EPS5:S_EPS5 + 1], LN_EPS))
            link(pool.memset(small[:, S_EPS6:S_EPS6 + 1], RMS_EPS))
            pool.memset(wT[:, :, :], 0.0).then_inc(s_wTz, 1)
            for b in range(0, AHEAD, 2):
                split_lo(pool, blocks[b][0], 0, blocks[b][1])
            ffn("f1")
            norm_tail("ln1")
            def level_args(s):
                h, n = STEPS[s]
                e, lv = NTH[s], LEVELS[n]
                b, o = halves(cum[:, h, :], lv), halves(dec[:, e % DEC, :], lv)
                c = 1 << lv
                ref = b[:, :, 0, c - 1:c].broadcast_to([P, T // (2 * c), c])
                pool.wait_ge(s_cum, h + 1)
                if e >= DEC:
                    pool.wait_ge(s_qk, e - DEC + 1)
                pool.tensor_tensor(o[:, :, 0, :], ref, b[:, :, 0, :], ALU.subtract)
                pool.tensor_tensor(o[:, :, 1, :], b[:, :, 1, :], ref, ALU.subtract).then_inc(s_arg, 1)

            for n, tasks in enumerate(plan):
                if n == 1:
                    wait_block(pool, phases["in"], 0, 0)
                    pool.memset(kt[:, :, :], 0.0).then_inc(s_az, 1)
                    for h in range(2):
                        pool.memset(acc[:, h, :], 0.0).then_inc(s_az, 1)
                for kind, s in plan[n + 1] if n + 1 < len(plan) else []:
                    if kind == "level" and s in NTH:
                        level_args(s)
                    if kind == "power" and s + 2 < HG:
                        pool.wait_ge(s_om, s + 1)
                        pool.memset(acc[:, s % 2, :], 0.0).then_inc(s_az, 1)
                lo_stream(phases["in"], 0, n)
            for n, k in enumerate(OUT_TILES):
                if by("out", n) == POOL:
                    pool.wait_ge(hi_act, 8 + n + 1)
                    pool.tensor_tensor(alo[:, k, :], mixed(k), ahi[:, k, :], ALU.subtract).then_inc(act_pool, 1)
            for j in range(KD):
                lo_stream(phases["out"], 0, j)
                if j == MEM_AT + 1:
                    for k in range(KD):
                        pool.wait_ge(s_mh, k + 1)
                        pool.tensor_tensor(mlo[:, k, :], mval[:, k % MVAL, :], mhi[:, k, :], ALU.subtract).then_inc(s_ml, 1)
            for name in ("mk", "mv", "xq", "xo"):
                for j in range(KD):
                    lo_stream(phases[name], 0, j)
            norm_tail("ln3")
            ffn("f2")
            pool.wait_ge(mean_ready, NORMS["ln4"][0] + 1)
            for k in POOL_SUB:
                pool.tensor_tensor(res[:, k, :], res[:, k, :], mean[:, :], ALU.subtract).then_inc(s_mid, 1)
            norm_tail("rms1")
            for j in range(10):
                lo_stream(phases["in2"], 0, j)
            for n, g in enumerate(POOL_ORDER):
                pool.wait_ge(bank_free, RAW + phases["in2"].base + 6 + n + 1)
                if n:
                    pool.wait_ge(s_pool, n)
                src = su[:, n, :]
                bufs = [pa, pb]
                for lv in range(g + 1):
                    w = (1 << lv) // 2
                    reach = (1 << g) - (1 << lv)
                    lo, wide = 8 - reach, T + 2 * reach
                    dst = bufs[lv % 2]
                    a0, a1 = (lo - 1, lo) if lv == 0 else (lo - w, lo + w)
                    link(pool.tensor_tensor(dst[:, lo:lo + wide], src[:, a0:a0 + wide], src[:, a1:a1 + wide], ALU.add))
                    src = dst
                pool.wait_ge(s_rcn[n % 2], 16 * (n // 2 + 1))
                link(pool.tensor_tensor(src[:, 8:8 + T], src[:, 8:8 + T], rcnt[:, n % 2, :], ALU.mult))
                pool.tensor_tensor(su[:, n, 8:8 + T], src[:, 8:8 + T], su[:, n, 8:8 + T], ALU.subtract).then_inc(s_pool, 1)
            for j in range(KD):
                lo_stream(phases["out2"], 0, j)
            norm_tail("rms2")
            ffn("f3")

        @block.vector
        def _(dve):
            link = linker(dve, dve_chain)

            def lo_stream(ph, j):
                ahead(split_lo, dve, ph, 0, j, DVE)

            def hidden(ph, i, jj, t0, scale):
                tile = t0 + 2 * i + jj // 2
                slot = (t0 + jj // 2) % 2
                at = 2 * i + jj // 2
                wait_block(dve, ph, i, jj)
                dve.wait_ge(gate_done, tile + 1)
                dve.wait_ge(hidden_ready, tile + 1)
                dve.scalar_tensor_tensor(out=hval[:, slot, :], in0=gate[:, slot, :], scalar=scale,
                                         in1=bank_of(ph, jj)[:, :], op0=ALU.mult, op1=ALU.mult).then_inc(value_done, 1)
                dve.wait_ge(value_done, 2 + tile + 1)
                dve.tensor_copy(hhi[:, bass.ds(at, 1), :].rearrange("p a t -> p (a t)"), hval[:, slot, :]).then_inc(bank_free, 2)
                dve.wait_ge(bank_free, RAW + ph.base + jj + 4 * i + 1)
                dve.tensor_tensor(hlo[:, bass.ds(at, 1), :].rearrange("p a t -> p (a t)"), hval[:, slot, :],
                                  hhi[:, bass.ds(at, 1), :].rearrange("p a t -> p (a t)"), ALU.subtract).then_inc(hidden_ready, 1)

            def add_res(ph, j, scale):
                wait_block(dve, ph, 0, j)
                dve.scalar_tensor_tensor(out=res[:, j, :], in0=res[:, j, :], scalar=scale,
                                         in1=bank_of(ph, j)[:, :], op0=ALU.mult, op1=ALU.add).then_inc(bank_free, 1)

            def add_sums(norm, j):
                idx, centred = NORMS[norm][:2]
                if not 1 <= j <= SUM_STEPS:
                    return
                dve.wait_ge(square_done, 8 * idx + j + 1)
                if j > 1:
                    dve.wait_ge(sums_done, steps_before(norm) + j - 1)
                last = (res[:, 0, :], square[:, 0, :]) if j == 1 else (sum1[:, :], sum2[:, :])
                if centred:
                    dve.tensor_tensor(sum1[:, :], last[0], res[:, j, :], ALU.add)
                dve.tensor_tensor(sum2[:, :], last[1], square[:, j % 2, :], ALU.add).then_inc(sums_done, 1)

            def norm_tail(norm, between=None):
                idx, centred, grow, brow = NORMS[norm]
                layer = OPERAND.get(norm)
                if centred:
                    dve.wait_ge(stat_sq, idx + 1)
                    dve.wait_ge(mean_sq, idx + 1)
                    link(dve.tensor_tensor(var[:, 1, :], bank[5][:, :], var[:, 0, :], ALU.subtract))
                    dve.tensor_scalar(var[:, 1, :], var[:, 1, :], 0.0, None, ALU.max).then_inc(var_ready, 1)
                    link(dve.tensor_copy(mean[:, :], bank[4][:, :]))
                    dve.sem_inc(mean_ready, 1)
                    link(dve.tensor_tensor(res[:, 0, :], res[:, 0, :], mean[:, :], ALU.subtract))
                dve.wait_ge(rstd_ready, idx + 1)

                def lo(k):
                    if k >= 0 and layer and by(layer, k) == DVE:
                        dve.wait_ge(*((normed, 8 * idx + k + 1) if centred else (hi_act, HI0[norm] + k + 1)))
                        src = res[:, k, :] if centred else hval[:, k % 2, :]
                        dve.tensor_tensor(alo[:, k, :], src, ahi[:, k, :], ALU.subtract).then_inc(act_dve, 1)
                for k in range(KD):
                    if centred:
                        if norm == "ln4" and k in POOL_SUB:
                            dve.wait_ge(s_mid, POOL_SUB.index(k) + 1)
                        elif k:
                            link(dve.tensor_tensor(res[:, k, :], res[:, k, :], mean[:, :], ALU.subtract))
                        dve.tensor_tensor(res[:, k, :], res[:, k, :], rstd[:, :], ALU.mult).then_inc(scaled, 1)
                    else:
                        if k >= 2:
                            dve.wait_ge(*operand(layer, k - 2))
                        dve.scalar_tensor_tensor(out=hval[:, k % 2, :], in0=res[:, k, :], scalar=vcol(grow + k),
                                                 in1=rstd[:, :], op0=ALU.mult, op1=ALU.mult).then_inc(scaled, 1)
                    lo(k - 1)
                    if between:
                        between(k)
                lo(KD - 1)

            def ffn(name, alpha, scale, norm, once=None):
                for part in range(len(PARTS)):
                    ph = phases[f"{name}_up{part}"]
                    t0 = part_tile0(ph.name)

                    def step(i, jj, ph=ph, t0=t0):
                        if jj % 2:
                            hidden(ph, i, jj, t0, scale)
                    each_block(dve, ph, step)
                    if once and part == 0:
                        once()
                    ph = phases[f"{name}_down{part}"]
                    last = part == len(PARTS) - 1
                    for j in range(KD):
                        if last and norm:
                            add_sums(norm, j - 1)
                        add_res(ph, j, alpha if part == 0 else 1.0)
                        lo_stream(ph, j)
                        if last and norm is None and j >= 1:
                            store_tile(j - 1)
                if norm is None:
                    store_tile(KD - 1)

            def store_tile(j):
                dve.wait_ge(s_oT, j + 1)
                if j >= 2:
                    dve.wait_ge(s_out, 16 * (j - 1))
                dve.tensor_copy(ob[:, j % 2, :, :], bank[4 + j % 2][:, :].rearrange("p (n f) -> p n f", f=P)).then_inc(s_ob, 1)

            split_lo(dve, blocks[1][0], 0, blocks[1][1])
            for k in range(KD):
                dve.wait_ge(s_xhi, k + 1)
                dve.tensor_tensor(alo[:, k, :], res[:, k, :], ahi[:, k, :], ALU.subtract).then_inc(act_dve, 1)

            def vectors():
                dve.wait_ge(s_vT0, 1)
                link(dve.tensor_copy(vecs[:, 0:V_ROWS], bank[4][:, 0:V_ROWS]))
                link(dve.tensor_scalar(vcol(V_QN), vcol(V_QN), HD ** -0.5, None, ALU.mult))
                link(dve.tensor_tensor(small[:, S_LB:S_LB + 4], vecs[:, V_LB:V_LB + 4], vecs[:, V_LB + 4:V_LB + 8], ALU.max))
                dve.tensor_tensor(small[:, S_E0:S_E0 + 4], vecs[:, V_LB:V_LB + 4], small[:, S_LB:S_LB + 4], ALU.subtract).then_inc(s_vecs, 1)
                dve.tensor_tensor(small[:, S_E1:S_E1 + 4], vecs[:, V_LB + 4:V_LB + 8], small[:, S_LB:S_LB + 4], ALU.subtract).then_inc(s_vecs, 1)
                dve.wait_ge(s_wsT, 1)
                dve.wait_ge(s_wTz, 1)
                dve.wait_ge(s_const, 48)
                dve.copy_predicated(wT[:, :, :], masks[:, len(LEVELS) + 1:len(LEVELS) + 2, :].broadcast_to([P, SG, P]),
                                    bank[5][:, :].rearrange("p (g t) -> p g t", g=SG)).then_inc(s_wTr, 1)
                dve.wait_ge(s_lbe, 1)
                link(dve.tensor_tensor(small[:, S_OML:S_OML + 4], small[:, S_E0:S_E0 + 4], small[:, S_E1:S_E1 + 4], ALU.add))
                link(dve.reciprocal(small[:, S_OML:S_OML + 4], small[:, S_OML:S_OML + 4]))
                link(dve.tensor_tensor(small[:, S_LB:S_LB + 4], small[:, S_E0:S_E0 + 4], small[:, S_OML:S_OML + 4], ALU.mult))
                link(dve.tensor_scalar(small[:, S_OML:S_OML + 4], small[:, S_LB:S_LB + 4], -1.0, 1.0, ALU.mult, ALU.add))

            ffn("f1", ALPHA, 0.5, "ln1", vectors)
            norm_tail("ln1")

            def level_scale(s):
                h, n = STEPS[s]
                e, lv = NTH[s], LEVELS[n]
                d = halves(dec[:, e % DEC, :], lv)
                dve.wait_ge(s_dexp, e + 1)
                if e >= 2:
                    dve.wait_ge(s_smm, SCALED[e - 2] + 1)
                else:
                    dve.wait_ge(s_az, 1)
                dve.tensor_tensor(qt[:, e % 2, :].rearrange("p (n c) -> p n c", c=1 << lv), halves(mq[:, h, :], lv)[:, :, 1, :],
                                  d[:, :, 1, :], ALU.mult)
                dve.tensor_tensor(halves(kt[:, e % 2, :], lv)[:, :, 0, :], halves(mk[:, h, :], lv)[:, :, 0, :],
                                  d[:, :, 0, :], ALU.mult).then_inc(s_qk, 1)

            def level_put(s):
                h, n = STEPS[s]
                dve.wait_ge(s_smm, s + 1)
                dve.wait_ge(s_az, 1 + h + 1)
                if s:
                    dve.wait_ge(s_put, s)
                if n < len(LEVELS):
                    c = 1 << LEVELS[n]
                    to = acc[:, h % 2, :].rearrange("p (m n two c) -> p m n two c", m=TT, two=2, c=c)[:, :, :, 1, :]
                    mask = masks[:, n:n + 1, 0:P // 2].broadcast_to([P, TT, P // 2]).rearrange("p m (n c) -> p m n c", c=c)
                    new = bank[4 + s % 2][:, 0:T // 2].rearrange("p (m n c) -> p m n c", m=TT, c=c)
                else:
                    to = acc[:, h % 2, :].rearrange("p (n t) -> p n t", t=P)
                    mask = masks[:, n:n + 1, :].broadcast_to([P, TT, P])
                    new = bank[4 + s % 2][:, :].rearrange("p (n t) -> p n t", t=P)
                dve.copy_predicated(to, mask, new).then_inc(s_put, 1)

            def mixer(kind, n):
                if kind == "forget":
                    lb, oml = small[:, S_LB + n:S_LB + n + 1], small[:, S_OML + n:S_OML + n + 1]
                    dve.wait_ge(s_sig, n + 1)
                    link(dve.tensor_scalar(cum[:, n, :], cum[:, n, :], oml, lb, ALU.mult, ALU.add))
                    link(dve.tensor_scalar(cum[:, n, :], cum[:, n, :], 2.0 ** -60, None, ALU.max))
                    dve.tensor_scalar(mk[:, n, :], mk[:, n, :], oml, None, ALU.mult).then_inc(s_fg, 1)
                elif kind == "logs":
                    for h in range(HG):
                        dve.wait_ge(s_lf, h + 1)
                        dve.tensor_tensor_scan(cum[:, h, :], restart[:, :], cum[:, h, :], 0.0, ALU.mult, ALU.add).then_inc(s_cum, 1)
                elif kind == "take_values":
                    dve.wait_ge(s_ivT, n + 1)
                    dve.tensor_copy(vT[:, n, :, :], bank[7][:, :].rearrange("p (n f) -> p n f", f=P)).then_inc(s_ivc, 1)
                elif kind == "level" and n in NTH:
                    if STEPS[n][1] == 0:
                        wait_in(dve, Q0 + STEPS[n][0])
                    level_scale(n)
                elif kind == "put":
                    level_put(n)
                elif kind == "ends":
                    c, q, k = cum[:, n, :], mq[:, n, :], mk[:, n, :]
                    ct = c.rearrange("p (n t) -> p n t", t=P)
                    if n:
                        dve.wait_ge(s_keT, n)
                    dve.tensor_tensor(kend[:, :].rearrange("p (n t) -> p n t", t=P), ct[:, 0:3, P - 1:P].broadcast_to([P, 3, P]),
                                      ct[:, 0:3, :], ALU.subtract).then_inc(s_kd, 1)
                    dve.wait_ge(s_ebd, n + 1)
                    link(dve.tensor_tensor(qe[:, :], q, eb[:, :], ALU.mult))
                    dve.wait_ge(s_kde, n + 1)
                    dve.tensor_tensor(kend[:, :], kend[:, :], k[:, 0:3 * P], ALU.mult).then_inc(s_ke, 1)
                elif kind == "update":
                    dve.wait_ge(s_keT, n + 1)
                    dve.tensor_copy(kendT[:, :], bank[7][:, 0:3 * P]).then_inc(s_kec, 1)
                elif kind == "outputs":
                    dve.wait_ge(s_um, n + 1)
                    link(dve.tensor_copy(state[:, 0, :], bank[7][:, 0:P]))
                    for j in range(1, 3):
                        i = dve.scalar_tensor_tensor(out=state[:, j, :], in0=state[:, j - 1, :],
                                                     scalar=eb[:, (j + 1) * P - 1:(j + 1) * P],
                                                     in1=bank[7][:, j * P:(j + 1) * P], op0=ALU.mult, op1=ALU.add)
                        if j == 1:
                            link(i)
                    i.then_inc(s_st, 1)
                elif kind == "normed":
                    dve.wait_ge(s_ors, n + 1)
                    dve.scalar_tensor_tensor(out=mq[:, n, :], in0=bank[6][:, :], scalar=vcol(V_HGN), in1=ors[:, :],
                                             op0=ALU.mult, op1=ALU.mult).then_inc(s_on, 1)
                elif kind == "gate":
                    dve.wait_ge(s_act2, n + 1)
                    dve.wait_ge(s_on, n + 1)
                    dve.tensor_tensor(mq[:, n, :], mq[:, n, :], mg[:, n, :], ALU.mult).then_inc(s_prod, 1)
                elif kind == "centre":
                    pb_ = bank[SPATIAL_BANK[n]]
                    dve.wait_ge(s_gvT, n + 1)
                    for t in range(TT):
                        link(dve.bn_stats(sgst[:, t, :], pb_[:, t * P:(t + 1) * P]))
                    for t in range(TT):
                        i = dve.bn_aggr(sgmv[:, t, :], sgst[:, t, :])
                        if t < TT - 1:
                            link(i)
                    i.then_inc(s_sgv, 1)
                    dve.wait_ge(s_sgr, n + 1)
                    for t in range(TT):
                        link(dve.tensor_scalar(vn[:, n, t * P:(t + 1) * P], pb_[:, t * P:(t + 1) * P],
                                               sgmv[:, t, 0:1], sgr[:, t:t + 1], ALU.subtract, ALU.mult))
                    v3 = vn[:, n, :].rearrange("p (n f) -> p n f", f=P)
                    dve.wait_ge(s_rows, 48)
                    link(dve.tensor_tensor(v3, v3, row(0, n), ALU.mult))
                    dve.tensor_tensor(v3, v3, row(1, n), ALU.add).then_inc(s_vn, 1)
                elif kind == "bias":
                    dve.wait_ge(s_sm, n + 1)
                    dve.tensor_tensor(mv[:, n, :].rearrange("p (n f) -> p n f", f=P),
                                      bank[SPATIAL_BANK[n]][:, :].rearrange("p (n f) -> p n f", f=P), row(2, n), ALU.add).then_inc(s_so, 1)
                elif kind == "spatial":
                    dve.wait_ge(s_gv, 4 + n + 1)
                    dve.wait_ge(s_so, n + 1)
                    dve.tensor_tensor(mu[:, n, :], mu[:, n, :], mv[:, n, :], ALU.mult).then_inc(s_mul, 1)

            def row(r, g):
                return sgb[:, r, g * P:(g + 1) * P].unsqueeze(1).broadcast_to([P, TT, P])

            for n, tasks in enumerate(plan):
                for task in tasks:
                    mixer(*task)
                if IN_ORDER[n] in (IV0 + 2, IV0 + 3):
                    dve.wait_ge(s_ivT, IN_ORDER[n] - IV0 - 1)
                wait_block(dve, phases["in"], 0, n)
                dve.tensor_copy(IN_DST[n], bank_of(phases["in"], n)[:, :]).then_inc(bank_free, 1)
                lo_stream(phases["in"], n)
            for n, k in enumerate(OUT_TILES):
                if n == 5:
                    mixer("gate", 3)
                if by("out", n) == DVE:
                    dve.wait_ge(hi_act, 8 + n + 1)
                    dve.tensor_tensor(alo[:, k, :], mixed(k), ahi[:, k, :], ALU.subtract).then_inc(act_dve, 1)
                if n == 0:
                    mixer("bias", 3)
                    mixer("spatial", 3)
            for j in range(KD):
                add_sums("ln2", j - 1)
                add_res(phases["out"], j, ALPHA)
                lo_stream(phases["out"], j)
                if j == MEM_AT - 1:
                    dve.wait_ge(s_mem, 16)
                    for t in range(MT):
                        for hf in range(2):
                            link(dve.bn_stats(mst[:, 2 * t + hf, :], memin[:, t, hf * T:(hf + 1) * T]))
                    for t in range(MT):
                        link(dve.bn_aggr(mmv[:, t, :], mst[:, 2 * t:2 * t + 2, :].rearrange("p a b -> p (a b)")))
                    dve.sem_inc(s_mv, 1)
                if j == MEM_AT:
                    dve.wait_ge(s_mr, 1)
                    for t in range(MT):
                        dve.tensor_scalar(memin[:, t, :], memin[:, t, :], mmv[:, t, 0:1], mrs[:, t:t + 1],
                                          ALU.subtract, ALU.mult).then_inc(s_mn, 1)
                if j == MEM_AT + 1:
                    for k in range(KD):
                        dve.wait_ge(s_mT, k // 2 + 1)
                        if k >= MVAL:
                            dve.wait_ge(s_ml, k - MVAL + 1)
                        dve.tensor_scalar(mval[:, k % MVAL, :], bank[4 + k // 2][:, (k % 2) * MEM:(k % 2 + 1) * MEM],
                                          vcol(V_MEMG + k), vcol(V_MEMB + k), ALU.mult, ALU.add).then_inc(s_ma, 1)

            def mem_key(j):
                wait_block(dve, phases["mk"], 0, j)
                dve.tensor_copy(kx[:, j, :], bank_of(phases["mk"], j)[:, 0:MEM]).then_inc(bank_free, 1)
                lo_stream(phases["mk"], j)
            for j in range(2):
                mem_key(j)
            norm_tail("ln2", lambda k: mem_key(k + 2) if k + 2 < KD else None)
            for j in range(KD):
                wait_block(dve, phases["mv"], 0, j)
                if j >= 2:
                    dve.wait_ge(s_vxT, j - 1)
                dve.tensor_copy(vxt[:, j % 2, :], bank_of(phases["mv"], j)[:, 0:MEM]).then_inc(bank_free, 1)
                lo_stream(phases["mv"], j)
                if j >= 1:
                    dve.wait_ge(s_vxT, j)
                    dve.tensor_copy(vx[:, :, (j - 1) * P:j * P], bank[4 + (j - 1) % 2][:, 0:MEM].rearrange("p (n f) -> p n f", f=P)).then_inc(s_kv, 1)
            dve.wait_ge(s_vxT, KD)
            dve.tensor_copy(vx[:, :, (KD - 1) * P:KD * P], bank[4 + (KD - 1) % 2][:, 0:MEM].rearrange("p (n f) -> p n f", f=P)).then_inc(s_kv, 1)
            for j in range(KD):
                wait_block(dve, phases["xq"], 0, j)
                dve.tensor_scalar(qx[:, j, :], bank_of(phases["xq"], j)[:, :], (D // XH) ** -0.5, None, ALU.mult).then_inc(bank_free, 1)
                lo_stream(phases["xq"], j)
            def cross_max(h):
                n0 = S_NM + 4 * (h % 2)
                dve.wait_ge(s_sc, h + 1)
                for half in range(2):
                    dve.tensor_reduce(small[:, n0 + 2 * half:n0 + 2 * half + 2],
                                      bank[2 * (h % 2) + half][:, :].rearrange("p (n m) -> p n m", m=MEM), AX.X, ALU.max,
                                      negate=True).then_inc(s_nm, 1)

            def attended_lo(h):
                for d in range(2):
                    dve.wait_ge(s_ah, 2 * h + d + 1)
                    dve.tensor_tensor(alo[:, 2 * h + d, :], bank[6 + d][:, :], ahi[:, 2 * h + d, :], ALU.subtract).then_inc(act_dve, 1)

            cross_max(0)
            for h in range(XH):
                for t in range(TT):
                    c = 4 * (h % 2) + t
                    if t == 0:
                        dve.wait_ge(s_pe, TT * (h + 1))
                        link(dve.reciprocal(small[:, S_RI + c:S_RI + c + 4], small[:, S_SM + c:S_SM + c + 4]))
                    dve.tensor_scalar(px[:, h % 2, t, :], px[:, h % 2, t, :], small[:, S_RI + c:S_RI + c + 1], None,
                                      ALU.mult).then_inc(s_pn, 1)
                if h + 1 < XH:
                    cross_max(h + 1)
                if h >= 2:
                    attended_lo(h - 2)
                dve.wait_ge(s_pT, 2 * h + 1)
                if h >= 2:
                    dve.wait_ge(s_pv, 2 * (h - 1))
                dve.tensor_copy(pxT[:, h % 2, 0, :], bank[4][:, :]).then_inc(s_pcd, 1)
            attended_lo(XH - 2)
            attended_lo(XH - 1)
            for j in range(KD):
                add_sums("ln3", j - 1)
                add_res(phases["xo"], j, ALPHA)
                lo_stream(phases["xo"], j)
            norm_tail("ln3")
            ffn("f2", ALPHA, 0.5, "ln4")
            norm_tail("ln4")
            norm_tail("rms1")
            def prepare(kind, j):
                x = in2_dst(j)
                if kind == "rstd":
                    dve.wait_ge(s_hrs, j + 1)
                    dve.scalar_tensor_tensor(out=x, in0=x, scalar=vcol(V_QN if j else V_KN), in1=r2[:, j % 2, :],
                                             op0=ALU.mult, op1=ALU.mult).then_inc(s_hn, 1)
                elif kind == "rope":
                    dve.wait_ge(s_rope, 32)
                    dve.wait_ge(s_hrot, j + 1)
                    if j:
                        dve.wait_ge(s_hr, j)
                    link(dve.tensor_tensor(r3[:, :], bank[6 + j % 2][:, :], rope[:, 1, :], ALU.mult))
                    link(dve.tensor_tensor(x, x, rope[:, 0, :], ALU.mult))
                    dve.tensor_tensor(x, x, r3[:, :], ALU.add).then_inc(s_hr, 1)
                elif kind == "take_v":
                    dve.wait_ge(s_svT, 1)
                    dve.tensor_copy(sv[:, :, :], bank[5][:, :].rearrange("p (n f) -> p n f", f=P)).then_inc(s_dupc, 1)
                elif kind == "take_k":
                    for g in range(2):
                        dve.wait_ge(s_kh, g + 1)
                        dve.tensor_tensor(klo[:, g, :], bank[(4, 7)[g]][:, :], khi[:, g, :], ALU.subtract).then_inc(s_dupc, 1)
                elif kind == "stack":
                    for n in range(2):
                        own, other = slice(HD * n, HD * n + HD), slice(HD * (1 - n), HD * (1 - n) + HD)
                        dve.wait_ge(s_sth, 2 * (j - 1) + n + 1)
                        dve.tensor_tensor(sst[other, 2 * (j - 1) + n, :], x[own, :], sst[own, 2 * (j - 1) + n, :],
                                          ALU.subtract).then_inc(s_stl, 1)

            for j, tasks in enumerate(plan2):
                for task in tasks:
                    prepare(*task)
                wait_block(dve, phases["in2"], 0, j)
                if j == 6:
                    link(dve.memset(su[:, :, 0:8], 0.0))
                    link(dve.memset(su[:, :, 8 + T:16 + T], 0.0))
                dve.tensor_copy(in2_dst(j), bank_of(phases["in2"], j)[:, :]).then_inc(bank_free, 1)
                lo_stream(phases["in2"], j)

            def self_max(h, t):
                n = TT * h + t
                c = n % 8
                if h >= QH:
                    return
                dve.wait_ge(s_sc, XH + n + 1)
                dve.tensor_reduce(small[:, S_NM + c:S_NM + c + 1], bank[n % 3][:, :], AX.X, ALU.max, negate=True).then_inc(s_nm, 1)

            def self_normalise(h, t):
                n = TT * h + t
                c = n % 8
                if h >= QH:
                    return
                dve.wait_ge(s_pe, TT * XH + n + 1)
                link(dve.reciprocal(small[:, S_RI + c:S_RI + c + 1], small[:, S_SM + c:S_SM + c + 1]))
                dve.tensor_scalar(ps[:, h % 2, t, :], ps[:, h % 2, t, :], small[:, S_RI + c:S_RI + c + 1], None, ALU.mult).then_inc(s_pn, 1)

            def take_transposed(h, st):
                dve.wait_ge(s_pT, 2 * XH + TT * h + st + 1)
                if h >= 2:
                    dve.wait_ge(s_pv, 2 * XH + h - 1)
                dve.tensor_copy(psT[:, h % 2, st, :], bank[3][:, :]).then_inc(s_pcd, 1)

            def attended_lo(h):
                if h % 2:
                    dve.wait_ge(s_ah, 2 * XH + h // 2 + 1)
                    dve.tensor_tensor(alo[:, h // 2, :], bank[6 + (h // 2) % 2][:, :], ahi[:, h // 2, :],
                                      ALU.subtract).then_inc(act_dve, 1)

            for t in range(TT):
                self_max(0, t)
                if t:
                    self_normalise(0, t - 1)
            for h in range(QH):
                self_normalise(h, TT - 1)
                self_max(h + 1, 0)
                self_max(h + 1, 1)
                if h >= 2:
                    attended_lo(h - 2)
                if 0 <= h - POOL_AT - 2 < 4:
                    n = h - POOL_AT - 2
                    dve.wait_ge(s_pyh, n + 1)
                    g = POOL_ORDER[n]
                    dve.tensor_tensor(alo[:, 4 + g, :], po[:, n % 2, :], ahi[:, 4 + g, :], ALU.subtract).then_inc(act_dve, 1)
                if 0 <= h - POOL_AT - 1 < 4:
                    n = h - POOL_AT - 1
                    g = POOL_ORDER[n]
                    dve.wait_ge(s_pmm, n + 1)
                    if n >= 2:
                        dve.wait_ge(*operand("out2", OUT2_TILES.index(4 + POOL_ORDER[n - 2])))
                    dve.tensor_scalar(po[:, n % 2, :], bank[5][:, :], vcol(V_POOLB + g), vcol(V_POOLS + g),
                                      ALU.add, ALU.mult).then_inc(s_py, 1)
                take_transposed(h, 0)
                self_max(h + 1, 2)
                self_normalise(h + 1, 0)
                self_normalise(h + 1, 1)
                self_max(h + 1, 3)
                self_normalise(h + 1, 2)
            attended_lo(QH - 1)
            for j in range(KD):
                add_sums("rms2", j - 1)
                add_res(phases["out2"], j, 1.0)
                lo_stream(phases["out2"], j)
            norm_tail("rms2")
            ffn("f3", 1.0, 1.0, None)

        @block.tensor
        def _(pe):
            def linear(name, ready=None, xhi=ahi, xlo=alo, width=T, after=None, order=None):
                ph = phases[name]
                multiply_two(pe, ph, xhi, xlo, width, ready or made(name), order=order)
                for j in range(ph.n):
                    if j >= 2:
                        multiply(pe, ph, 0, j, xhi, xlo, width)
                    if j >= 1 and after:
                        after(j)

            def made(layer):
                return lambda k: operand(layer, k)

            def stats(norm, ph=None):
                idx, centred = NORMS[norm][:2]
                last = KD - 1
                pe.wait_ge(sums_done, steps_before(norm) + SUM_STEPS)
                if centred:
                    pe.matmul(bank[4][:, :], mats[:, C_MEAN, :], sum1[:, :], start=True, stop=False)
                pe.matmul(bank[5][:, :], mats[:, C_MEAN, :], sum2[:, :], start=True, stop=False)
                if centred:
                    pe.wait_ge(bank_free, RAW + ph.base + last + 1)
                    pe.matmul(bank[4][:, :], mats[:, C_MEAN, :], res[:, last, :], start=False, stop=True).then_inc(stat_mean, 1)
                pe.wait_ge(square_done, 8 * (idx + 1))
                pe.matmul(bank[5][:, :], mats[:, C_MEAN, :], square[:, last % 2, :], start=False, stop=True).then_inc(stat_sq, 1)

            def ffn(name, norm, once=None, before=None):
                for part in range(len(PARTS)):
                    ph = phases[f"{name}_up{part}"]
                    if part == 0:
                        multiply_two(pe, ph, ahi, alo, T, made(name), before)
                        for jj in range(2, 4):
                            multiply(pe, ph, 0, jj, ahi, alo)
                        start = 1
                    else:
                        start = 0
                    with pe.Fori(start, ph.n // 4) as i:
                        for jj in range(4):
                            multiply(pe, ph, i, jj, ahi, alo)
                    if once and part == 0:
                        once()
                    ph = phases[f"{name}_down{part}"]
                    t0 = part_tile0(ph.name)
                    for j in range(KD):
                        r = (lambda k: (hidden_ready, 2 + t0 + k + 1)) if j == 0 else None
                        multiply(pe, ph, 0, j, hhi, hlo, T, r)
                        if norm is None and part == len(PARTS) - 1 and j >= 1:
                            store_tile(ph, j - 1)
                if norm:
                    stats(norm, ph)
                else:
                    store_tile(ph, KD - 1)

            def store_tile(ph, j):
                pe.wait_ge(bank_free, RAW + ph.base + j + 1)
                if j >= 2:
                    pe.wait_ge(s_ob, j - 1)
                for t in range(TT):
                    i = pe.transpose(bank[4 + j % 2][:, t * P:(t + 1) * P], res[:, j, t * P:(t + 1) * P], ident)
                i.then_inc(s_oT, 1)

            def four(o, src, s):
                for t in range(TT):
                    i = pe.transpose(o[:, t * P:(t + 1) * P], src[:, t * P:(t + 1) * P], ident)
                i.then_inc(s, 1)

            def turn_x(k):
                pe.wait_ge(s_x[k // 2], 16)
                if k >= 4:
                    pe.wait_ge(s_xhi, k - 3)
                for t in range(TT):
                    i = pe.transpose(bank[4 + k % 4][:, t * P:(t + 1) * P], xin[:, t, k * P:(k + 1) * P], ident)
                i.then_inc(s_xT, 1)

            def turn_vectors():
                pe.wait_ge(s_const, 48)
                pe.wait_ge(s_vec, 16 * 20)
                pe.transpose(bank[4][:, 0:V_ROWS], vrow[0:V_ROWS, :], ident[0:V_ROWS, 0:V_ROWS]).then_inc(s_vT0, 1)
                pe.wait_ge(s_ws, 16)
                for g in range(SG):
                    i = pe.transpose(bank[5][:, g * P:(g + 1) * P], wsin[:, g, :], ident)
                i.then_inc(s_wsT, 1)

            pe.wait_ge(s_ident, 16)
            for k in range(2):
                turn_x(k)
            ffn("f1", "ln1", turn_vectors, lambda k: turn_x(k + 2) if k < KD - 2 else None)

            def level_product(s):
                h, n = STEPS[s]
                if n < len(LEVELS):
                    e = NTH[s]
                    pe.wait_ge(s_qk, e + 1)
                    q, k, w = qt[:, e % 2, :], kt[:, e % 2, :], P // 2
                else:
                    q, k, w = mq[:, h, :], mk[:, h, :], P
                if s >= 2:
                    pe.wait_ge(s_put, s - 1)
                for t in range(TT):
                    i = pe.matmul(bank[4 + s % 2][:, t * w:(t + 1) * w], k[:, t * P:(t + 1) * P], q[:, t * w:(t + 1) * w],
                                  start=True, stop=True)
                i.then_inc(s_smm, 1)

            ph = phases["in"]
            def mixer(kind, n):
                o, u = bank[6], bank[7]
                if kind == "values":
                    wait_in(pe, IV0 + n)
                    if n:
                        pe.wait_ge(s_st, n)
                    four(u, ivt[:, n % 2, :], s_ivT)
                elif kind == "level":
                    level_product(n)
                elif kind == "ends":
                    pe.wait_ge(s_ke, n + 1)
                    if n:
                        pe.wait_ge(s_ors, n)
                    if n == 0:
                        pe.wait_ge(s_ivc, 1)
                    for t in range(3):
                        i = pe.transpose(u[:, t * P:(t + 1) * P], kend[:, t * P:(t + 1) * P], ident)
                    i.then_inc(s_keT, 1)
                elif kind == "update":
                    pe.wait_ge(s_kec, n + 1)
                    pe.wait_ge(s_ivc, n + 1)
                    for t in range(3):
                        i = pe.matmul(u[:, t * P:(t + 1) * P], kendT[:, t * P:(t + 1) * P], vT[:, n, t, :], start=True, stop=True)
                    i.then_inc(s_um, 1)
                elif kind == "outputs":
                    pe.wait_ge(s_st, n + 1)
                    pe.wait_ge(s_put, (n + 1) * (len(LEVELS) + 1))
                    if n:
                        pe.wait_ge(s_so, n)
                    for t in range(TT):
                        ot = o[:, t * P:(t + 1) * P]
                        i = pe.matmul(ot, vT[:, n, t, :], acc[:, n % 2, t * P:(t + 1) * P], start=True, stop=(t == 0))
                        if t:
                            i = pe.matmul(ot, state[:, t - 1, :], qe[:, t * P:(t + 1) * P], start=False, stop=True)
                    i.then_inc(s_om, 1)
                elif kind == "power":
                    if n + 1 < HG:
                        pe.wait_ge(s_ivc, n + 2)
                    pe.wait_ge(s_osq, n + 1)
                    pe.matmul(u[:, :], mats[:, C_M128, :], osq[:, :], start=True, stop=True).then_inc(s_oss, 1)
                elif kind == "turn":
                    pe.wait_ge(s_gv, n + 1)
                    if SPATIAL_BANK[n] == 6:
                        pe.wait_ge(s_on, n + 1)
                    else:
                        pe.wait_ge(s_put, len(STEPS))
                    four(bank[SPATIAL_BANK[n]], mv[:, n, :], s_gvT)
                elif kind == "mix":
                    pe.wait_ge(s_vn, n + 1)
                    pe.wait_ge(s_wTr, 1)
                    for t in range(TT):
                        i = pe.matmul(bank[SPATIAL_BANK[n]][:, t * P:(t + 1) * P], vn[:, n, t * P:(t + 1) * P], wT[:, n, :],
                                      start=True, stop=True)
                    i.then_inc(s_sm, 1)

            multiply_two(pe, ph, ahi, alo, T, made("in"))
            for n, tasks in enumerate(plan):
                if n >= 2:
                    multiply(pe, ph, 0, n, ahi, alo)
                for task in tasks:
                    mixer(*task)

            def turn_memory(j):
                if j == MEM_AT + 1:
                    pe.wait_ge(s_mn, MT)
                    for k in range(KD):
                        for t in range(MT):
                            at = (k % 2) * MEM + t * P
                            i = pe.transpose(bank[4 + k // 2][:, at:at + P], memin[:, t, k * P:(k + 1) * P], ident)
                        if k % 2:
                            i.then_inc(s_mT, 1)
            linear("out", after=turn_memory, order=OUT_TILES)

            def stats_ln2(j):
                if j == 1:
                    pe.wait_ge(s_ma, KD)
                    stats("ln2", phases["out"])
            linear("mk", lambda k: (s_ml, k + 1), mhi, mlo, MEM, after=stats_ln2)

            def turn_values(j):
                if j < 1:
                    return
                if j == 1:
                    pe.wait_ge(var_ready, 2)
                pe.wait_ge(bank_free, RAW + phases["mv"].base + j)
                if j >= 3:
                    pe.wait_ge(s_kv, j - 2)
                for t in range(MT):
                    i = pe.transpose(bank[4 + (j - 1) % 2][:, t * P:(t + 1) * P], vxt[:, (j - 1) % 2, t * P:(t + 1) * P], ident)
                i.then_inc(s_vxT, 1)
            linear("mv", lambda k: (s_ml, KD), mhi, mlo, MEM, after=turn_values)
            turn_values(KD)
            linear("xq")
            def cross_scores(h):
                if h < 2:
                    pe.wait_ge(bank_free, RAW + phases["xq"].base + last_block_in(phases["xq"], 2 * h + 1) + 1)
                else:
                    pe.wait_ge(s_pe, TT * (h - 1))
                for t in range(TT):
                    for k in range(2):
                        i = pe.matmul(bank[2 * (h % 2) + t // 2][:, (t % 2) * MEM:(t % 2 + 1) * MEM],
                                      qx[:, 2 * h + k, t * P:(t + 1) * P], kx[:, 2 * h + k, :], start=(k == 0), stop=(k == 1))
                i.then_inc(s_sc, 1)

            def cross_turn(h):
                pe.wait_ge(s_pn, TT * (h + 1))
                if h:
                    pe.wait_ge(s_pcd, h)
                    pe.wait_ge(s_pca, h)
                else:
                    pe.wait_ge(s_kv, KD)
                for m in range(MT):
                    for t in range(TT):
                        i = pe.transpose(bank[4 + m][:, t * P:(t + 1) * P], px[:, h % 2, t, m * P:(m + 1) * P], ident)
                    i.then_inc(s_pT, 1)

            def cross_attend(h):
                pe.wait_ge(s_pcd, h + 1)
                pe.wait_ge(s_pca, h + 1)
                if h:
                    pe.wait_ge(*operand("xo", 2 * h - 1))
                for d in range(2):
                    for m in range(MT):
                        i = pe.matmul(bank[6 + d][:, :], vx[:, m, (2 * h + d) * P:(2 * h + d + 1) * P], pxT[:, h % 2, m, :],
                                      start=(m == 0), stop=(m == MT - 1))
                    i.then_inc(s_pv, 1)

            cross_scores(0)
            for h in range(XH):
                if h + 1 < XH:
                    cross_scores(h + 1)
                cross_turn(h)
                if h:
                    cross_attend(h - 1)
            cross_attend(XH - 1)
            linear("xo")
            stats("ln3", phases["xo"])
            ffn("f2", "ln4")
            for k in range(KD):
                pe.wait_ge(square_done, 8 * NORMS["rms1"][0] + k + 1)
                i = pe.matmul(bank[5][:, :], mats[:, C_MEAN, :], square[:, k % 2, :], start=(k == 0), stop=(k == KD - 1))
                i.then_inc(stat_sq if k == KD - 1 else rms1_sum, 1)
            def prepare(kind, j):
                if kind == "square":
                    pe.wait_ge(s_hsq, j + 1)
                    pe.matmul(bank[4 + j % 2][:, :], mats[:, C_HEAD, :], r1[:, j % 2, :], start=True, stop=True).then_inc(s_hss, 1)
                elif kind == "rstd":
                    pe.wait_ge(s_hn, j + 1)
                    pe.matmul(bank[6 + j % 2][:, :], mats[:, C_ROT, :], in2_dst(j), start=True, stop=True).then_inc(s_hrot, 1)
                elif kind == "turn_v":
                    pe.wait_ge(bank_free, RAW + phases["in2"].base + 6)
                    four(bank[5], skv[:, 1, :], s_svT)
                elif kind == "double":
                    pe.wait_ge(s_hrs, 5)
                    pe.wait_ge(s_hr, 5)
                    for g in range(2):
                        pe.matmul(bank[(4, 7)[g]][:, :], mats[:, C_DUP0 + g, :], skv[:, 0, :], start=True, stop=True).then_inc(s_dup, 1)

            multiply_two(pe, phases["in2"], ahi, alo, T, made("in2"))
            for j, tasks in enumerate(plan2):
                if j >= 2:
                    multiply(pe, phases["in2"], 0, j, ahi, alo)
                for task in tasks:
                    prepare(*task)

            def self_scores(h, t):
                n = TT * h + t
                if h >= QH:
                    return
                pe.wait_ge(s_stl, h + 1)
                if n < 3:
                    pe.wait_ge(bank_free, RAW + phases["in2"].base + last_block_in(phases["in2"], n) + 1)
                else:
                    pe.wait_ge(s_pe, TT * XH + n - 2)
                q = sst[:, h, t * P:(t + 1) * P]
                pe.matmul(bank[n % 3][:, :], q, khi[:, h // 4, :], start=True, stop=False)
                pe.matmul(bank[n % 3][:, :], q, klo[:, h // 4, :], start=False, stop=True).then_inc(s_sc, 1)

            def self_turn(h, st):
                if st == 0:
                    pe.wait_ge(s_pn, TT * XH + TT * (h + 1))
                if st == 2:
                    pe.wait_ge(s_pcd, XH + h + 1)
                elif st == 3:
                    pe.wait_ge(s_pca, XH + 3 * h + 1)
                elif h:
                    pe.wait_ge(s_pca, XH + 3 * (h - 1) + 2 + st)
                for t in range(TT):
                    i = pe.transpose(bank[3 + st % 2][:, t * P:(t + 1) * P], ps[:, h % 2, t, st * P:(st + 1) * P], ident)
                i.then_inc(s_pT, 1)

            def self_attend(h, st):
                p0 = HD * (h % 2)
                if h < 0:
                    return
                if st == 0:
                    pe.wait_ge(s_pcd, XH + h + 1)
                    pe.wait_ge(s_pca, XH + 3 * (h + 1))
                    if h >= 4 and h % 2 == 0:
                        pe.wait_ge(*operand("out2", OUT2_TILES.index(h // 2 - 2)))
                i = pe.matmul(bank[6 + (h // 2) % 2][p0:p0 + HD, :], sv[:, st, HD * (h // 4):HD * (h // 4) + HD],
                              psT[:, h % 2, st, :], start=(st == 0), stop=(st == TT - 1))
                if st == TT - 1:
                    i.then_inc(s_pv, 1)

            pe.wait_ge(s_dupc, 3)
            for t in range(TT):
                self_scores(0, t)
            for h in range(QH):
                self_scores(h + 1, 0)
                self_scores(h + 1, 1)
                self_turn(h, 0)
                self_turn(h, 1)
                self_scores(h + 1, 2)
                self_attend(h - 1, 0)
                self_attend(h - 1, 1)
                self_scores(h + 1, 3)
                self_turn(h, 2)
                self_turn(h, 3)
                self_attend(h - 1, 2)
                self_attend(h - 1, 3)
                if 0 <= h - POOL_AT < 4:
                    n = h - POOL_AT
                    pe.wait_ge(s_pool, n + 1)
                    if n:
                        pe.wait_ge(s_py, n)
                    pe.matmul(bank[5][:, :], poolw[:, POOL_ORDER[n], :], su[:, n, 8:8 + T], start=True, stop=True).then_inc(s_pmm, 1)
            for st in range(TT):
                self_attend(QH - 1, st)
            linear("out2", order=OUT2_TILES)
            stats("rms2")
            ffn("f3", None)


def kernel(**inputs):
    import concourse.bacc as bacc
    from concourse.bass_utils import run_bass_kernel_spmd as run

    nc = bacc.Bacc("TRN2", target_bir_lowering=False, num_devices=1)
    arrays = {name: np.ascontiguousarray(a) for name, a in inputs.items()}
    arrays.update(shape_constants())
    aps = {}
    arrays = {f"in_{name}": a for name, a in arrays.items()}
    for name, a in arrays.items():
        aps[name[3:]] = nc.dram_tensor(name, a.shape, mybir.dt.from_np(a.dtype), kind="ExternalInput").ap()
    out = nc.dram_tensor("out_dram", (1, T, D), F32, kind="ExternalOutput").ap()
    build(nc, aps, out)
    return run(nc, [arrays], core_ids=[0]).results[0]["out_dram"]
```
